# Optimizing a Trainium2 kernel written in Bass

```python
import math
import jax, jax.numpy as jnp
from jax import lax
import numpy as np

D_MODEL = 1024
BATCH = 1
SEQ = 1024
DEPTH = 2

N_EVEN = (DEPTH + 1) // 2
N_ODD = DEPTH // 2
NORM_EPS = 1e-6

A_HEADS = 4
A_DK = 128
A_DV = 128
A_WIDTH = A_HEADS * A_DK
A_CHUNK = 32
B_HEADS = 4
B_HD = 128
B_WIDTH = B_HEADS * B_HD
B_DILATIONS = ((128, 1), (512, 4), (2048, 16))
ROPE_THETA = 10000.0
IN_AB_WIDTH = 4 * A_WIDTH + 3 * B_WIDTH
MIX_WIDTH = A_WIDTH + B_WIDTH
C_GROUP = 16
C_GROUPS = D_MODEL // C_GROUP
C_STATE = 64
C_CHUNK = 128
C_MIN_NEG_RE = -1e-4
MEM_LEN = 256
X_HEADS = 4
X_HD = D_MODEL // X_HEADS
D_FF = -(-8 * D_MODEL // (3 * 256)) * 256

kernel_name = "hybrid_hgrn2_dilated_s5_block"

def rms_norm(x, w):
    xf = x.astype(jnp.float32)
    y = xf * lax.rsqrt(jnp.mean(xf * xf, axis=-1, keepdims=True) + NORM_EPS)
    return (y * w.astype(jnp.float32)).astype(x.dtype)

def split_heads(t, n_heads):
    b, l, _ = t.shape
    return t.reshape(b, l, n_heads, -1).transpose(0, 2, 1, 3)

def merge_heads(t):
    b, h, l, d = t.shape
    return t.transpose(0, 2, 1, 3).reshape(b, l, h * d)

def rotary(x, pos):
    half = x.shape[-1] // 2
    inv_freq = ROPE_THETA ** (-jnp.arange(half, dtype=jnp.float32) / half)
    ang = pos.astype(jnp.float32)[:, None] * inv_freq[None, :]
    cos, sin = jnp.cos(ang), jnp.sin(ang)
    x1, x2 = x[..., :half], x[..., half:]
    return jnp.concatenate([x1 * cos - x2 * sin, x1 * sin + x2 * cos], axis=-1)

def hgrn2_mixer(q, f_logit, i_val, g, lb, onorm_w):
    bsz, L, _ = q.shape
    nc = L // A_CHUNK
    f = lb + (1.0 - lb) * jax.nn.sigmoid(f_logit)
    log_f = jnp.log(f)
    k = 1.0 - f

    def chunked(t):
        return split_heads(t, A_HEADS).reshape(bsz, A_HEADS, nc, A_CHUNK, -1)

    qc, kc, vc, lfc = chunked(q), chunked(k), chunked(i_val), chunked(log_f)
    b = jnp.cumsum(lfc, axis=3)
    b_last = b[:, :, :, -1:, :]
    q_dec = qc * jnp.exp(b)
    k_inv = kc * jnp.exp(-b)
    k_end = kc * jnp.exp(b_last - b)
    decay = jnp.exp(b_last[:, :, :, 0, :])
    causal = jnp.tril(jnp.ones((A_CHUNK, A_CHUNK), dtype=bool))
    scores = jnp.einsum('bhncd,bhnsd->bhncs', q_dec, k_inv)
    scores = jnp.where(causal, scores, 0.0)
    o_intra = jnp.einsum('bhncs,bhnsv->bhncv', scores, vc)

    def step(S, inp):
        qd, ke, v, dec = inp
        o = jnp.einsum('bhcd,bhdv->bhcv', qd, S)
        S = dec[..., None] * S + jnp.einsum('bhcd,bhcv->bhdv', ke, v)
        return S, o

    S0 = jnp.zeros((bsz, A_HEADS, A_DK, A_DV), jnp.float32)
    xs = (jnp.moveaxis(q_dec, 2, 0), jnp.moveaxis(k_end, 2, 0),
          jnp.moveaxis(vc, 2, 0), jnp.moveaxis(decay, 2, 0))
    _, o_inter = lax.scan(step, S0, xs)
    o = (o_intra + jnp.moveaxis(o_inter, 0, 2)).reshape(bsz, A_HEADS, L, A_DV)
    o = o * lax.rsqrt(jnp.mean(o * o, axis=-1, keepdims=True) + NORM_EPS)
    o = merge_heads(o) * onorm_w.astype(jnp.float32)
    return o * jax.nn.silu(g)

def dilated_branch(q, k, v, dil, span):
    bsz, H, L, hd = q.shape
    Ls = L // dil
    nb = -(-Ls // span)
    pad = nb * span - Ls

    def strided(t):
        t = t.reshape(bsz, H, Ls, dil, hd).transpose(0, 1, 3, 2, 4)
        t = jnp.pad(t, ((0, 0), (0, 0), (0, 0), (0, pad), (0, 0)))
        return t.reshape(bsz, H, dil, nb, span, hd)

    def with_prev(t):
        prev = jnp.pad(t[:, :, :, :-1], ((0, 0), (0, 0), (0, 0), (1, 0), (0, 0), (0, 0)))
        return jnp.concatenate([prev, t], axis=4)

    qb = strided(q)
    kw, vw = with_prev(strided(k)), with_prev(strided(v))
    s = jnp.einsum('bhrnqd,bhrnkd->bhrnqk', qb, kw) * (hd ** -0.5)
    iq = jnp.arange(span)[:, None]
    ik = jnp.arange(2 * span)[None, :]
    delta = span + iq - ik
    kpos = (jnp.arange(nb)[:, None, None] - 1) * span + ik[None]
    mask = (delta >= 0) & (delta <= span) & (kpos >= 0)
    s = jnp.where(mask, s, -jnp.inf)
    m = jnp.max(s, axis=-1, keepdims=True)
    p = jnp.exp(s - m)
    l = jnp.sum(p, axis=-1)
    o = jnp.einsum('bhrnqk,bhrnkd->bhrnqd', p, vw) / l[..., None]
    lse = m[..., 0] + jnp.log(l)

    def unstride(t):
        t = t.reshape(bsz, H, dil, nb * span, -1)[:, :, :, :Ls]
        return t.transpose(0, 1, 3, 2, 4).reshape(bsz, H, L, -1)

    return unstride(o), unstride(lse[..., None])[..., 0]

def dilated_attention(q, k, v):
    outs, lses = [], []
    for window, dil in B_DILATIONS:
        o, lse = dilated_branch(q, k, v, dil, window // dil)
        outs.append(o)
        lses.append(lse)
    wts = jax.nn.softmax(jnp.stack(lses), axis=0)
    return jnp.einsum('gbhl,gbhld->bhld', wts, jnp.stack(outs))

def mix_ab(h, w_in, w_out, lb, onorm_w, pos):
    z = (h @ w_in).astype(jnp.float32)
    offs = np.cumsum([A_WIDTH] * 4 + [B_WIDTH] * 2).tolist()
    qa, fa, ia, ga, qb, kb, vb = jnp.split(z, offs, axis=-1)
    oa = hgrn2_mixer(qa, fa, ia, ga, lb, onorm_w)
    qh = rotary(split_heads(qb, B_HEADS), pos)
    kh = rotary(split_heads(kb, B_HEADS), pos)
    vh = split_heads(vb, B_HEADS)
    ob = merge_heads(dilated_attention(qh, kh, vh))
    y = jnp.concatenate([oa, ob], axis=-1).astype(h.dtype)
    return y @ w_out

def complex_affine(e1, e2):
    a1r, a1i, b1r, b1i = e1
    a2r, a2i, b2r, b2i = e2
    return (a2r * a1r - a2i * a1i,
            a2r * a1i + a2i * a1r,
            a2r * b1r - a2i * b1i + b2r,
            a2r * b1i + a2i * b1r + b2i)

def s5_mixer(h, lam_re, lam_im, log_dt, b_re, b_im, c_re, c_im, d_skip, w_glu):
    f32 = jnp.float32
    u = h.astype(f32)
    bsz, L, _ = u.shape
    lr = jnp.minimum(lam_re.astype(f32), C_MIN_NEG_RE)
    li = lam_im.astype(f32)
    dt = jnp.exp(log_dt.astype(f32))[:, None]
    mag = jnp.exp(dt * lr)
    ar, ai = mag * jnp.cos(dt * li), mag * jnp.sin(dt * li)
    den = lr * lr + li * li
    zr = ((ar - 1.0) * lr + ai * li) / den
    zi = (ai * lr - (ar - 1.0) * li) / den
    br, bi = b_re.astype(f32), b_im.astype(f32)
    bbr = zr[..., None] * br - zi[..., None] * bi
    bbi = zr[..., None] * bi + zi[..., None] * br
    cr, ci = c_re.astype(f32), c_im.astype(f32)
    nc = L // C_CHUNK
    ug = u.reshape(bsz, nc, C_CHUNK, C_GROUPS, C_GROUP).transpose(1, 0, 2, 3, 4)

    def step(state, uc):
        hr, hi = state
        xr = jnp.einsum('btgc,gpc->btgp', uc, bbr)
        xi = jnp.einsum('btgc,gpc->btgp', uc, bbi)
        a_r = jnp.broadcast_to(ar, xr.shape)
        a_i = jnp.broadcast_to(ai, xr.shape)
        pr, pi_, sr, si = lax.associative_scan(complex_affine, (a_r, a_i, xr, xi), axis=1)
        str_ = pr * hr[:, None] - pi_ * hi[:, None] + sr
        sti = pr * hi[:, None] + pi_ * hr[:, None] + si
        y = (jnp.einsum('btgp,gcp->btgc', str_, cr)
             - jnp.einsum('btgp,gcp->btgc', sti, ci))
        return (str_[:, -1], sti[:, -1]), y

    h0 = (jnp.zeros((bsz, C_GROUPS, C_STATE), f32), jnp.zeros((bsz, C_GROUPS, C_STATE), f32))
    _, y = lax.scan(step, h0, ug)
    y = y.transpose(1, 0, 2, 3, 4).reshape(bsz, L, D_MODEL)
    y = y + d_skip.astype(f32) * u
    gl = jax.nn.gelu(y, approximate=False).astype(h.dtype)
    z = gl @ w_glu
    return z[..., :D_MODEL] * jax.nn.sigmoid(z[..., D_MODEL:])

def memory_cross_attention(h, mem_n, wq, wkv, wo):
    q = split_heads(h @ wq, X_HEADS).astype(jnp.float32)
    kv = mem_n @ wkv
    k = split_heads(kv[..., :D_MODEL], X_HEADS).astype(jnp.float32)
    v = split_heads(kv[..., D_MODEL:], X_HEADS).astype(jnp.float32)
    s = jnp.einsum('bhqd,bhkd->bhqk', q, k) * (X_HD ** -0.5)
    p = jax.nn.softmax(s, axis=-1)
    o = jnp.einsum('bhqk,bhkd->bhqd', p, v).astype(h.dtype)
    return merge_heads(o) @ wo

def swiglu(h, w_in, w_out):
    z = h @ w_in
    return (jax.nn.silu(z[..., :D_FF]) * z[..., D_FF:]) @ w_out

def setup_inputs(seed: int = 0) -> dict:
    key = jax.random.key(seed)
    ks = jax.random.split(key, 24)
    f32 = jnp.float32
    nrm = lambda k, shape, scale: jax.random.normal(k, shape, f32) * scale
    return {
        "x": nrm(ks[0], (BATCH, SEQ, D_MODEL), 1.0),
        "mem": nrm(ks[1], (BATCH, MEM_LEN, D_MODEL), 1.0),
        "norm_w": 1.0 + nrm(ks[2], (DEPTH, 6, D_MODEL), 0.05),
        "mem_norm_w": 1.0 + nrm(ks[3], (DEPTH, D_MODEL), 0.05),
        "ab_w_in": nrm(ks[4], (N_EVEN, D_MODEL, IN_AB_WIDTH), D_MODEL ** -0.5),
        "ab_w_out": nrm(ks[5], (N_EVEN, MIX_WIDTH, D_MODEL), MIX_WIDTH ** -0.5),
        "hgrn_lb_logits": nrm(ks[6], (DEPTH + 1, A_WIDTH), 0.1),
        "hgrn_out_norm_w": 1.0 + nrm(ks[7], (N_EVEN, A_WIDTH), 0.05),
        "s5_lambda_re": -0.5 + nrm(ks[8], (N_ODD, C_GROUPS, C_STATE), 0.01),
        "s5_lambda_im": np.pi * jnp.arange(C_STATE, dtype=f32) + nrm(ks[9], (N_ODD, C_GROUPS, C_STATE), 0.01),
        "s5_log_dt": jax.random.uniform(ks[10], (N_ODD, C_GROUPS), f32, math.log(1e-3), math.log(1e-1)),
        "s5_b_re": nrm(ks[11], (N_ODD, C_GROUPS, C_STATE, C_GROUP), (2 * C_GROUP) ** -0.5),
        "s5_b_im": nrm(ks[12], (N_ODD, C_GROUPS, C_STATE, C_GROUP), (2 * C_GROUP) ** -0.5),
        "s5_c_re": nrm(ks[13], (N_ODD, C_GROUPS, C_GROUP, C_STATE), 2.0 ** -0.5),
        "s5_c_im": nrm(ks[14], (N_ODD, C_GROUPS, C_GROUP, C_STATE), 2.0 ** -0.5),
        "s5_d": nrm(ks[15], (N_ODD, D_MODEL), 1.0),
        "s5_w_glu": nrm(ks[16], (N_ODD, D_MODEL, 2 * D_MODEL), D_MODEL ** -0.5),
        "xattn_wq": nrm(ks[17], (DEPTH, D_MODEL, D_MODEL), D_MODEL ** -0.5),
        "xattn_wkv": nrm(ks[18], (DEPTH, D_MODEL, 2 * D_MODEL), D_MODEL ** -0.5),
        "xattn_wo": nrm(ks[19], (DEPTH, D_MODEL, D_MODEL), D_MODEL ** -0.5),
        "ffn_w_in": nrm(ks[20], (DEPTH, D_MODEL, 2 * D_FF), D_MODEL ** -0.5),
        "ffn_w_out": nrm(ks[21], (DEPTH, D_FF, D_MODEL), D_FF ** -0.5),
    }

def reference(x, mem, norm_w, mem_norm_w, ab_w_in, ab_w_out, hgrn_lb_logits,
              hgrn_out_norm_w, s5_lambda_re, s5_lambda_im, s5_log_dt, s5_b_re,
              s5_b_im, s5_c_re, s5_c_im, s5_d, s5_w_glu, xattn_wq, xattn_wkv,
              xattn_wo, ffn_w_in, ffn_w_out):
    L = x.shape[1]
    pos = jnp.arange(L, dtype=jnp.int32)
    lb_table = jnp.cumsum(jax.nn.softmax(hgrn_lb_logits.astype(jnp.float32), axis=0), axis=0)
    for layer in range(DEPTH):
        j = layer // 2
        h = rms_norm(x, norm_w[layer, 0])
        if layer % 2 == 0:
            y = mix_ab(h, ab_w_in[j], ab_w_out[j], lb_table[layer], hgrn_out_norm_w[j], pos)
        else:
            y = s5_mixer(h, s5_lambda_re[j], s5_lambda_im[j], s5_log_dt[j], s5_b_re[j],
                         s5_b_im[j], s5_c_re[j], s5_c_im[j], s5_d[j], s5_w_glu[j])
        x = x + rms_norm(y, norm_w[layer, 1])
        h = rms_norm(x, norm_w[layer, 2])
        mem_n = rms_norm(mem, mem_norm_w[layer])
        y = memory_cross_attention(h, mem_n, xattn_wq[layer], xattn_wkv[layer], xattn_wo[layer])
        x = x + rms_norm(y, norm_w[layer, 3])
        h = rms_norm(x, norm_w[layer, 4])
        x = x + rms_norm(swiglu(h, ffn_w_in[layer], ffn_w_out[layer]), norm_w[layer, 5])
    return x


_drawn_inputs = setup_inputs


def setup_inputs(seed=0):
    import zlib

    import numpy as np

    out = dict(_drawn_inputs(seed))
    spreads = {}
    factors = {}
    for name, (base, spread) in spreads.items():
        noise = np.random.default_rng([zlib.crc32(name.encode()), seed]).standard_normal(out[name].shape)
        drawn = base * np.exp(spread * noise) if base else spread * noise
        out[name] = __import__('jax').numpy.asarray(drawn.astype(out[name].dtype))
    for name, factor in factors.items():
        out[name] = (out[name] * factor).astype(out[name].dtype)
    return out
```

```python
from contextlib import ExitStack, contextmanager

import concourse.bass as bass
import numpy as np
from concourse import mybir

F32 = mybir.dt.float32
F32R = mybir.dt.float32r
ALU = mybir.AluOpType
ACT = mybir.ActivationFunctionType
AX = mybir.AxisListType.X
ds = bass.ds

P = 128
D = 1024
L = 1024
LAYERS = 2
KT = D // P
HALF = 512
MEM = 256
DFF = 2816
FT = DFF // P
FC = FT // 2
HEADS = 4
CH = 32
NCH = L // CH
EPS = 1e-6
B_SCALE = 128 ** -0.5
X_SCALE = 256 ** -0.5
AW = 512

GR = 64
GC = 16
SB = 16
NB = L // SB

TWO_PI = 2 * np.pi
ROUND = 1.5 * 2 ** 23
TURN = (6.28125, 0.0019350051879882812, float(TWO_PI - 6.28125 - 0.0019350051879882812))
PI_IN = 3.1415925

NW = 0
MNW = NW + 2 * 6 * KT
LBL = MNW + 2 * KT
ONW = LBL + 3 * HEADS
SD = ONW + HEADS
NPAR = SD + KT
C_ID = 0
C_CAUSAL = C_ID + P
C_BLK = C_CAUSAL + P
C_SIGN = C_BLK + 4
C_LOGC = C_SIGN + 4
C_COS = C_LOGC + L
C_SIN = C_COS + L
C_FIRST = C_SIN + L
NCON = C_FIRST + L


ALIASES = (("product", 2), ("lin_out", 2), ("sum_out", 2), ("acc_sum", 2), ("x_taken", 2), ("y2_added", 2))


class Count:

    def __init__(self, n=0):
        self.n, self.i, self.per, self.base = n, None, 0, 0

    def next(self, k=1):
        self.n += k
        return self.n if self.i is None else self.i * self.per + self.n


class Counts:

    def __init__(self, eng, names):
        self.eng = eng
        self.c = {name: Count() for name in names}
        for name, primed in ALIASES:
            self.c[name] = Count(primed)

    def at(self, name, k=1):
        return self.c[name].next(k)

    def skip(self, name, k=1):
        self.c[name].next(k)

    @contextmanager
    def repeat(self, n, **per):
        with self.eng.Fori(0, n) as i:
            for name, c in self.c.items():
                c.i, c.per, c.base = i, per.get(name, 0), c.n
            yield i
            for name, c in self.c.items():
                assert c.n - c.base == c.per, (name, c.n - c.base, c.per)
                c.i, c.n = None, c.base + c.per * n


def program(nc, t):
    with ExitStack() as ctx:
        def place(name, shape, dt, at):
            return nc.alloc_sbuf_tensor_at(name, shape, dt, offset=BASE + at)

        BASE = (nc.sbuf_base + 31) // 32 * 32
        KB = 1024
        FENCE = 163 * KB + 45 * KB - 256
        ctx.enter_context(nc.sbuf_tensor("fence", [P, FENCE // 4], F32))
        x = place("x", [P, KT, L], F32, 0)
        h_hi = place("h_hi", [P, KT, L], F32R, 32 * KB)
        h_lo = place("h_lo", [P, KT, L], F32R, 64 * KB)
        y = place("y", [P, KT, L], F32, 96 * KB)
        w_raw = place("w_raw", [P, 2, L], F32, 128 * KB)
        w_hi = place("w_hi", [P, 2, L], F32R, 136 * KB)
        w_lo = place("w_lo", [P, 2, L], F32R, 144 * KB)
        rstd = place("rstd", [P, L], F32, 152 * KB)
        acc = place("acc", [P, L], F32, 156 * KB)
        ident = place("ident", [P, P], F32, 160 * KB)
        ones = place("ones", [P, P], F32, 160 * KB + 512)
        par = place("par", [P, NPAR], F32, 161 * KB)
        eps = place("eps", [P, 2], F32, 161 * KB + 640)
        lbt = place("lbt", [P, 8 * HEADS], F32, 161 * KB + 704)
        rstd_m = place("rstd_m", [P, MEM], F32, 162 * KB)
        A0 = 163 * KB
        sq = place("sq", [P, 2, L], F32, A0 + 32 * KB)
        tmp = place("tmp", [P, 2, L], F32, A0)

        zq = place("zq", [P, L], F32, 0)
        zf = place("zf", [P, L], F32, 4 * KB)
        zi = place("zi", [P, L], F32, 8 * KB)
        zg = place("zg", [P, L], F32, 12 * KB)
        gk = place("gk", [P, L], F32, 16 * KB)
        gb = place("gb", [P, L], F32, 20 * KB)
        ge = place("ge", [P, L], F32, 24 * KB)
        bq = place("bq", [P, L], F32, 28 * KB)
        bk = place("bk", [P, L], F32, A0)
        vtok_b = place("vtok_b", [P, KT, P], F32, A0 + 4 * KB)
        prob = place("prob", [P, 2, L], F32, A0 + 8 * KB)
        probT = place("probT", [P, KT, P], F32, A0 + 16 * KB)
        cosr = place("cosr", [P, L], F32, A0 + 20 * KB)
        sinr = place("sinr", [P, L], F32, A0 + 24 * KB)
        logc = place("logc", [P, L], F32, A0 + 28 * KB)
        first = place("first", [P, L], F32, A0 + 32 * KB)
        states = place("states", [P, 8, P], F32, A0 + 36 * KB)
        M0 = A0 + 40 * KB
        ktok = place("ktok", [P, P], F32, M0)
        vtok = place("vtok", [P, 2, P], F32, M0 + 512)
        X0 = M0 + 1536
        causal = place("causal", [P, P], F32, X0)
        scm = place("scm", [P, 2, P], F32, X0 + 512)
        blk = place("blk", [P, 4], F32, X0 + 1536)
        dec = place("dec", [P, NCH], F32, X0 + 1536 + 32)
        hp = place("hp", [P, HEADS, 3], F32, X0 + 1536 + 160)
        cur = place("cur", [P, 3], F32, X0 + 1536 + 224)
        stat = place("stat", [P, 2, 4], F32, X0 + 1536 + 256)
        vblk = acc[:, 0:512].rearrange("p (c v) -> p c v", c=4)

        hid_hi = place("hid_hi", [P, 4, L], F32R, A0)
        hid_lo = place("hid_lo", [P, 4, L], F32R, A0 + 16 * KB)
        gate = place("gate", [P, L], F32, A0 + 32 * KB)
        f_act = place("act", [P, L], F32, A0 + 36 * KB)

        m_hi = place("m_hi", [P, KT, MEM], F32R, A0)
        m_lo = place("m_lo", [P, KT, MEM], F32R, A0 + 8 * KB)
        xq = place("xq", [P, 2, L], F32, A0 + 16 * KB)
        xk = place("xk", [P, 2, MEM], F32, A0 + 24 * KB)
        xv = place("xv", [P, 2, MEM], F32, A0 + 26 * KB)
        xvt = place("xvt", [P, 2, MEM], F32, A0 + 28 * KB)
        xp = place("xp", [P, 2, MEM], F32, A0 + 30 * KB)
        xpT = place("xpT", [P, 2, HALF], F32, A0 + 32 * KB)
        xstat = place("xstat", [P, 2, 4], F32, A0 + 36 * KB)
        m_raw = place("m_raw", [P, KT, MEM], F32, A0 + 36 * KB + 64)
        m_sq = place("m_sq", [P, KT, MEM], F32, 96 * KB)

        sg = place("sg", [P, L], F32, A0 + 8 * KB)
        sgn = place("sgn", [P, 2], F32, 161 * KB + 672)
        o_src = [place(f"o_src{i}", [P, GR, GC], F32, 4 * i * KB) for i in range(2)]
        o_dst = [place(f"o_dst{i}", [P, GR, GC], F32, (8 + 4 * i) * KB) for i in range(2)]
        o_tmp = place("o_tmp", [P, GR, GC], F32, 16 * KB)
        pw = place("pw", [P, 2, GR], F32, 20 * KB)
        pc = place("pc", [P, 4, GR], F32, 20 * KB + 8704)
        pt = place("pt", [P, 4, GR], F32, 20 * KB + 8704 + 1024)
        sp_in = place("sp_in", [P, 3, GR], F32, A0)
        sv = place("sv", [P, 16, GR], F32, A0 + 1024)

        ub = place("ub", [P, 2, GR, NB], F32, 32 * KB)
        hs = place("hs", [P, 2, GR, NB], F32, 64 * KB)
        yT = place("yT", [P, KT, L], F32, 64 * KB)
        wt = [place(f"wt{i}", [P, SB, P], F32, A0 + 32 * i * KB) for i in range(2)]
        m1 = place("m1", [P, 2, 2, 8, P], F32, A0 + 8 * KB)
        wr = place("wr", [P, 8, SB, GC], F32, A0 + 24 * KB)
        dr = [place(f"dr{i}", [P, 8, SB, GC], F32, A0 + (18 + 8 * i) * KB) for i in range(2)]
        dt_ = [place(f"dt{i}", [P, SB + 1, P], F32, A0 + 8704 * i) for i in range(2)]
        w15 = [place(f"w15_{i}", [P, P], F32, A0 + 17408 + 512 * i) for i in range(2)]
        kpad = place("kpad", [16, 8, 23 * GC], F32, A0 + 18432)
        tz = place("tz", [P, 8, 2 * P], F32, A0 + 30208)
        ar_b = place("ar_b", [P, GR], F32, A0 + 41 * KB)
        sai_b = place("sai_b", [P, 2, GR], F32, A0 + 41 * KB + 256)
        sc1 = place("sc1", [P, 2, GR], F32, A0 + 41 * KB + 768)
        sc2 = place("sc2", [P, 2, GR], F32, A0 + 41 * KB + 1280)

        bank = [ctx.enter_context(nc.psum_tensor(f"bank{i}", [P, 1024], F32)) for i in range(4)]
        lin = bank[0:2]
        wide = bank[2:4]

        names = ("par_in x_in con_in mem_in out_done w_load0 w_load1 w_hi_done w_ready w_used lin_free out_full "
                 "out_free setup lb_max lb_exp sq_done sq_free acc_done stat_full sqrt_done rstd_done x_done hi_done "
                 "h_ready v_step g_step f_exp f_sig f_kept f_log b_scan b_exp q_dec b_neg y_zero "
                 "k_inv b_left b_left_exp k_end g_exp a1_full a1_out ctr_full st_done ao_full "
                 "ao_out s_full s_max p_exp p_sum p_ready t_full t_out bo_full bo_out vt_full vt_out o_sq o_stat "
                 "o_root o_done rope_done s5_in s5_exp s5_mag s5_abs s5_trig s5_made s5_kept  x_sent ops_in ops_out0 ops_out1 x_back u_done u_out u_in wt_in0 wt_in1 wr_done dr_done m1_full m1a_out m1b_out x_full x_out pw_in d_in0 d_in1 k_full k_out t_in yt_full yt_out scan_done y2_full y2_out y_sent yT_in g_in g_done sg_done glu_done m_hi_done m_ready silu_done hid_done hid_hi_done hid_ready")
        sems = {n: ctx.enter_context(nc.semaphore(n)) for n in names.split()}
        s = type("Sems", (), sems)
        block = ctx.enter_context(nc.Block())

        def nw(layer, which, k):
            c = NW + (layer * 6 + which) * KT + k
            return par[:, c:c + 1]

        con = t["con"]
        xv_d = t["xT"].rearrange("(k p) t -> p k t", p=P)
        mem_d = t["memT"].rearrange("(k p) t -> p k t", p=P)
        out_d = t["out"].rearrange("(k p) t -> p k t", p=P)

        def w_view(name, layer=0):
            return t[name][layer].rearrange("(k p) n -> p k n", p=P)

        def col8(ap, parity):
            return ap[:, parity].rearrange("p (k n) -> p k n", k=KT)

        def col2(ap, parity):
            return ap[:, parity].rearrange("p (k n) -> p k n", k=2)

        @block.sync
        def _(sp):
            w = Counts(sp, sems)
            sp.dma_start(x[:], xv_d).then_inc(s.x_in, 16)
            sp.dma_start(par[:], t["par"]).then_inc(s.par_in, 16)
            sp.dma_start(ident[:], con[:, C_ID:C_ID + P]).then_inc(s.par_in, 16)
            sp.dma_start(m_raw[:], mem_d).then_inc(s.mem_in, 16)
            sp.dma_start(sp_in[:].rearrange("p a g -> p (a g)"), t["s5_small"]).then_inc(s.s5_in, 16)
            sp.dma_start(sgn[:], con[:, C_SIGN:C_SIGN + 2]).then_inc(s.s5_in, 16)

            def load(parity, dst, src):
                sp.wait_ge(s.w_used, w.at("w_used"))
                sp.dma_start(dst, src).then_inc((s.w_load0, s.w_load1)[parity], 16)

            def columns(parity, src, n0):
                load(parity, col8(w_raw, parity), src[:, :, ds(n0, P)])

            win = w_view("ab_w_in")
            sp.wait_ge(s.rstd_done, w.at("rstd_done", 2))
            sp.wait_ge(s.s5_made, w.at("s5_made"))
            sp.dma_start(t["pc_d"], sv[:, 8:12]).then_inc(s.s5_kept, 16)
            sp.wait_ge(s.s5_kept, 16)
            sp.dma_start(cosr[:], con[:, C_COS:C_COS + L]).then_inc(s.con_in, 16)
            sp.dma_start(sinr[:], con[:, C_SIN:C_SIN + L]).then_inc(s.con_in, 16)
            sp.dma_start(logc[:], con[:, C_LOGC:C_LOGC + L]).then_inc(s.con_in, 16)
            sp.dma_start(first[:], con[:, C_FIRST:C_FIRST + L]).then_inc(s.con_in, 16)
            sp.dma_start(causal[:], con[:, C_CAUSAL:C_CAUSAL + P]).then_inc(s.con_in, 16)
            sp.dma_start(blk[:], con[:, C_BLK:C_BLK + 4]).then_inc(s.con_in, 16)
            with w.repeat(HEADS, w_used=8) as h:
                for j in range(7):
                    columns(j % 2, win, h * P + j * AW)
                w.skip("w_used")
            wout = w_view("ab_w_out")
            with w.repeat(KT // 2, w_used=2) as i:
                for j in range(2):
                    columns(j, wout, i * (2 * P) + j * P)
            for layer in range(LAYERS):
                wq, wkv, wo = w_view("xattn_wq", layer), w_view("xattn_wkv", layer), w_view("xattn_wo", layer)
                with w.repeat(HEADS, w_used=6) as h:
                    for j in range(2):
                        columns(j, wq, h * MEM + j * P)
                    for j in range(2):
                        columns(j, wkv, h * MEM + j * P)
                    for j in range(2):
                        columns(j, wkv, h * MEM + (D + j * P))
                with w.repeat(KT // 2, w_used=2) as i:
                    for j in range(2):
                        columns(j, wo, i * (2 * P) + j * P)
                wi, wd = w_view("ffn_w_in", layer), t["ffn_w_out"][layer]

                def up(c):
                    for j in range(2):
                        columns(0, wi, c * (2 * P) + j * P)
                        columns(1, wi, c * (2 * P) + (DFF + j * P))

                def down(c):
                    for j in range(2):
                        load(j, col2(w_raw, j),
                             wd[ds(c * (2 * P), 2 * P), j * HALF:(j + 1) * HALF].rearrange("(k p) n -> p k n", p=P))

                up(0)
                with w.repeat(FC // 2, w_used=12) as i:
                    up(i * 2 + 1)
                    down(i * 2)
                    up(i * 2 + 2)
                    down(i * 2 + 1)
                down(FC - 1)
                if layer == 1 or LAYERS == 1:
                    continue
                wg = w_view("s5_w_glu")
                for j in range(2):
                    columns(j, wg, j * D)
                ud = t["u_d"].rearrange("(k p) t -> k p t", p=P)
                for k in range(KT):
                    sp.wait_ge(s.u_done, w.at("u_done"))
                    sp.dma_start(ud[k], y[:, k]).then_inc(s.u_out, 16)
                sp.wait_ge(s.u_out, w.at("u_out", 16 * KT))

                def by_channel(name, n):
                    return t[name].rearrange("(g c) (s j) -> s c g j", c=GC, s=SB)[n]

                def wt_load(k, b):
                    sp.dma_start(wt[b][:], t["w_d"].rearrange("n p c -> p n c")[:, :, ds(k * P, P)]).then_inc(
                        (s.wt_in0, s.wt_in1)[b], 16)

                wt_load(0, 0)
                wt_load(1, 1)
                for n in range(SB):
                    p0 = (n % 8) * GC
                    sp.dma_start(ub[p0:p0 + GC, n // 8], by_channel("u_d", n)).then_inc(s.u_in, 16)
                with w.repeat(KT // 2 - 1, wr_done=2) as i:
                    for b in range(2):
                        sp.wait_ge(s.wr_done, w.at("wr_done"))
                        wt_load(i * 2 + (2 + b), b)
                sp.wait_ge(s.x_out, w.at("x_taken", KT))
                sp.dma_start(ar_b[:], t["pw_d"][:, 0]).then_inc(s.pw_in, 16)
                sp.dma_start(sai_b[:, 1], t["pw_d"][:, 1]).then_inc(s.pw_in, 16)

                def d_load(k, b, with_w15):
                    sp.dma_start(dt_[b][:], t["dd_d"].rearrange("n p c -> p n c")[:, :, ds(k * P, P)]).then_inc((s.d_in0, s.d_in1)[b], 16)
                    if with_w15:
                        sp.dma_start(w15[b][:], t["w_d"][SB - 1][:, ds(k * P, P)]).then_inc((s.d_in0, s.d_in1)[b], 16)

                def t_load():
                    sp.wait_ge(s.k_out, w.at("k_out"))
                    for n in range(8):
                        c = (7 - n) * GC
                        sp.dma_start(tz[n * GC:(n + 1) * GC], kpad[:, :, c:c + 2 * P]).then_inc(s.t_in, 16)

                d_load(0, 0, True)
                d_load(1, 1, True)
                t_load()
                with w.repeat(KT // 2 - 1, k_out=2, yt_full=2) as i:
                    d_load(i * 2 + 2, 0, True)
                    sp.wait_ge(s.yt_full, w.at("yt_full"))
                    t_load()
                    d_load(i * 2 + 3, 1, True)
                    sp.wait_ge(s.yt_full, w.at("yt_full"))
                    t_load()
                sp.wait_ge(s.yt_full, w.at("yt_full"))
                t_load()
                sp.wait_ge(s.yt_full, w.at("yt_full"))
                d_load(0, 0, False)
                d_load(1, 1, False)
                with w.repeat(KT // 2 - 1, dr_done=2) as i:
                    for b in range(2):
                        sp.wait_ge(s.dr_done, w.at("dr_done"))
                        d_load(i * 2 + 2 + b, b, False)
                sp.wait_ge(s.y2_out, w.at("y2_added", KT))
                for n in range(SB):
                    p0 = (n % 8) * GC
                    sp.dma_start(by_channel("y_d", n), ub[p0:p0 + GC, n // 8]).then_inc(s.y_sent, 16)
                sp.wait_ge(s.y_sent, w.at("y_sent", 16 * SB))
                sp.dma_start(yT[:], t["y_d"].rearrange("(k p) t -> p k t", p=P)).then_inc(s.yT_in, 16)
                with w.repeat(KT - 1, w_used=2) as i:
                    for j in range(2):
                        columns(j, wg, i * P + (P + j * D))
            sp.wait_ge(s.x_done, w.at("x_done", KT * (2 * LAYERS + LAYERS)))
            sp.dma_start(out_d, x[:]).then_inc(s.out_done, 16)
            sp.wait_ge(s.out_done, 16)

        @block.scalar
        def _(act):
            w = Counts(act, sems)
            A = nc.scalar.activation

            def split(parity):
                act.wait_ge((s.w_load0, s.w_load1)[parity], w.at(f"w_load{parity}", 16))
                act.wait_ge(s.w_used, w.at("w_used"))
                A(w_hi[:, parity], w_raw[:, parity], ACT.Copy).then_inc(s.w_hi_done, 1)

            def root(dst, src, n):
                act.wait_ge(s.stat_full, w.at("stat_full"))
                A(dst, src, ACT.Sqrt, bias=eps[:, 0:1], scale=1.0 / n).then_inc(s.sqrt_done, 1)

            def prenorm(layer, which, k):
                A(h_hi[:, k], x[:, k], ACT.Copy, scale=nw(layer, which, k)).then_inc(s.hi_done, 1)
                act.wait_ge(s.sq_free, w.at("sq_free"))
                A(sq[:, k % 2], x[:, k], ACT.Square).then_inc(s.sq_done, 1)

            def boundary(layer, which, s5=False):
                root(rstd[:], wide[0][:], D)
                for k in range(KT):
                    act.wait_ge(s.x_done, w.at("x_done"))
                    if which is not None:
                        prenorm(layer, which, k)
                    if s5:
                        act.wait_ge(s.sq_free, w.at("sq_free"))
                        A(sq[:, k % 2], x[:, k], ACT.Square).then_inc(s.sq_done, 1)
                if which is not None or s5:
                    root(rstd[:], wide[0][:], D)

            def split_y():
                for k in range(KT):
                    A(h_hi[:, k], y[:, k], ACT.Copy).then_inc(s.hi_done, 1)

            def out_projection():
                with w.repeat(KT // 2, product=2, w_used=2, w_load0=16, w_load1=16, sq_free=2) as i:
                    for j in range(2):
                        act.wait_ge(s.w_used, w.at("product"))
                        act.wait_ge(s.sq_free, w.at("sq_free"))
                        A(sq[:, j], lin[j][:], ACT.Square).then_inc(s.sq_done, 1)
                        A(y[:, ds(i * 2 + j, 1)].rearrange("p k t -> p (k t)"), lin[j][:],
                          ACT.Copy).then_inc(s.lin_free, 1)
                        split(j)
                w.skip("lin_out", KT)

            act.wait_ge(s.setup, w.at("setup"))
            act.wait_ge(s.par_in, w.at("par_in", 32))
            act.wait_ge(s.mem_in, w.at("mem_in", 16))
            A(m_sq[:], m_raw[:], ACT.Square).then_inc(s.sq_done, 1)
            act.wait_ge(s.sq_done, w.at("sq_done"))
            act.wait_ge(s.x_in, w.at("x_in", 16))
            for k in range(KT):
                prenorm(0, 0, k)
            root(rstd_m[:], wide[1][:, 0:MEM], D)
            root(rstd[:], wide[0][:], D)
            act.wait_ge(s.lb_max, w.at("lb_max"))
            A(lbt[:, 4:16], lbt[:, 4:16], ACT.Exp).then_inc(s.lb_exp, 1)

            act.wait_ge(s.s5_in, w.at("s5_in", 32))
            A(sv[:, 0], sp_in[:, 2], ACT.Exp).then_inc(s.s5_exp, 1)
            act.wait_ge(s.s5_mag, w.at("s5_mag"))
            A(sv[:, 3], sv[:, 1], ACT.Exp).then_inc(s.s5_abs, 1)
            A(sv[:, 4], sv[:, 2], ACT.Abs).then_inc(s.s5_abs, 1)
            act.wait_ge(s.s5_abs, w.at("s5_abs", 2))
            A(sv[:, 5], sv[:, 2], ACT.Sin).then_inc(s.s5_trig, 1)
            A(sv[:, 6], sv[:, 4], ACT.Sin, scale=-1.0, bias=eps[:, 1:2]).then_inc(s.s5_trig, 1)
            split(0)
            split(1)
            with w.repeat(HEADS, product=8, w_used=8, w_load0=64, w_load1=48, lin_out=7, f_sig=1, f_kept=1, b_scan=1,
                          q_dec=1, b_left=1, vt_full=1, s_max=8, t_full=8, ao_full=8, bo_full=8,
                          ao_out=8, o_stat=1) as h:
                act.wait_ge(s.w_used, w.at("product"))
                split(0)
                act.wait_ge(s.w_used, w.at("product"))
                split(1)
                act.wait_ge(s.lin_free, w.at("lin_out", 2))
                A(zf[:], zf[:], ACT.Exp, scale=-1.0).then_inc(s.f_exp, 1)
                act.wait_ge(s.w_used, w.at("product"))
                split(0)
                act.wait_ge(s.f_sig, w.at("f_sig"))
                A(ge[:], zf[:], ACT.Ln).then_inc(s.f_log, 1)
                A(gk[:], zf[:], ACT.Copy, scale=-1.0, bias=1.0).then_inc(s.f_kept, 1)
                act.wait_ge(s.b_scan, w.at("b_scan"))
                A(ge[:], gb[:], ACT.Exp).then_inc(s.b_exp, 1)
                act.wait_ge(s.f_kept, w.at("f_kept"))
                A(zf[:], gb[:], ACT.Exp, scale=-1.0).then_inc(s.b_neg, 1)
                act.wait_ge(s.w_used, w.at("product"))
                split(1)
                act.wait_ge(s.q_dec, w.at("q_dec"))
                act.wait_ge(s.b_left, w.at("b_left"))
                A(ge[:], ge[:], ACT.Exp).then_inc(s.b_left_exp, 1)
                act.wait_ge(s.lin_free, w.at("lin_out", 2))
                A(gb[:], zg[:], ACT.Exp, scale=-1.0).then_inc(s.g_exp, 1)
                act.wait_ge(s.w_used, w.at("product"))
                split(0)
                w.skip("lin_out", 3)
                w.skip("w_used")
                act.wait_ge(s.w_used, w.at("product", 3))
                split(0)
                split(1)

                def a_out(T):
                    act.wait_ge(s.ao_full, w.at("ao_full"))
                    A(zi[:, T * P:(T + 1) * P], lin[1][:, 0:P], ACT.Copy).then_inc(s.ao_out, 1)

                def b_out(T):
                    act.wait_ge(s.bo_full, w.at("bo_full"))
                    A(y[:, ds(h + HEADS, 1), T * P:(T + 1) * P].rearrange("p k t -> p (k t)"),
                      lin[1][:, HALF:HALF + P], ACT.Copy).then_inc(s.bo_out, 1)

                act.wait_ge(s.vt_full, w.at("vt_full"))
                A(vtok_b[:].rearrange("p k d -> p (k d)"), wide[1][:], ACT.Copy).then_inc(s.vt_out, 1)
                for T in range(KT):
                    W = (T + 1) * P
                    act.wait_ge(s.s_max, w.at("s_max"))
                    A(prob[:, T % 2, 0:W], prob[:, T % 2, 0:W], ACT.Exp, bias=stat[:, T % 2, 1:2], scale=B_SCALE,
                      accum_out=stat[:, T % 2, 2:3]).then_inc(s.p_exp, 1)
                    if T:
                        a_out(T - 1)
                        b_out(T - 1)
                    act.wait_ge(s.t_full, w.at("t_full"))
                    A(probT[:, 0:T + 1].rearrange("p k q -> p (k q)"), wide[1][:, 0:W], ACT.Copy).then_inc(s.t_out, 1)
                a_out(KT - 1)
                b_out(KT - 1)
                act.wait_ge(s.ao_out, w.at("ao_out", 8))
                A(ge[:], zi[:], ACT.Square).then_inc(s.o_sq, 1)
                act.wait_ge(s.o_stat, w.at("o_stat"))
                A(gb[:], wide[0][:], ACT.Sqrt, bias=eps[:, 0:1], scale=1.0 / P).then_inc(s.o_root, 1)
            act.wait_ge(s.o_done, w.at("o_done", HEADS))
            act.dma_start(x[:], xv_d).then_inc(s.x_in, 16)
            act.wait_ge(s.bo_out, w.at("bo_out", KT * HEADS))
            split_y()
            out_projection()
            boundary(0, 2)

            for layer in range(LAYERS):
                act.dma_start(m_raw[:], mem_d).then_inc(s.mem_in, 16)
                act.wait_ge(s.mem_in, w.at("mem_in", 16))
                for k in range(KT):
                    c = MNW + layer * KT + k
                    A(m_hi[:, k], m_raw[:, k], ACT.Copy, scale=par[:, c:c + 1]).then_inc(s.m_hi_done, 1)
                with w.repeat(HEADS, product=6, w_used=6, w_load0=48, w_load1=48, vt_full=1, s_max=8, t_full=8,
                              bo_full=4) as h:
                    for j in range(6):
                        act.wait_ge(s.w_used, w.at("product"))
                        split(j % 2)
                    act.wait_ge(s.vt_full, w.at("vt_full"))
                    A(xvt[:].rearrange("p k d -> p (k d)"), wide[0][:, 0:HALF], ACT.Copy).then_inc(s.vt_out, 1)

                    def softmax(q):
                        act.wait_ge(s.s_max, w.at("s_max"))
                        A(xp[:, q % 2], wide[0][:, (q % 2) * HALF:(q % 2) * HALF + MEM], ACT.Exp,
                          bias=xstat[:, q % 2, 1:2], scale=X_SCALE, accum_out=xstat[:, q % 2, 2:3]).then_inc(s.p_exp, 1)

                    softmax(0)
                    for q in range(KT):
                        if q + 1 < KT:
                            softmax(q + 1)
                        act.wait_ge(s.t_full, w.at("t_full"))
                        A(xpT[:, :, (q % 4) * P:(q % 4 + 1) * P], wide[1][:, 0:MEM].rearrange("p (k q) -> p k q", k=2),
                          ACT.Copy).then_inc(s.t_out, 1)
                        if q % 4 == 3:
                            for j in range(2):
                                act.wait_ge(s.bo_full, w.at("bo_full"))
                                A(y[:, ds(h * 2 + j, 1), (q // 4) * HALF:(q // 4 + 1) * HALF].rearrange("p k t -> p (k t)"),
                                  lin[q // 4][:, j * HALF:(j + 1) * HALF], ACT.Copy).then_inc(s.bo_out, 1)
                w.skip("lin_out", 6 * HEADS)
                act.wait_ge(s.bo_out, w.at("bo_out", 4 * HEADS))
                split_y()
                out_projection()
                boundary(layer, 4)

                def up(c):
                    for j in range(2):
                        act.wait_ge(s.w_used, w.at("product"))
                        split(0)
                        act.wait_ge(s.lin_free, w.at("lin_out"))
                        A(f_act[:], gate[:], ACT.Silu).then_inc(s.silu_done, 1)
                        act.wait_ge(s.w_used, w.at("product"))
                        w.skip("lin_out")
                        split(1)
                        act.wait_ge(s.hid_done, w.at("hid_done"))
                        A(hid_hi[:, 2 * (c % 2) + j], f_act[:], ACT.Copy).then_inc(s.hid_hi_done, 1)

                def down(c, last):
                    for j in range(2):
                        act.wait_ge(s.w_used, w.at("product"))
                        if not last:
                            split(j)
                        if c == FC - 1:
                            for n in range(4 * j, 4 * j + 4):
                                act.wait_ge(s.out_free, w.at("sum_out"))
                                act.wait_ge(s.sq_free, w.at("sq_free"))
                                A(sq[:, n % 2], y[:, n], ACT.Square).then_inc(s.sq_done, 1)
                        else:
                            w.skip("sum_out", 4)

                up(0)
                with w.repeat(FC // 2, product=12, w_used=12, w_load0=96, w_load1=96, lin_out=8, hid_done=4,
                              sum_out=16):
                    up(1)
                    down(0, False)
                    up(0)
                    down(1, False)
                down(FC - 1, layer == LAYERS - 1)
                if layer == LAYERS - 1:
                    boundary(None, None)
                    continue
                boundary(None, None, s5=True)

                with w.repeat(KT, m1_full=2):
                    act.wait_ge(s.m1_full, w.at("m1_full"))
                    src = lin[0][:].rearrange("p (g c) -> p g c", g=8)
                    A(m1[:, 0, 0], src, ACT.Copy)
                    A(m1[:, 1, 0].rearrange("p g (h c) -> p g h c", h=2),
                      src.rearrange("p g (h c) -> p g h c", h=2)[:, :, ::-1], ACT.Copy).then_inc(s.m1a_out, 1)
                    w.skip("m1_full")
                act.wait_ge(s.x_out, w.at("x_taken", KT))
                A(kpad[:, :, 0:7 * GC], ident[0:16, 0:112].unsqueeze(1).to_broadcast([16, 8, 112]), ACT.Copy,
                  scale=0.0)

                def kernels(wait):
                    act.wait_ge(s.k_full, w.at("k_full"))
                    if wait:
                        act.wait_ge(s.t_in, w.at("t_in", 128))
                    for b in range(2):
                        ins = A(kpad[:, 4 * b:4 * b + 4, 7 * GC:23 * GC],
                                lin[b][0:16, :].rearrange("p (g c) -> p g c", g=4), ACT.Copy)
                    ins.then_inc(s.k_out, 1)

                def toeplitz(b, k):
                    act.wait_ge(s.yt_full, w.at("yt_full"))
                    A(ub[:, :, ds(k * 8, 8)].rearrange("p t g j -> p t (g j)"),
                      wide[b][:].rearrange("p (t c) -> p t c", t=2), ACT.Copy).then_inc(s.yt_out, 1)

                kernels(False)
                with w.repeat(KT // 2 - 1, k_full=2, t_in=256, yt_full=2) as i:
                    for b in range(2):
                        kernels(True)
                        toeplitz(b, i * 2 + b)
                kernels(True)
                toeplitz(0, KT - 2)
                toeplitz(1, KT - 1)
                for k in range(KT):
                    act.wait_ge(s.g_in, w.at("g_in"))
                    A(y[:, k], yT[:, k], ACT.Gelu).then_inc(s.g_done, 1)
                    act.wait_ge(s.g_done, w.at("g_done"))
                    A(h_hi[:, k], y[:, k], ACT.Copy).then_inc(s.hi_done, 1)

                with w.repeat(KT // 2, product=4, w_used=4, w_load0=32, w_load1=32, glu_done=2, sq_free=2) as i:
                    for b in range(2):
                        act.wait_ge(s.w_used, w.at("product"))
                        split(0)
                        act.wait_ge(s.w_used, w.at("product"))
                        A(sg[:], lin[1][:], ACT.Sigmoid).then_inc(s.sg_done, 1)
                        split(1)
                        act.wait_ge(s.glu_done, w.at("glu_done"))
                        act.wait_ge(s.sq_free, w.at("sq_free"))
                        A(sq[:, b], y[:, ds(i * 2 + b, 1)].rearrange("p k t -> p (k t)"),
                          ACT.Square).then_inc(s.sq_done, 1)
                w.skip("lin_out", 2 * KT)
                boundary(1, 2)

        @block.vector
        def _(dve):
            w = Counts(dve, sems)
            V = nc.vector

            def step(ins):
                ins.then_inc(s.v_step, 1)
                dve.wait_ge(s.v_step, w.at("v_step"))

            def split(parity):
                dve.wait_ge(s.w_hi_done, w.at("w_hi_done"))
                V.tensor_tensor(w_lo[:, parity], w_raw[:, parity], w_hi[:, parity].bitcast(F32),
                                ALU.subtract).then_inc(s.w_ready, 1)

            def factor(dst):
                dve.wait_ge(s.sqrt_done, w.at("sqrt_done"))
                V.reciprocal(dst, dst).then_inc(s.rstd_done, 1)
                dve.wait_ge(s.rstd_done, w.at("rstd_done"))

            def low(src, k, scale=None):
                dve.wait_ge(s.hi_done, w.at("hi_done"))
                if scale is None:
                    V.tensor_tensor(h_lo[:, k], src[:, k], h_hi[:, k].bitcast(F32), ALU.subtract).then_inc(s.h_ready, 1)
                else:
                    V.scalar_tensor_tensor(h_lo[:, k], src[:, k], scale, h_hi[:, k].bitcast(F32), ALU.mult,
                                           ALU.subtract).then_inc(s.h_ready, 1)

            def natural(ap):
                return ap.rearrange("p (s j) -> p j s", s=SB)

            def boundary(layer, post, nlayer, pre, blocked=False):
                factor(rstd[:])
                for k in range(KT):
                    step(V.tensor_tensor(tmp[:, k % 2], y[:, k], rstd[:], ALU.mult))
                    xk_, tk = x[:, k], tmp[:, k % 2]
                    if blocked:
                        xk_, tk = xk_.rearrange("p (j s) -> p j s", s=SB), natural(tk)
                    V.scalar_tensor_tensor(xk_, tk, nw(layer, post, k), xk_, ALU.mult,
                                           ALU.add).then_inc(s.x_done, 1)
                    if pre is not None and k:
                        low(x, k - 1, nw(nlayer, pre, k - 1))
                w.skip("x_done", KT)
                if pre is not None:
                    low(x, KT - 1, nw(nlayer, pre, KT - 1))
                    factor(rstd[:])

            def split_y():
                for k in range(KT):
                    low(y, k)

            def out_projection():
                with w.repeat(KT // 2, w_hi_done=2):
                    for j in range(2):
                        split(j)
                w.skip("lin_out", KT)
                w.skip("product", KT)

            V.memset(ones[:], 1.0)
            V.memset(eps[:, 1:2], float(np.pi / 2))
            V.memset(eps[:, 0:1], EPS).then_inc(s.setup, 1)
            dve.wait_ge(s.par_in, w.at("par_in", 32))
            lg = par[:, LBL:LBL + 3 * HEADS]
            step(V.tensor_tensor(lbt[:, 0:4], lg[:, 0:4], lg[:, 4:8], ALU.max))
            step(V.tensor_tensor(lbt[:, 0:4], lbt[:, 0:4], lg[:, 8:12], ALU.max))
            V.tensor_tensor(lbt[:, 4:16].rearrange("p (r h) -> p r h", r=3), lg.rearrange("p (r h) -> p r h", r=3),
                            lbt[:, 0:4].unsqueeze(1).to_broadcast([P, 3, 4]), ALU.subtract).then_inc(s.lb_max, 1)
            dve.wait_ge(s.x_in, w.at("x_in", 16))
            for k in range(KT):
                low(x, k, nw(0, 0, k))
            factor(rstd_m[:])
            factor(rstd[:])
            dve.wait_ge(s.lb_exp, w.at("lb_exp"))
            step(V.tensor_tensor(lbt[:, 16:20], lbt[:, 4:8], lbt[:, 8:12], ALU.add))
            step(V.tensor_tensor(lbt[:, 16:20], lbt[:, 16:20], lbt[:, 12:16], ALU.add))
            step(V.reciprocal(lbt[:, 20:24], lbt[:, 16:20]))
            step(V.tensor_tensor(hp[:, :, 0], lbt[:, 4:8], lbt[:, 20:24], ALU.mult))
            step(V.tensor_scalar(hp[:, :, 1], hp[:, :, 0], -1.0, 1.0, ALU.mult, ALU.add))
            step(V.tensor_copy(hp[:, :, 2], par[:, ONW:ONW + HEADS]))
            dve.wait_ge(s.s5_in, w.at("s5_in", 32))
            dve.wait_ge(s.s5_exp, w.at("s5_exp"))
            step(V.tensor_scalar(sv[:, 7], sp_in[:, 0], -1e-4, None, ALU.min))
            V.tensor_tensor(sv[:, 1], sv[:, 0], sv[:, 7], ALU.mult)
            step(V.tensor_tensor(sv[:, 2], sv[:, 0], sp_in[:, 1], ALU.mult))
            step(V.tensor_scalar(sv[:, 12], sv[:, 2], 1.0 / TWO_PI, None, ALU.mult))
            step(V.tensor_scalar(sv[:, 12], sv[:, 12], ROUND, None, ALU.add))
            step(V.tensor_scalar(sv[:, 12], sv[:, 12], -ROUND, None, ALU.add))
            for part in TURN:
                step(V.scalar_tensor_tensor(sv[:, 2], sv[:, 12], -part, sv[:, 2], ALU.mult, ALU.add))
            V.tensor_scalar(sv[:, 2], sv[:, 2], PI_IN, -PI_IN, ALU.min, ALU.max).then_inc(s.s5_mag, 1)
            dve.wait_ge(s.s5_trig, w.at("s5_trig", 2))
            step(V.tensor_tensor(sv[:, 8], sv[:, 3], sv[:, 6], ALU.mult))
            step(V.tensor_tensor(sv[:, 13], sv[:, 3], sv[:, 5], ALU.mult))
            step(V.tensor_scalar(sv[:, 9], sv[:, 13], sgn[:, 0:1], None, ALU.mult))
            step(V.tensor_scalar(sv[:, 14], sv[:, 8], -1.0, None, ALU.add))
            step(V.tensor_tensor(sv[:, 0], sv[:, 7], sv[:, 7], ALU.mult))
            step(V.tensor_tensor(sv[:, 1], sp_in[:, 1], sp_in[:, 1], ALU.mult))
            step(V.tensor_tensor(sv[:, 0], sv[:, 0], sv[:, 1], ALU.add))
            step(V.reciprocal(sv[:, 0], sv[:, 0]))
            step(V.tensor_tensor(sv[:, 1], sv[:, 14], sv[:, 7], ALU.mult))
            step(V.tensor_tensor(sv[:, 2], sv[:, 13], sp_in[:, 1], ALU.mult))
            step(V.tensor_tensor(sv[:, 1], sv[:, 1], sv[:, 2], ALU.add))
            step(V.tensor_tensor(sv[:, 10], sv[:, 1], sv[:, 0], ALU.mult))
            step(V.tensor_tensor(sv[:, 1], sv[:, 13], sv[:, 7], ALU.mult))
            step(V.tensor_tensor(sv[:, 2], sv[:, 14], sp_in[:, 1], ALU.mult))
            step(V.tensor_tensor(sv[:, 1], sv[:, 1], sv[:, 2], ALU.subtract))
            step(V.tensor_tensor(sv[:, 1], sv[:, 1], sv[:, 0], ALU.mult))
            V.tensor_scalar(sv[:, 11], sv[:, 1], sgn[:, 0:1], None, ALU.mult).then_inc(s.s5_made, 1)
            dve.wait_ge(s.con_in, w.at("con_in", 96))
            V.tensor_tensor(cosr[:], cosr[:], rstd[:], ALU.mult)
            V.tensor_tensor(sinr[:], sinr[:], rstd[:], ALU.mult)
            step(V.memset(scm[:], 0.0))
            split(0)
            split(1)
            with w.repeat(HEADS, product=8, w_hi_done=7, v_step=9 + 4 * KT, f_exp=1, f_log=1, b_exp=1, g_exp=1, a1_full=8,
                          ctr_full=8, s_full=8, p_exp=8, ao_full=8, o_root=1, st_done=8, rope_done=2, lin_out=7, o_done=1) as h:
                step(V.tensor_copy(cur[:], hp[:, ds(h, 1)].rearrange("p a b -> p (a b)")))
                dve.wait_ge(s.w_used, w.at("product"))
                V.tensor_tensor(zq[:], lin[0][:], rstd[:], ALU.mult).then_inc(s.lin_free, 1)
                split(0)
                dve.wait_ge(s.w_used, w.at("product"))
                V.tensor_tensor(zf[:], lin[1][:], rstd[:], ALU.mult).then_inc(s.lin_free, 1)
                split(1)
                dve.wait_ge(s.f_exp, w.at("f_exp"))
                step(V.tensor_scalar(zf[:], zf[:], 1.0, None, ALU.add))
                step(V.reciprocal(zf[:], zf[:]))
                V.tensor_scalar(zf[:], zf[:], cur[:, 1:2], cur[:, 0:1], ALU.mult, ALU.add).then_inc(s.f_sig, 1)
                dve.wait_ge(s.w_used, w.at("product"))
                V.tensor_tensor(zi[:], lin[0][:], rstd[:], ALU.mult).then_inc(s.lin_free, 1)
                split(0)
                dve.wait_ge(s.f_log, w.at("f_log"))
                V.tensor_tensor_scan(gb[:], first[:], ge[:], 0.0, ALU.mult, ALU.add).then_inc(s.b_scan, 1)
                dve.wait_ge(s.b_exp, w.at("b_exp"))
                V.tensor_copy(dec[:], ge[:].rearrange("p (c t) -> p c t", t=CH)[:, :, CH - 1])
                V.tensor_tensor(zq[:], zq[:], ge[:], ALU.mult).then_inc(s.q_dec, 1)
                dve.wait_ge(s.w_used, w.at("product"))
                V.tensor_tensor(zg[:], lin[1][:], rstd[:], ALU.mult).then_inc(s.lin_free, 1)
                split(1)
                for j, dst in ((0, bq), (1, bk)):
                    dve.wait_ge(s.w_used, w.at("product"))
                    if j:
                        dve.wait_ge(s.g_exp, w.at("g_exp"))
                        step(V.tensor_scalar(gb[:], gb[:], 1.0, None, ALU.add))
                        step(V.reciprocal(gb[:], gb[:]))
                        step(V.tensor_tensor(zg[:], zg[:], gb[:], ALU.mult))
                    V.tensor_tensor(dst[:], lin[j][:], cosr[:], ALU.mult)
                    V.tensor_tensor(prob[0:64, 0], lin[j][64:128, :], sinr[64:128, :], ALU.mult)
                    V.tensor_tensor(prob[64:128, 0], lin[j][0:64, :], sinr[0:64, :], ALU.mult).then_inc(s.lin_free, 1)
                    dve.wait_ge(s.lin_free, w.at("lin_out", (5, 1)[j]))
                    V.tensor_tensor(dst[:], dst[:], prob[:, 0], ALU.add).then_inc(s.rope_done, 1)
                    dve.wait_ge(s.rope_done, w.at("rope_done"))
                    if j == 0:
                        split(0)
                dve.wait_ge(s.w_used, w.at("product"))
                V.tensor_tensor(prob[:, 1], lin[0][:], rstd[:], ALU.mult).then_inc(s.lin_free, 1)
                dve.wait_ge(s.lin_free, w.at("lin_out"))
                w.skip("product")
                split(0)
                split(1)
                step(V.memset(states[:, 0], 0.0))

                for T in range(KT):
                    W = (T + 1) * P
                    dve.wait_ge(s.a1_full, w.at("a1_full"))
                    if T >= 2:
                        dve.wait_ge(s.ao_full, w.at("ao_full"))
                    dve.wait_ge(s.s_full, w.at("s_full"))
                    V.tensor_copy(vtok[:, T % 2], lin[0][:, P:2 * P])
                    V.copy_predicated(scm[:, T % 2], causal[:].bitcast(mybir.dt.uint32), lin[0][:, 0:P])
                    V.tensor_tensor(vblk, lin[0][:, P:2 * P].unsqueeze(1).to_broadcast([P, 4, P]),
                                    blk[:].unsqueeze(2).to_broadcast([P, 4, P]), ALU.mult)
                    V.tensor_copy(ktok[:], lin[0][:, 2 * P:3 * P]).then_inc(s.a1_out, 1)
                    step(V.tensor_tensor_reduce(prob[:, T % 2, 0:W], wide[0][:, 0:W], logc[:, L - W:L], 1.0, -3e38,
                                                ALU.add, ALU.max, stat[:, T % 2, 0:1]))
                    V.tensor_scalar(stat[:, T % 2, 1:2], stat[:, T % 2, 0:1], -B_SCALE, None, ALU.mult).then_inc(s.s_max, 1)
                    dve.wait_ge(s.ctr_full, w.at("ctr_full"))
                    for c in range(4):
                        n = 4 * T + c
                        ins = V.scalar_tensor_tensor(states[:, (n + 1) % 8], states[:, n % 8], dec[:, n:n + 1],
                                                     lin[0][:, HALF + c * P:HALF + (c + 1) * P], ALU.mult, ALU.add)
                        if c < 3:
                            step(ins)
                        else:
                            ins.then_inc(s.st_done, 1)
                            dve.wait_ge(s.st_done, w.at("st_done"))
                    dve.wait_ge(s.p_exp, w.at("p_exp"))
                    V.reciprocal(stat[:, T % 2, 3:4], stat[:, T % 2, 2:3]).then_inc(s.p_sum, 1)
                dve.wait_ge(s.ao_full, w.at("ao_full", 2))
                dve.wait_ge(s.o_root, w.at("o_root"))
                step(V.reciprocal(gb[:], gb[:]))
                step(V.tensor_tensor(gb[:], gb[:], zi[:], ALU.mult))
                V.scalar_tensor_tensor(y[:, ds(h, 1)].rearrange("p k t -> p (k t)"), gb[:], cur[:, 2:3], zg[:],
                                       ALU.mult, ALU.mult).then_inc(s.o_done, 1)
                dve.wait_ge(s.o_done, w.at("o_done"))
            dve.wait_ge(s.bo_out, w.at("bo_out", KT * HEADS))
            split_y()
            out_projection()
            dve.wait_ge(s.x_in, w.at("x_in", 16))
            boundary(0, 1, 0, 2)

            for layer in range(LAYERS):
                for k in range(KT):
                    dve.wait_ge(s.m_hi_done, w.at("m_hi_done"))
                    c = MNW + layer * KT + k
                    V.scalar_tensor_tensor(m_lo[:, k], m_raw[:, k], par[:, c:c + 1], m_hi[:, k].bitcast(F32),
                                           ALU.mult, ALU.subtract).then_inc(s.m_ready, 1)
                with w.repeat(HEADS, product=6, w_hi_done=6, s_full=8, p_exp=8, v_step=8):
                    for j in range(6):
                        dve.wait_ge(s.w_used, w.at("product"))
                        if j < 2:
                            V.tensor_tensor(xq[:, j], lin[j][:], rstd[:], ALU.mult).then_inc(s.lin_free, 1)
                        else:
                            V.tensor_tensor((xk, xv)[j // 4][:, j % 2], lin[j % 2][:, 0:MEM], rstd_m[:],
                                            ALU.mult).then_inc(s.lin_free, 1)
                        split(j % 2)

                    def largest(q):
                        dve.wait_ge(s.s_full, w.at("s_full"))
                        step(V.tensor_reduce(xstat[:, q % 2, 0:1], wide[0][:, (q % 2) * HALF:(q % 2) * HALF + MEM],
                                             AX, ALU.max))
                        V.tensor_scalar(xstat[:, q % 2, 1:2], xstat[:, q % 2, 0:1], -X_SCALE, None,
                                        ALU.mult).then_inc(s.s_max, 1)

                    largest(0)
                    for q in range(KT):
                        if q + 1 < KT:
                            largest(q + 1)
                        dve.wait_ge(s.p_exp, w.at("p_exp"))
                        V.reciprocal(xstat[:, q % 2, 3:4], xstat[:, q % 2, 2:3]).then_inc(s.p_sum, 1)
                w.skip("lin_out", 6 * HEADS)
                dve.wait_ge(s.bo_out, w.at("bo_out", 4 * HEADS))
                split_y()
                out_projection()
                boundary(layer, 3, layer, 4)

                def up(c):
                    for j in range(2):
                        dve.wait_ge(s.w_used, w.at("product"))
                        V.tensor_tensor(gate[:], lin[0][:], rstd[:], ALU.mult).then_inc(s.lin_free, 1)
                        w.skip("lin_out")
                        split(0)
                        dve.wait_ge(s.w_used, w.at("product"))
                        dve.wait_ge(s.silu_done, w.at("silu_done"))
                        V.tensor_tensor(gate[:], lin[1][:], rstd[:], ALU.mult).then_inc(s.lin_free, 1)
                        dve.wait_ge(s.lin_free, w.at("lin_out"))
                        V.tensor_tensor(f_act[:], f_act[:], gate[:], ALU.mult).then_inc(s.hid_done, 1)
                        split(1)
                        dve.wait_ge(s.hid_hi_done, w.at("hid_hi_done"))
                        V.tensor_tensor(hid_lo[:, 2 * (c % 2) + j], f_act[:], hid_hi[:, 2 * (c % 2) + j].bitcast(F32),
                                        ALU.subtract).then_inc(s.hid_ready, 1)

                def down(c, last):
                    for j in range(2):
                        for n in range(4 * j, 4 * j + 4):
                            if n % 4 == 3:
                                dve.wait_ge(s.w_used, w.at("product"))
                            else:
                                dve.wait_ge(s.out_full, w.at("out_full"))
                            V.tensor_tensor(y[:, n], y[:, n], wide[n % 2][:], ALU.add).then_inc(s.out_free, 1)
                        if not last:
                            split(j)

                dve.wait_ge(s.y_zero, w.at("y_zero"))
                up(0)
                with w.repeat(FC // 2, product=12, w_hi_done=12, out_full=12, silu_done=4, hid_hi_done=4, lin_out=8):
                    up(1)
                    down(0, False)
                    up(0)
                    down(1, False)
                down(FC - 1, layer == LAYERS - 1)
                if layer == 0:
                    dve.wait_ge(s.x_back, w.at("x_back", 16))
                boundary(layer, 5, None, None)
                if layer == LAYERS - 1:
                    continue
                factor(rstd[:])
                for k in range(KT):
                    V.scalar_tensor_tensor(natural(y[:, k]), x[:, k].rearrange("p (j s) -> p j s", s=SB), nw(1, 0, k),
                                           rstd[:].rearrange("p (j s) -> p j s", s=SB), ALU.mult,
                                           ALU.mult).then_inc(s.u_done, 1)
                with w.repeat(KT // 2, m1_full=4, x_full=2) as i:
                    for b in range(2):
                        dve.wait_ge(s.m1_full, w.at("m1_full", 2))
                        src = lin[1][:].rearrange("p (g c) -> p g c", g=8)
                        V.tensor_copy(m1[:, 0, 1], src)
                        V.tensor_copy(m1[:, 1, 1].rearrange("p g (h c) -> p g h c", h=2),
                                      src.rearrange("p g (h c) -> p g h c", h=2)[:, :, ::-1]).then_inc(s.m1b_out, 1)
                        dve.wait_ge(s.x_full, w.at("x_full"))
                        V.tensor_copy(hs[:, :, ds(i * 16 + 8 * b, 8)].rearrange("p o g j -> p o (g j)"),
                                      wide[b][:].rearrange("p (o c) -> p o c", o=2)).then_inc(s.x_out, 1)
                dve.wait_ge(s.pw_in, w.at("pw_in", 32))
                dve.wait_ge(s.x_out, w.at("x_taken", KT))
                step(V.tensor_scalar(sai_b[:, 0], sai_b[:, 1], -1.0, None, ALU.mult))

                UNROLL = 7
                with w.repeat((NB - 1) // UNROLL, v_step=4 * UNROLL) as i:
                    for n in range(UNROLL):
                        prev = hs[:, :, :, ds(i * UNROLL + n, 1)].rearrange("p o g j -> p o (g j)")
                        here = hs[:, :, :, ds(i * UNROLL + n + 1, 1)].rearrange("p o g j -> p o (g j)")
                        V.tensor_tensor(sc1[:], ar_b[:].unsqueeze(1).to_broadcast([P, 2, GR]), prev,
                                        ALU.mult).then_inc(s.v_step, 1)
                        V.tensor_tensor(sc2[:, ::-1], sai_b[:], prev, ALU.mult).then_inc(s.v_step, 1)
                        dve.wait_ge(s.v_step, w.at("v_step"))
                        V.tensor_tensor(sc1[:], sc1[:], here, ALU.add).then_inc(s.v_step, 1)
                        dve.wait_ge(s.v_step, w.at("v_step", 2))
                        step(V.tensor_tensor(here, sc1[:], sc2[:], ALU.add))
                dve.sem_inc(s.scan_done, 1)
                dve.wait_ge(s.yt_out, w.at("yt_out", KT))
                with w.repeat(KT // 2, y2_full=2) as i:
                    for b in range(2):
                        dve.wait_ge(s.y2_full, w.at("y2_full"))
                        v = ub[:, :, ds(i * 16 + 8 * b, 8), 1:NB]
                        V.tensor_tensor(v, wide[b][:].rearrange("p (t g j) -> p t g j", t=2, g=8)[:, :, :, 1:NB], v,
                                        ALU.add).then_inc(s.y2_out, 1)
                dve.wait_ge(s.yT_in, w.at("yT_in", 16))
                for k in range(KT):
                    V.scalar_tensor_tensor(yT[:, k], y[:, k], par[:, SD + k:SD + k + 1], yT[:, k], ALU.mult,
                                           ALU.add).then_inc(s.g_in, 1)
                    if k:
                        low(y, k - 1)
                low(y, KT - 1)
                with w.repeat(KT // 2, w_hi_done=4, sg_done=2, glu_done=2, product=4) as i:
                    for b in range(2):
                        dve.wait_ge(s.w_used, w.at("product"))
                        split(0)
                        dve.wait_ge(s.w_used, w.at("product"))
                        dve.wait_ge(s.sg_done, w.at("sg_done"))
                        V.tensor_tensor(y[:, ds(i * 2 + b, 1)].rearrange("p k t -> p (k t)"), lin[0][:], sg[:],
                                        ALU.mult).then_inc(s.glu_done, 1)
                        dve.wait_ge(s.glu_done, w.at("glu_done"))
                        dve.sem_inc(s.lin_free, 2)
                        split(1)
                w.skip("lin_out", 2 * KT)
                boundary(1, 1, 1, 2, blocked=True)

        @block.gpsimd
        def _(pool):
            w = Counts(pool, sems)
            G = nc.gpsimd

            def sum_squares():
                for k in range(KT):
                    pool.wait_ge(s.sq_done, w.at("sq_done"))
                    if k == 0:
                        G.tensor_copy(acc[:], sq[:, 0]).then_inc(s.sq_free, 1)
                    else:
                        G.tensor_tensor(acc[:], acc[:], sq[:, k % 2], ALU.add).then_inc(s.sq_free, 1)
                    pool.wait_ge(s.sq_free, w.at("acc_sum"))

            def boundary(pre=True):
                if pre:
                    sum_squares()

            def step(ins):
                ins.then_inc(s.g_step, 1)
                pool.wait_ge(s.g_step, w.at("g_step"))

            def operators():
                pool.wait_ge(s.h_ready, w.at("h_ready", 5 * KT))
                pool.dma_start(t["x_d"].rearrange("(k p) t -> p k t", p=P), x[:]).then_inc(s.x_sent, 16)
                pool.wait_ge(s.x_sent, w.at("x_sent", 16))
                pool.dma_start(pc[:], t["pc_d"]).then_inc(s.ops_in, 16)
                pool.dma_start(o_src[0][:].rearrange("p g c -> p (g c)"), t["s5_b"][0]).then_inc(s.ops_in, 16)
                pool.dma_start(o_src[1][:].rearrange("p g c -> p (g c)"), t["s5_b"][1]).then_inc(s.ops_in, 16)
                pool.wait_ge(s.ops_in, w.at("ops_in", 48))

                def wide_(ap):
                    return ap.unsqueeze(2).to_broadcast([P, GR, GC])

                for own, sign in ((0, ALU.add), (1, ALU.subtract)):
                    step(G.tensor_tensor(o_dst[own][:], o_src[own][:], wide_(pc[:, 2]), ALU.mult))
                    step(G.tensor_tensor(o_tmp[:], o_src[1 - own][:], wide_(pc[:, 3]), ALU.mult))
                    step(G.tensor_tensor(o_dst[own][:], o_dst[own][:], o_tmp[:], sign))

                def first_power():
                    G.memset(pw[:, 0], 1.0)
                    step(G.memset(pw[:, 1], 0.0))

                def one(src, dst, dram, at, b, advance=True):
                    ins = G.tensor_tensor(dst[b][:], src[0][:], wide_(pw[:, 0]), ALU.mult)
                    ins = G.tensor_tensor(o_tmp[:], src[1][:], wide_(pw[:, 1]), ALU.mult)
                    if advance:
                        G.tensor_tensor(pt[:, 0], pw[:, 0], pc[:, 0], ALU.mult)
                        G.tensor_tensor(pt[:, 1], pw[:, 1], pc[:, 1], ALU.mult)
                        G.tensor_tensor(pt[:, 2], pw[:, 0], pc[:, 1], ALU.mult)
                        ins = G.tensor_tensor(pt[:, 3], pw[:, 1], pc[:, 0], ALU.mult)
                    step(ins)
                    step(G.tensor_tensor(dst[b][:], dst[b][:], o_tmp[:], ALU.add))
                    if advance:
                        G.tensor_tensor(pw[:, 0], pt[:, 0], pt[:, 1], ALU.subtract)
                    pool.dma_start(dram[ds(at, 1)].rearrange("a p c -> p (a c)"),
                                   dst[b][:].rearrange("p g c -> p (g c)")).then_inc((s.ops_out0, s.ops_out1)[b], 16)
                    if advance:
                        step(G.tensor_tensor(pw[:, 1], pt[:, 2], pt[:, 3], ALU.add))

                first_power()
                for n in range(2):
                    one(o_dst, o_src, t["w_d"], SB - 1 - n, n)
                with w.repeat(SB // 2 - 1, g_step=6, ops_out0=16, ops_out1=16) as i:
                    for b in range(2):
                        pool.wait_ge((s.ops_out0, s.ops_out1)[b], w.at(f"ops_out{b}", 16))
                        one(o_dst, o_src, t["w_d"], i * -2 + (SB - 3 - b), b)
                pool.wait_ge(s.ops_out0, w.at("ops_out0", 16))
                pool.wait_ge(s.ops_out1, w.at("ops_out1", 16))
                pool.dma_start(o_src[0][:].rearrange("p g c -> p (g c)"), t["s5_c"][0]).then_inc(s.ops_in, 16)
                pool.dma_start(o_src[1][:].rearrange("p g c -> p (g c)"), t["s5_c"][1]).then_inc(s.ops_in, 16)
                pool.wait_ge(s.ops_in, w.at("ops_in", 32))
                for b in range(2):
                    step(G.tensor_tensor(o_src[b][:], o_src[b][:], wide_(sgn[:, 1:2].to_broadcast([P, GR])), ALU.mult))
                first_power()
                for n in range(2):
                    one(o_src, o_dst, t["dd_d"], n, n)
                with w.repeat(SB // 2 - 1, g_step=6, ops_out0=16, ops_out1=16) as i:
                    for b in range(2):
                        pool.wait_ge((s.ops_out0, s.ops_out1)[b], w.at(f"ops_out{b}", 16))
                        one(o_src, o_dst, t["dd_d"], i * 2 + (2 + b), b)
                pool.wait_ge(s.ops_out0, w.at("ops_out0", 16))
                one(o_src, o_dst, t["dd_d"], SB, 0, advance=False)
                pool.dma_start(t["pw_d"], pw[:]).then_inc(s.ops_out1, 16)
                pool.wait_ge(s.ops_out0, w.at("ops_out0", 16))
                pool.wait_ge(s.ops_out1, w.at("ops_out1", 32))
                pool.dma_start(x[:], t["x_d"].rearrange("(k p) t -> p k t", p=P)).then_inc(s.x_back, 16)

            pool.wait_ge(s.sq_done, w.at("sq_done"))
            sum_squares()
            with w.repeat(HEADS, b_neg=1, q_dec=1, b_left_exp=1, p_sum=8):
                pool.wait_ge(s.b_neg, w.at("b_neg"))
                G.tensor_tensor(zf[:], zf[:], gk[:], ALU.mult).then_inc(s.k_inv, 1)
                pool.wait_ge(s.q_dec, w.at("q_dec"))
                b3 = gb[:].rearrange("p (c t) -> p c t", t=CH)
                G.tensor_tensor(ge[:].rearrange("p (c t) -> p c t", t=CH), b3[:, :, CH - 1:CH].to_broadcast([P, NCH, CH]),
                                b3, ALU.subtract).then_inc(s.b_left, 1)
                pool.wait_ge(s.b_left_exp, w.at("b_left_exp"))
                G.tensor_tensor(gk[:], gk[:], ge[:], ALU.mult).then_inc(s.k_end, 1)
                for T in range(KT):
                    W = (T + 1) * P
                    pool.wait_ge(s.p_sum, w.at("p_sum"))
                    G.tensor_tensor(prob[:, T % 2, 0:W], prob[:, T % 2, 0:W],
                                    stat[:, T % 2, 3:4].to_broadcast([P, W]), ALU.mult).then_inc(s.p_ready, 1)
            sum_squares()
            boundary()
            for layer in range(LAYERS):
                w.skip("x_done", KT)
                with w.repeat(HEADS, p_sum=8):
                    for q in range(KT):
                        pool.wait_ge(s.p_sum, w.at("p_sum"))
                        G.tensor_tensor(xp[:, q % 2], xp[:, q % 2], xstat[:, q % 2, 3:4].to_broadcast([P, MEM]),
                                        ALU.mult).then_inc(s.p_ready, 1)
                sum_squares()
                boundary()
                pool.wait_ge(s.x_done, w.at("x_done", KT))
                G.memset(y[:], 0.0).then_inc(s.y_zero, 1)
                if layer == 0:
                    operators()
                sum_squares()
                if layer + 1 < LAYERS:
                    pool.wait_ge(s.x_done, w.at("x_done", KT))
                    sum_squares()

                    one4 = ones[:, 0:1].unsqueeze(2).unsqueeze(3).to_broadcast([P, SB, 8, GC])

                    def by_group(dst, src):
                        return G.tensor_tensor(dst[:].rearrange("p g n c -> p n g c"),
                                               src.rearrange("p n (g c) -> p n g c", c=GC),
                                               one4, ALU.mult)

                    with w.repeat(KT // 2, wt_in0=16, wt_in1=16, m1_full=4):
                        for b in range(2):
                            pool.wait_ge((s.wt_in0, s.wt_in1)[b], w.at(f"wt_in{b}", 16))
                            by_group(wr, wt[b][:]).then_inc(s.wr_done, 1)
                            pool.wait_ge(s.m1_full, w.at("m1_full", 2))
                    pool.wait_ge(s.yt_full, w.at("yt_full", KT))
                    pool.wait_ge(s.d_in0, w.at("d_in0", 16 * KT))
                    pool.wait_ge(s.d_in1, w.at("d_in1", 16 * KT))
                    for b in range(2):
                        pool.wait_ge((s.d_in0, s.d_in1)[b], w.at(f"d_in{b}", 16))
                        by_group(dr[b], dt_[b][:, 1:]).then_inc(s.dr_done, 1)
                    with w.repeat(KT // 2 - 1, d_in0=16, d_in1=16, y2_full=2):
                        for b in range(2):
                            pool.wait_ge(s.y2_full, w.at("y2_full"))
                            pool.wait_ge((s.d_in0, s.d_in1)[b], w.at(f"d_in{b}", 16))
                            by_group(dr[b], dt_[b][:, 1:]).then_inc(s.dr_done, 1)
                    sum_squares()
                    sum_squares()

        @block.tensor
        def _(pe):
            w = Counts(pe, sems)
            MM = nc.tensor.matmul
            for sem in (s.w_used, s.lin_free, s.out_free, s.sq_free, s.x_out, s.y2_out):
                pe.sem_inc(sem, 2)

            def passes(out, w_h, w_l, a_h, a_l, first, last, spans):
                for n, (a, b) in enumerate(((w_h, a_h), (w_h, a_l), (w_l, a_h))):
                    for lo_, hi_ in spans:
                        ins = MM(out[:, lo_:hi_], a, b[:, lo_:hi_], start=first and n == 0, stop=last and n == 2)
                return ins

            TOK = ((0, HALF), (HALF, L))

            def linear(parity, a_h, a_l, spans=TOK, used=1):
                pe.wait_ge(s.w_ready, w.at("w_ready"))
                pe.wait_ge(s.lin_free, w.at("lin_free"))
                for k in range(KT):
                    ins = passes(lin[parity], col8(w_hi, parity)[:, k], col8(w_lo, parity)[:, k], a_h[:, k], a_l[:, k],
                                 k == 0, k == KT - 1, spans)
                ins.then_inc(s.w_used, used)

            def sum_features():
                pe.wait_ge(s.sq_free, w.at("acc_sum", KT))
                for lo_, hi_ in TOK:
                    ins = MM(wide[0][:, lo_:hi_], ones[:], acc[:, lo_:hi_], start=True, stop=True)
                ins.then_inc(s.stat_full, 1)

            def out_projection():
                pe.wait_ge(s.h_ready, w.at("h_ready", KT))
                with w.repeat(KT // 2, w_ready=2, lin_free=2):
                    for j in range(2):
                        linear(j, h_hi, h_lo)
                w.skip("lin_out", KT)
                sum_features()

            pe.wait_ge(s.sq_done, w.at("sq_done"))
            for k in range(KT):
                ins = MM(wide[1][:, 0:MEM], ones[:], m_sq[:, k], start=k == 0, stop=k == KT - 1)
            ins.then_inc(s.stat_full, 1)
            pe.wait_ge(s.par_in, w.at("par_in", 32))
            sum_features()
            pe.wait_ge(s.h_ready, w.at("h_ready", KT))
            with w.repeat(HEADS, w_ready=7, lin_free=7, lin_out=7, q_dec=1, k_inv=1, k_end=1, rope_done=2, vt_out=1,
                          a1_out=8, s_max=8, st_done=8, ao_out=8, bo_out=8, t_out=8, p_ready=8, o_sq=1, o_root=0):
                for j in range(7):
                    linear(j % 2, h_hi, h_lo, used=2 if j == 6 else 1)
                pe.wait_ge(s.lin_free, w.at("lin_out", 7))
                pe.wait_ge(s.q_dec, w.at("q_dec"))
                pe.wait_ge(s.k_inv, w.at("k_inv"))
                pe.wait_ge(s.k_end, w.at("k_end"))
                pe.wait_ge(s.rope_done, w.at("rope_done", 2))

                def a_tile(T):
                    c = slice(T * P, (T + 1) * P)
                    MM(lin[0][:, 0:P], zf[:, c], zq[:, c], start=True, stop=True)
                    nc.tensor.transpose(lin[0][:, P:2 * P], zi[:, c], ident[:])
                    nc.tensor.transpose(lin[0][:, 2 * P:3 * P], gk[:, c], ident[:]).then_inc(s.a1_full, 1)

                def b_scores(T):
                    if T:
                        pe.wait_ge(s.s_max, w.at("s_max"))
                    W = (T + 1) * P
                    for lo_ in range(0, W, HALF):
                        hi_ = min(W, lo_ + HALF)
                        ins = MM(wide[0][:, lo_:hi_], bq[:, T * P:(T + 1) * P], bk[:, lo_:hi_], start=True, stop=True)
                    ins.then_inc(s.s_full, 1)

                def a_output(T):
                    pe.wait_ge(s.st_done, w.at("st_done"))
                    if T:
                        pe.wait_ge(s.ao_out, w.at("ao_out"))
                    MM(lin[1][:, 0:P], vtok[:, T % 2], scm[:, T % 2], start=True, stop=True)
                    for c in range(4):
                        n = 4 * T + c
                        ins = MM(lin[1][:, c * CH:(c + 1) * CH], states[:, n % 8], zq[:, n * CH:(n + 1) * CH],
                                 start=False, stop=True, skip_group_check=True)
                    ins.then_inc(s.ao_full, 1)

                def b_output(T):
                    pe.wait_ge(s.t_out, w.at("t_out"))
                    if T:
                        pe.wait_ge(s.bo_out, w.at("bo_out"))
                    for k in range(T + 1):
                        ins = MM(lin[1][:, HALF:HALF + P], vtok_b[:, k], probT[:, k], start=k == 0, stop=k == T)
                    ins.then_inc(s.bo_full, 1)

                for T in range(KT):
                    a_tile(T)
                    b_scores(T)
                    if T == 0:
                        for k in range(KT):
                            ins = nc.tensor.transpose(wide[1][:, k * P:(k + 1) * P], prob[:, 1, k * P:(k + 1) * P], ident[:])
                        ins.then_inc(s.vt_full, 1)
                    else:
                        a_output(T - 1)
                        b_output(T - 1)
                    pe.wait_ge(s.a1_out, w.at("a1_out"))
                    MM(lin[0][:, HALF:L], ktok[:], vblk.rearrange("p c v -> p (c v)"), start=True,
                       stop=True).then_inc(s.ctr_full, 1)
                    pe.wait_ge(s.p_ready, w.at("p_ready"))
                    if T == 0:
                        pe.wait_ge(s.vt_out, w.at("vt_out"))
                    for k in range(T + 1):
                        ins = nc.tensor.transpose(wide[1][:, k * P:(k + 1) * P], prob[:, T % 2, k * P:(k + 1) * P], ident[:])
                    ins.then_inc(s.t_full, 1)
                a_output(KT - 1)
                b_output(KT - 1)
                pe.wait_ge(s.s_max, w.at("s_max"))
                pe.wait_ge(s.o_sq, w.at("o_sq"))
                for lo_, hi_ in TOK:
                    ins = MM(wide[0][:, lo_:hi_], ones[:], ge[:, lo_:hi_], start=True, stop=True)
                ins.then_inc(s.o_stat, 1)
                pe.wait_ge(s.ao_out, w.at("ao_out"))
                pe.wait_ge(s.bo_out, w.at("bo_out"))
            out_projection()
            sum_features()

            for layer in range(LAYERS):
                pe.wait_ge(s.h_ready, w.at("h_ready", KT))
                with w.repeat(HEADS, w_ready=6, lin_free=6, lin_out=6, vt_out=1, p_exp=8, p_ready=8, t_out=8, bo_out=4):
                    for j in range(6):
                        if j == 2:
                            pe.wait_ge(s.m_ready, KT * (layer + 1))
                        if j < 2:
                            linear(j, h_hi, h_lo)
                        else:
                            linear(j % 2, m_hi, m_lo, ((0, MEM),))
                    pe.wait_ge(s.lin_free, w.at("lin_out", 6))
                    for k in range(2):
                        for j in range(2):
                            c = (2 * k + j) * P
                            ins = nc.tensor.transpose(wide[0][:, c:c + P], xv[:, j, k * P:(k + 1) * P], ident[:])
                    ins.then_inc(s.vt_full, 1)
                    pe.wait_ge(s.vt_out, w.at("vt_out"))

                    def scores(q):
                        if q >= 2:
                            pe.wait_ge(s.p_exp, w.at("p_exp"))
                        c = (q % 2) * HALF
                        for j in range(2):
                            ins = MM(wide[0][:, c:c + MEM], xq[:, j, q * P:(q + 1) * P], xk[:, j], start=j == 0, stop=j == 1)
                        ins.then_inc(s.s_full, 1)

                    scores(0)
                    for q in range(KT):
                        if q + 1 < KT:
                            scores(q + 1)
                        pe.wait_ge(s.p_ready, w.at("p_ready"))
                        if q % 4:
                            pe.wait_ge(s.t_out, w.at("t_out"))
                        for k in range(2):
                            ins = nc.tensor.transpose(wide[1][:, k * P:(k + 1) * P], xp[:, q % 2, k * P:(k + 1) * P], ident[:])
                        ins.then_inc(s.t_full, 1)
                        if q % 4 == 3:
                            pe.wait_ge(s.t_out, w.at("t_out"))
                            for j in range(2):
                                for k in range(2):
                                    ins = MM(lin[q // 4][:, j * HALF:(j + 1) * HALF], xvt[:, k, j * P:(j + 1) * P], xpT[:, k],
                                             start=k == 0, stop=k == 1)
                                ins.then_inc(s.bo_full, 1)
                    pe.wait_ge(s.p_exp, w.at("p_exp", 2))
                    pe.wait_ge(s.bo_out, w.at("bo_out", 4))
                out_projection()
                sum_features()
                pe.wait_ge(s.h_ready, w.at("h_ready", KT))

                def up():
                    for j in range(2):
                        linear(0, h_hi, h_lo)
                        linear(1, h_hi, h_lo)

                def down(c):
                    pe.wait_ge(s.hid_ready, w.at("hid_ready", 2))
                    for j in range(2):
                        pe.wait_ge(s.w_ready, w.at("w_ready"))
                        for n in range(4):
                            pe.wait_ge(s.out_free, w.at("out_free"))
                            for k in range(2):
                                m = n * P
                                t_ = 2 * (c % 2) + k
                                ins = passes(wide[n % 2], col2(w_hi, j)[:, k, m:m + P], col2(w_lo, j)[:, k, m:m + P],
                                             hid_hi[:, t_], hid_lo[:, t_], k == 0, k == 1, TOK)
                            ins.then_inc(s.w_used if n == 3 else s.out_full, 1)

                up()
                with w.repeat(FC // 2, w_ready=12, lin_free=8, hid_ready=4, out_free=16):
                    up()
                    down(0)
                    up()
                    down(1)
                down(FC - 1)
                w.skip("lin_out", 2 * FT)
                w.skip("sum_out", FC * KT)
                sum_features()
                if layer == LAYERS - 1:
                    continue
                sum_features()

                def u_dyn(t2, g):
                    return ub[:, t2, ds(g, 1)].rearrange("p g j -> p (g j)")

                with w.repeat(KT // 2, wr_done=2, m1a_out=2, m1b_out=2, x_out=2) as i:
                    for b in range(2):
                        pe.wait_ge(s.wr_done, w.at("wr_done"))
                        for t2 in range(2):
                            for g in range(8):
                                ins = nc.tensor.transpose(lin[t2][:, g * P:(g + 1) * P],
                                                          wr[:, g, 8 * t2:8 * t2 + 8].rearrange("p n c -> p (n c)"), ident[:])
                            ins.then_inc(s.m1_full, 1)
                        pe.wait_ge(s.m1a_out, w.at("m1a_out"))
                        pe.wait_ge(s.m1b_out, w.at("m1b_out"))
                        pe.wait_ge(s.u_in, 16 * SB)
                        pe.wait_ge(s.x_out, w.at("x_out"))
                        for o in range(2):
                            for g in range(8):
                                for t2 in range(2):
                                    ins = MM(wide[b][:, o * HALF + g * NB:o * HALF + (g + 1) * NB], m1[:, o, t2, g],
                                             u_dyn(t2, i * 16 + (8 * b + g)), start=t2 == 0, stop=t2 == 1)
                        ins.then_inc(s.x_full, 1)
                pe.wait_ge(s.x_out, w.at("x_out", 2))

                def kernels(b):
                    pe.wait_ge((s.d_in0, s.d_in1)[b], w.at(f"d_in{b}", 32))
                    for g in range(8):
                        ins = MM(lin[g // 4][0:16, (g % 4) * 256:(g % 4 + 1) * 256], w15[b][:, g * GC:(g + 1) * GC],
                                 dt_[b][:, 0:SB, g * GC:(g + 1) * GC], start=True, stop=True)
                    ins.then_inc(s.k_full, 1)

                def toeplitz(b, k8, wait):
                    pe.wait_ge(s.t_in, w.at("t_in", 128))
                    if wait:
                        pe.wait_ge(s.yt_out, w.at("yt_out"))
                    for g in range(8):
                        MM(wide[b][:, g * NB:(g + 1) * NB], tz[:, g, 0:P], u_dyn(0, k8 + g), start=True, stop=True)
                        o = wide[b][:, HALF + g * NB:HALF + (g + 1) * NB]
                        MM(o, tz[:, g, 0:P], u_dyn(1, k8 + g), start=True, stop=False)
                        ins = MM(o, tz[:, g, P:2 * P], u_dyn(0, k8 + g), start=False, stop=True)
                    ins.then_inc(s.yt_full, 1)

                kernels(0)
                pe.wait_ge(s.k_out, w.at("k_out"))
                with w.repeat(KT // 2 - 1, d_in0=32, d_in1=32, t_in=256, yt_out=2, k_out=2) as i:
                    for b in range(2):
                        kernels(1 - b)
                        toeplitz(b, i * 16 + 8 * b, False)
                        pe.wait_ge(s.yt_out, w.at("yt_out"))
                        pe.wait_ge(s.k_out, w.at("k_out"))
                kernels(1)
                toeplitz(0, (KT - 2) * 8, False)
                pe.wait_ge(s.yt_out, w.at("yt_out"))
                pe.wait_ge(s.k_out, w.at("k_out"))
                toeplitz(1, (KT - 1) * 8, False)
                pe.wait_ge(s.yt_out, w.at("yt_out"))
                pe.wait_ge(s.scan_done, w.at("scan_done"))
                with w.repeat(KT // 2, dr_done=2, y2_out=2) as i:
                    for b in range(2):
                        pe.wait_ge(s.dr_done, w.at("dr_done"))
                        pe.wait_ge(s.y2_out, w.at("y2_out"))
                        for t2 in range(2):
                            for g in range(8):
                                c = t2 * HALF + g * NB
                                ins = MM(wide[b][:, c + 1:c + NB], dr[b][:, g, 8 * t2:8 * t2 + 8].rearrange("p n c -> p (n c)"),
                                         hs[:, 0, ds(i * 16 + (8 * b + g), 1), 0:NB - 1].rearrange("p g j -> p (g j)"),
                                         start=True, stop=True)
                        ins.then_inc(s.y2_full, 1)
                pe.wait_ge(s.h_ready, w.at("h_ready", KT))
                with w.repeat(KT, w_ready=2, lin_free=2):
                    for j in range(2):
                        linear(j, h_hi, h_lo)
                w.skip("lin_out", 2 * KT)
                sum_features()
                sum_features()


_IN = ("ab_w_in", "ab_w_out", "s5_w_glu", "xattn_wq", "xattn_wkv", "xattn_wo", "ffn_w_in", "ffn_w_out")


def constants():
    c = np.zeros((P, NCON), np.float32)
    c[:, C_ID:C_ID + P] = np.eye(P)
    i = np.arange(P)
    c[:, C_CAUSAL:C_CAUSAL + P] = (i[:, None] // CH == i[None] // CH) & (i[:, None] <= i[None])
    c[:, C_BLK:C_BLK + 4] = i[:, None] // CH == np.arange(4)[None]
    back = i[:, None] + (L - P) - np.arange(L)[None]
    times = (back >= 0) * ((back <= 128) * 1.0 + ((back % 4 == 0) & (back <= 512)) + (back % 16 == 0))
    c[:, C_LOGC:C_LOGC + L] = np.where(times > 0, np.log(np.maximum(times, 1)) / B_SCALE, -1e30)
    half = 64
    freq = np.float32(10000.0) ** (-np.arange(half, dtype=np.float32) / half)
    ang = (np.arange(L, dtype=np.float32)[None] * freq[:, None]).astype(np.float32).astype(np.float64)
    c[:, C_COS:C_COS + L] = np.tile(np.cos(ang), (2, 1))
    c[:, C_SIN:C_SIN + L] = np.concatenate([np.sin(ang), -np.sin(ang)])
    c[:, C_SIGN] = np.where(i < 64, -1, 1)
    c[:, C_SIGN + 1] = np.where(i < 64, 1, -1)
    c[:, C_FIRST:C_FIRST + L] = (np.arange(L) % CH != 0)[None]
    return c


def kernel(**inputs):
    import concourse.bacc as bacc
    from concourse.bass_utils import run_bass_kernel_spmd

    a = {k: np.asarray(v) for k, v in inputs.items()}
    arrays = {n: np.ascontiguousarray(a[n]) for n in _IN}
    arrays["xT"] = np.ascontiguousarray(a["x"][0].T)
    arrays["memT"] = np.ascontiguousarray(a["mem"][0].T)

    def tiles(v):
        return np.moveaxis(v.reshape(*v.shape[:-1], -1, P), -1, 0).reshape(P, -1)

    arrays["par"] = np.concatenate([tiles(a[n]) for n in ("norm_w", "mem_norm_w", "hgrn_lb_logits",
                                                          "hgrn_out_norm_w", "s5_d")], axis=1)
    arrays["con"] = constants()
    lr, li = a["s5_lambda_re"][0].T, a["s5_lambda_im"][0].T
    dt = np.broadcast_to(a["s5_log_dt"][0][None], lr.shape)
    arrays["s5_small"] = np.tile(np.concatenate([lr, li, dt], axis=1), (2, 1))
    for n, re, im in (("s5_b", a["s5_b_re"][0].transpose(1, 0, 2), a["s5_b_im"][0].transpose(1, 0, 2)),
                      ("s5_c", a["s5_c_re"][0].transpose(2, 0, 1), a["s5_c_im"][0].transpose(2, 0, 1))):
        re, im = re.reshape(64, -1), im.reshape(64, -1)
        arrays[n] = np.stack([np.concatenate([re, im]), np.concatenate([im, re])])
    nc = bacc.Bacc("TRN2", target_bir_lowering=False, num_devices=1)
    t = {n: nc.dram_tensor(n, v.shape, F32, kind="ExternalInput").ap() for n, v in arrays.items()}
    t["out"] = nc.dram_tensor("out", (D, L), F32, kind="ExternalOutput").ap()
    for n, shape in (("u_d", (D, L)), ("y_d", (D, L)), ("x_d", (D, L)), ("w_d", (SB, P, GR * GC)),
                     ("dd_d", (SB + 1, P, GR * GC)), ("pc_d", (P, 4, GR)), ("pw_d", (P, 2, GR))):
        t[n] = nc.dram_tensor(n, shape, F32, kind="Internal").ap()
    program(nc, t)
    r = run_bass_kernel_spmd(nc, [arrays], core_ids=[0])
    return np.ascontiguousarray(r.results[0]["out"].T)[None]
```

```python
from contextlib import ExitStack, contextmanager

import concourse.bass as bass
import numpy as np
from concourse import mybir

F32 = mybir.dt.float32
F32R = mybir.dt.float32r
ALU = mybir.AluOpType
ACT = mybir.ActivationFunctionType
AX = mybir.AxisListType.X
ds = bass.ds

P = 128
D = 1024
L = 1024
LAYERS = 2
KT = D // P
HALF = 512
MEM = 256
DFF = 2816
FT = DFF // P
FC = FT // 2
HEADS = 4
CH = 32
NCH = L // CH
EPS = 1e-6
B_SCALE = 128 ** -0.5
X_SCALE = 256 ** -0.5
AW = 512

GR = 64
GC = 16
SB = 16
NB = L // SB

TWO_PI = 2 * np.pi
ROUND = 1.5 * 2 ** 23
TURN = (6.28125, 0.0019350051879882812, float(TWO_PI - 6.28125 - 0.0019350051879882812))
PI_IN = 3.1415925

NW = 0
MNW = NW + 2 * 6 * KT
LBL = MNW + 2 * KT
ONW = LBL + 3 * HEADS
SD = ONW + HEADS
NPAR = SD + KT
C_ID = 0
C_CAUSAL = C_ID + P
C_BLK = C_CAUSAL + P
C_SIGN = C_BLK + 4
C_LOGC = C_SIGN + 4
C_COS = C_LOGC + L
C_SIN = C_COS + L
C_FIRST = C_SIN + L
NCON = C_FIRST + L


ALIASES = (("product", 2), ("w_split", 2), ("lin_out", 2), ("sum_out", 2), ("acc_sum", 2), ("x_taken", 2), ("y2_added", 2))


class Count:

    def __init__(self, n=0):
        self.n, self.i, self.per, self.base = n, None, 0, 0

    def next(self, k=1):
        self.n += k
        return self.n if self.i is None else self.i * self.per + self.n


class Counts:

    def __init__(self, eng, names):
        self.eng = eng
        self.c = {name: Count() for name in names}
        for name, primed in ALIASES:
            self.c[name] = Count(primed)

    def at(self, name, k=1):
        return self.c[name].next(k)

    def skip(self, name, k=1):
        self.c[name].next(k)

    @contextmanager
    def repeat(self, n, **per):
        with self.eng.Fori(0, n) as i:
            for name, c in self.c.items():
                c.i, c.per, c.base = i, per.get(name, 0), c.n
            yield i
            for name, c in self.c.items():
                assert c.n - c.base == c.per, (name, c.n - c.base, c.per)
                c.i, c.n = None, c.base + c.per * n


def program(nc, t):
    with ExitStack() as ctx:
        def place(name, shape, dt, at):
            return nc.alloc_sbuf_tensor_at(name, shape, dt, offset=BASE + at)

        BASE = (nc.sbuf_base + 31) // 32 * 32
        KB = 1024
        FENCE = 163 * KB + 45 * KB - 256
        ctx.enter_context(nc.sbuf_tensor("fence", [P, FENCE // 4], F32))
        x = place("x", [P, KT, L], F32, 0)
        h_hi = place("h_hi", [P, KT, L], F32R, 32 * KB)
        h_lo = place("h_lo", [P, KT, L], F32R, 64 * KB)
        y = place("y", [P, KT, L], F32, 96 * KB)
        w_raw = place("w_raw", [P, 2, L], F32, 128 * KB)
        w_hi = place("w_hi", [P, 2, L], F32R, 136 * KB)
        w_lo = place("w_lo", [P, 2, L], F32R, 144 * KB)
        rstd = place("rstd", [P, L], F32, 152 * KB)
        acc = place("acc", [P, L], F32, 156 * KB)
        ident = place("ident", [P, P], F32, 160 * KB)
        ones = place("ones", [P, P], F32, 160 * KB + 512)
        par = place("par", [P, NPAR], F32, 161 * KB)
        eps = place("eps", [P, 2], F32, 161 * KB + 640)
        lbt = place("lbt", [P, 8 * HEADS], F32, 161 * KB + 704)
        root8 = place("root8", [P, KT], F32, 161 * KB + 832)
        rstd_m = place("rstd_m", [P, MEM], F32, 162 * KB)
        A0 = 163 * KB
        sq = place("sq", [P, 2, L], F32, A0 + 32 * KB)
        tmp = place("tmp", [P, 2, L], F32, A0)

        zq = place("zq", [P, L], F32, 0)
        zf = place("zf", [P, L], F32, 4 * KB)
        zi = place("zi", [P, L], F32, 8 * KB)
        zg = place("zg", [P, L], F32, 12 * KB)
        gk = place("gk", [P, L], F32, 16 * KB)
        gb = place("gb", [P, L], F32, 20 * KB)
        ge = place("ge", [P, L], F32, 24 * KB)
        bq = place("bq", [P, L], F32, 28 * KB)
        bk = place("bk", [P, L], F32, A0)
        vtok_b = place("vtok_b", [P, KT, P], F32, A0 + 4 * KB)
        prob = place("prob", [P, 2, L], F32, A0 + 8 * KB)
        probT = place("probT", [P, KT, P], F32, A0 + 16 * KB)
        cosr = place("cosr", [P, L], F32, A0 + 20 * KB)
        sinr = place("sinr", [P, L], F32, A0 + 24 * KB)
        logc = place("logc", [P, L], F32, A0 + 28 * KB)
        first = place("first", [P, L], F32, A0 + 32 * KB)
        states = place("states", [P, 8, P], F32, A0 + 36 * KB)
        M0 = A0 + 40 * KB
        ktok = place("ktok", [P, P], F32, M0)
        vtok = place("vtok", [P, 2, P], F32, M0 + 512)
        X0 = M0 + 1536
        causal = place("causal", [P, P], F32, X0)
        scm = place("scm", [P, 2, P], F32, X0 + 512)
        blk = place("blk", [P, 4], F32, X0 + 1536)
        dec = place("dec", [P, NCH], F32, X0 + 1536 + 32)
        hp = place("hp", [P, HEADS, 3], F32, X0 + 1536 + 160)
        cur = place("cur", [P, 3], F32, X0 + 1536 + 224)
        stat = place("stat", [P, 2, 4], F32, X0 + 1536 + 256)
        vblk = acc[:, 0:512].rearrange("p (c v) -> p c v", c=4)

        hid_hi = place("hid_hi", [P, 4, L], F32R, A0)
        hid_lo = place("hid_lo", [P, 4, L], F32R, A0 + 16 * KB)
        gate = place("gate", [P, L], F32, A0 + 32 * KB)
        f_act = place("act", [P, L], F32, A0 + 36 * KB)

        m_hi = place("m_hi", [P, KT, MEM], F32R, A0)
        m_lo = place("m_lo", [P, KT, MEM], F32R, A0 + 8 * KB)
        xq = place("xq", [P, 2, L], F32, A0 + 16 * KB)
        xk = place("xk", [P, 2, MEM], F32, A0 + 24 * KB)
        xv = place("xv", [P, 2, MEM], F32, A0 + 26 * KB)
        xvt = place("xvt", [P, 2, MEM], F32, A0 + 28 * KB)
        xp = place("xp", [P, 2, 2, MEM], F32, A0 + 36 * KB + 64)
        xpT = [place(f"xpT{i}", [P, 2, HALF], F32, A0 + (32, 40)[i] * KB + 64 * i) for i in range(2)]
        xstat = place("xstat", [P, 2, 4, 2], F32, A0 + 36 * KB)
        m_raw = place("m_raw", [P, KT, MEM], F32, A0 + 36 * KB + 64)
        m_sq = place("m_sq", [P, KT, MEM], F32, 96 * KB)

        sg = place("sg", [P, L], F32, A0 + 8 * KB)
        sgn = place("sgn", [P, 2], F32, 161 * KB + 672)
        o_src = [place(f"o_src{i}", [P, GR, GC], F32, 4 * i * KB) for i in range(2)]
        o_dst = [place(f"o_dst{i}", [P, GR, GC], F32, (8 + 4 * i) * KB) for i in range(2)]
        o_tmp = place("o_tmp", [P, GR, GC], F32, 16 * KB)
        pw = place("pw", [P, 2, GR], F32, 20 * KB)
        pc = place("pc", [P, 4, GR], F32, 20 * KB + 8704)
        pt = place("pt", [P, 4, GR], F32, 20 * KB + 8704 + 1024)
        sp_in = place("sp_in", [P, 3, GR], F32, A0)
        sv = place("sv", [P, 16, GR], F32, A0 + 1024)

        ub = place("ub", [P, 2, GR, NB], F32, 32 * KB)
        hs = place("hs", [P, 2, GR, NB], F32, 64 * KB)
        yT = place("yT", [P, KT, L], F32, 64 * KB)
        wt = [place(f"wt{i}", [P, SB, P], F32, A0 + 32 * i * KB) for i in range(2)]
        m1 = place("m1", [P, 2, 2, 8, P], F32, A0 + 8 * KB)
        wr = place("wr", [P, 8, SB, GC], F32, A0 + 24 * KB)
        dr = [place(f"dr{i}", [P, 8, SB, GC], F32, A0 + (18 + 8 * i) * KB) for i in range(2)]
        dt_ = [place(f"dt{i}", [P, SB + 1, P], F32, A0 + 8704 * i) for i in range(2)]
        w15 = [place(f"w15_{i}", [P, P], F32, A0 + 17408 + 512 * i) for i in range(2)]
        kpad = place("kpad", [16, 8, 23 * GC], F32, A0 + 18432)
        tz = place("tz", [P, 8, 2 * P], F32, A0 + 30208)
        ar_b = place("ar_b", [P, GR], F32, A0 + 41 * KB)
        sai_b = place("sai_b", [P, 2, GR], F32, A0 + 41 * KB + 256)
        sc1 = place("sc1", [P, 2, GR], F32, A0 + 41 * KB + 768)
        sc2 = place("sc2", [P, 2, GR], F32, A0 + 41 * KB + 1280)

        bank = [ctx.enter_context(nc.psum_tensor(f"bank{i}", [P, 1024], F32)) for i in range(4)]
        lin = bank[0:2]
        wide = bank[2:4]

        names = ("par_in x_in con_in mem_in out_done w_load0 w_load1 w_hi_done w_ready w_used lin_free out_full "
                 "out_free setup lb_max lb_exp sq_done sq_free stat_full sqrt_done diag_done spread_full tmp_done rstd_m_done rstd_done x_done hi_done "
                 "h_ready v_step g_step f_exp f_sig f_kept f_log b_scan b_exp q_dec b_neg y_zero "
                 "k_inv b_left b_left_exp k_end g_exp a1_full a1_out ctr_full st_done ao_full "
                 "ao_out s_full s_max p_exp p_sum p_ready t_full t_out bo_full bo_out vt_full vt_out o_sq o_stat "
                 "o_root o_done rope_done s5_in s5_exp s5_mag s5_abs s5_trig s5_made s5_kept  x_sent ops_in ops_out0 ops_out1 x_back u_done u_out u_in wt_in0 wt_in1 wr_done dr_done m1_full m1a_out m1b_out x_full x_out pw_in d_in0 d_in1 k_full k_out t_in yt_full yt_out scan_done y2_full y2_out y_sent yT_in g_in g_done sg_done glu_done m_hi_done m_ready silu_done hid_done hid_hi_done hid_ready")
        sems = {n: ctx.enter_context(nc.semaphore(n)) for n in names.split()}
        s = type("Sems", (), sems)
        block = ctx.enter_context(nc.Block())

        def nw(layer, which, k):
            c = NW + (layer * 6 + which) * KT + k
            return par[:, c:c + 1]

        con = t["con"]
        xv_d = t["xT"].rearrange("(k p) t -> p k t", p=P)
        mem_d = t["memT"].rearrange("(k p) t -> p k t", p=P)
        out_d = t["out"].rearrange("(k p) t -> p k t", p=P)

        def w_view(name, layer=0):
            return t[name][layer].rearrange("(k p) n -> p k n", p=P)

        def col8(ap, parity):
            return ap[:, parity].rearrange("p (k n) -> p k n", k=KT)

        def col2(ap, parity):
            return ap[:, parity].rearrange("p (k n) -> p k n", k=2)

        @block.sync
        def _(sp):
            w = Counts(sp, sems)
            sp.dma_start(x[:], xv_d).then_inc(s.x_in, 16)
            sp.dma_start(par[:], t["par"]).then_inc(s.par_in, 16)
            sp.dma_start(ident[:], con[:, C_ID:C_ID + P]).then_inc(s.par_in, 16)
            sp.dma_start(m_raw[:], mem_d).then_inc(s.mem_in, 16)
            sp.dma_start(sp_in[:].rearrange("p a g -> p (a g)"), t["s5_small"]).then_inc(s.s5_in, 16)
            sp.dma_start(sgn[:], con[:, C_SIGN:C_SIGN + 2]).then_inc(s.s5_in, 16)

            def load(parity, dst, src):
                sp.wait_ge(s.w_ready, w.at("w_ready"))
                sp.dma_start(dst, src).then_inc((s.w_load0, s.w_load1)[parity], 16)

            def columns(parity, src, n0):
                load(parity, col8(w_raw, parity), src[:, :, ds(n0, P)])

            win = w_view("ab_w_in")
            sp.wait_ge(s.rstd_done, w.at("rstd_done"))
            sp.wait_ge(s.s5_made, w.at("s5_made"))
            sp.dma_start(t["pc_d"], sv[:, 8:12]).then_inc(s.s5_kept, 16)
            sp.wait_ge(s.s5_kept, 16)
            sp.dma_start(cosr[:], con[:, C_COS:C_COS + L]).then_inc(s.con_in, 16)
            sp.dma_start(sinr[:], con[:, C_SIN:C_SIN + L]).then_inc(s.con_in, 16)
            sp.dma_start(logc[:], con[:, C_LOGC:C_LOGC + L]).then_inc(s.con_in, 16)
            sp.dma_start(first[:], con[:, C_FIRST:C_FIRST + L]).then_inc(s.con_in, 16)
            sp.dma_start(causal[:], con[:, C_CAUSAL:C_CAUSAL + P]).then_inc(s.con_in, 16)
            sp.dma_start(blk[:], con[:, C_BLK:C_BLK + 4]).then_inc(s.con_in, 16)
            with w.repeat(HEADS, w_ready=8) as h:
                for j in range(7):
                    columns(j % 2, win, h * P + j * AW)
                w.skip("w_ready")
            wout = w_view("ab_w_out")
            with w.repeat(KT // 2, w_ready=2) as i:
                for j in range(2):
                    columns(j, wout, i * (2 * P) + j * P)
            for layer in range(LAYERS):
                wq, wkv, wo = w_view("xattn_wq", layer), w_view("xattn_wkv", layer), w_view("xattn_wo", layer)
                with w.repeat(HEADS, w_ready=6) as h:
                    for j in range(2):
                        columns(j, wq, h * MEM + j * P)
                    for j in range(2):
                        columns(j, wkv, h * MEM + j * P)
                    for j in range(2):
                        columns(j, wkv, h * MEM + (D + j * P))
                with w.repeat(KT // 2, w_ready=2) as i:
                    for j in range(2):
                        columns(j, wo, i * (2 * P) + j * P)
                wi, wd = w_view("ffn_w_in", layer), t["ffn_w_out"][layer]

                def up(c):
                    for j in range(2):
                        columns(0, wi, c * (2 * P) + j * P)
                        columns(1, wi, c * (2 * P) + (DFF + j * P))

                def down(c):
                    for j in range(2):
                        load(j, col2(w_raw, j),
                             wd[ds(c * (2 * P), 2 * P), j * HALF:(j + 1) * HALF].rearrange("(k p) n -> p k n", p=P))

                up(0)
                with w.repeat(FC // 2, w_ready=12) as i:
                    up(i * 2 + 1)
                    down(i * 2)
                    up(i * 2 + 2)
                    down(i * 2 + 1)
                down(FC - 1)
                if layer == 1 or LAYERS == 1:
                    continue
                wg = w_view("s5_w_glu")
                for j in range(2):
                    columns(j, wg, j * D)
                ud = t["u_d"].rearrange("(k p) t -> k p t", p=P)
                for k in range(KT):
                    sp.wait_ge(s.u_done, w.at("u_done"))
                    sp.dma_start(ud[k], y[:, k]).then_inc(s.u_out, 16)
                sp.wait_ge(s.u_out, w.at("u_out", 16 * KT))

                def by_channel(name, n):
                    return t[name].rearrange("(g c) (s j) -> s c g j", c=GC, s=SB)[n]

                def wt_load(k, b):
                    sp.dma_start(wt[b][:], t["w_d"].rearrange("n p c -> p n c")[:, :, ds(k * P, P)]).then_inc(
                        (s.wt_in0, s.wt_in1)[b], 16)

                wt_load(0, 0)
                wt_load(1, 1)
                for n in range(SB):
                    p0 = (n % 8) * GC
                    sp.dma_start(ub[p0:p0 + GC, n // 8], by_channel("u_d", n)).then_inc(s.u_in, 16)
                with w.repeat(KT // 2 - 1, wr_done=2) as i:
                    for b in range(2):
                        sp.wait_ge(s.wr_done, w.at("wr_done"))
                        wt_load(i * 2 + (2 + b), b)
                sp.wait_ge(s.x_out, w.at("x_taken", KT))
                sp.dma_start(ar_b[:], t["pw_d"][:, 0]).then_inc(s.pw_in, 16)
                sp.dma_start(sai_b[:, 1], t["pw_d"][:, 1]).then_inc(s.pw_in, 16)

                def d_load(k, b, with_w15):
                    sp.dma_start(dt_[b][:], t["dd_d"].rearrange("n p c -> p n c")[:, :, ds(k * P, P)]).then_inc((s.d_in0, s.d_in1)[b], 16)
                    if with_w15:
                        sp.dma_start(w15[b][:], t["w_d"][SB - 1][:, ds(k * P, P)]).then_inc((s.d_in0, s.d_in1)[b], 16)

                def t_load():
                    sp.wait_ge(s.k_out, w.at("k_out"))
                    for n in range(8):
                        c = (7 - n) * GC
                        sp.dma_start(tz[n * GC:(n + 1) * GC], kpad[:, :, c:c + 2 * P]).then_inc(s.t_in, 16)

                d_load(0, 0, True)
                d_load(1, 1, True)
                t_load()
                with w.repeat(KT // 2 - 1, k_out=2, yt_full=2) as i:
                    d_load(i * 2 + 2, 0, True)
                    sp.wait_ge(s.yt_full, w.at("yt_full"))
                    t_load()
                    d_load(i * 2 + 3, 1, True)
                    sp.wait_ge(s.yt_full, w.at("yt_full"))
                    t_load()
                sp.wait_ge(s.yt_full, w.at("yt_full"))
                t_load()
                sp.wait_ge(s.yt_full, w.at("yt_full"))
                d_load(0, 0, False)
                d_load(1, 1, False)
                with w.repeat(KT // 2 - 1, dr_done=2) as i:
                    for b in range(2):
                        sp.wait_ge(s.dr_done, w.at("dr_done"))
                        d_load(i * 2 + 2 + b, b, False)
                sp.wait_ge(s.y2_out, w.at("y2_added", KT))
                for n in range(SB):
                    p0 = (n % 8) * GC
                    sp.dma_start(by_channel("y_d", n), ub[p0:p0 + GC, n // 8]).then_inc(s.y_sent, 16)
                sp.wait_ge(s.y_sent, w.at("y_sent", 16 * SB))
                sp.dma_start(yT[:], t["y_d"].rearrange("(k p) t -> p k t", p=P)).then_inc(s.yT_in, 16)
                with w.repeat(KT - 1, w_ready=2) as i:
                    for j in range(2):
                        columns(j, wg, i * P + (P + j * D))
            sp.wait_ge(s.x_done, w.at("x_done", KT * (2 * LAYERS + LAYERS)))
            sp.dma_start(out_d, x[:]).then_inc(s.out_done, 16)
            sp.wait_ge(s.out_done, 16)

        @block.scalar
        def _(act):
            w = Counts(act, sems)
            A = nc.scalar.activation

            def split(parity):
                act.wait_ge((s.w_load0, s.w_load1)[parity], w.at(f"w_load{parity}", 16))
                act.wait_ge(s.w_used, w.at("w_used"))
                A(w_hi[:, parity], w_raw[:, parity], ACT.Copy).then_inc(s.w_hi_done, 1)

            def factor(pre):
                if pre:
                    act.wait_ge(s.sq_free, w.at("acc_sum", KT))
                else:
                    act.wait_ge(s.stat_full, w.at("stat_full"))
                    w.skip("acc_sum", KT)
                A(root8[:], wide[1][:, 0:KT], ACT.Sqrt, bias=eps[:, 0:1], scale=1.0 / D).then_inc(s.sqrt_done, 1)
                for lo_, hi_ in ((0, HALF), (HALF, L)):
                    act.wait_ge(s.spread_full, w.at("spread_full"))
                    ins = A(rstd[:, lo_:hi_], wide[0][:, lo_:hi_], ACT.Copy)
                ins.then_inc(s.rstd_done, 1)

            def prenorm(layer, which, k):
                A(h_hi[:, k], x[:, k], ACT.Copy, scale=nw(layer, which, k)).then_inc(s.hi_done, 1)
                act.wait_ge(s.sq_free, w.at("sq_free"))
                A(sq[:, k % 2], x[:, k], ACT.Square).then_inc(s.sq_done, 1)

            def boundary(layer, which, s5=False):
                factor(False)
                for k in range(KT):
                    act.wait_ge(s.x_done, w.at("x_done"))
                    if which is not None:
                        prenorm(layer, which, k)
                    if s5:
                        act.wait_ge(s.sq_free, w.at("sq_free"))
                        A(sq[:, k % 2], x[:, k], ACT.Square).then_inc(s.sq_done, 1)
                if which is not None or s5:
                    factor(True)

            def split_y():
                for k in range(KT):
                    A(h_hi[:, k], y[:, k], ACT.Copy).then_inc(s.hi_done, 1)

            def out_projection():
                with w.repeat(KT // 2, product=2, w_used=2, w_load0=16, w_load1=16, sq_free=2) as i:
                    for j in range(2):
                        act.wait_ge(s.w_used, w.at("product"))
                        act.wait_ge(s.sq_free, w.at("sq_free"))
                        A(sq[:, j], lin[j][:], ACT.Square).then_inc(s.sq_done, 1)
                        A(y[:, ds(i * 2 + j, 1)].rearrange("p k t -> p (k t)"), lin[j][:],
                          ACT.Copy).then_inc(s.lin_free, 1)
                        split(j)
                w.skip("lin_out", KT)

            act.wait_ge(s.setup, w.at("setup"))
            act.wait_ge(s.par_in, w.at("par_in", 32))
            act.wait_ge(s.mem_in, w.at("mem_in", 16))
            A(m_sq[:], m_raw[:], ACT.Square).then_inc(s.sq_done, 1)
            act.wait_ge(s.sq_done, w.at("sq_done"))
            act.wait_ge(s.x_in, w.at("x_in", 16))
            for k in range(KT):
                prenorm(0, 0, k)
            act.wait_ge(s.stat_full, w.at("stat_full"))
            A(rstd_m[:], lin[1][:, 0:MEM], ACT.Sqrt, bias=eps[:, 0:1], scale=1.0 / D).then_inc(s.sqrt_done, 1)
            factor(True)
            act.wait_ge(s.lb_max, w.at("lb_max"))
            A(lbt[:, 4:16], lbt[:, 4:16], ACT.Exp).then_inc(s.lb_exp, 1)

            act.wait_ge(s.s5_in, w.at("s5_in", 32))
            A(sv[:, 0], sp_in[:, 2], ACT.Exp).then_inc(s.s5_exp, 1)
            act.wait_ge(s.s5_mag, w.at("s5_mag"))
            A(sv[:, 3], sv[:, 1], ACT.Exp).then_inc(s.s5_abs, 1)
            A(sv[:, 4], sv[:, 2], ACT.Abs).then_inc(s.s5_abs, 1)
            act.wait_ge(s.s5_abs, w.at("s5_abs", 2))
            A(sv[:, 5], sv[:, 2], ACT.Sin).then_inc(s.s5_trig, 1)
            A(sv[:, 6], sv[:, 4], ACT.Sin, scale=-1.0, bias=eps[:, 1:2]).then_inc(s.s5_trig, 1)
            split(0)
            split(1)
            with w.repeat(HEADS, product=8, w_used=8, w_load0=64, w_load1=48, lin_out=7, f_sig=1, f_kept=1, b_scan=1,
                          q_dec=1, b_left=1, vt_full=1, s_max=8, t_full=8, ao_full=8, bo_full=8,
                          ao_out=8, o_stat=1) as h:
                act.wait_ge(s.w_used, w.at("product"))
                split(0)
                act.wait_ge(s.w_used, w.at("product"))
                split(1)
                act.wait_ge(s.lin_free, w.at("lin_out", 2))
                A(zf[:], zf[:], ACT.Exp, scale=-1.0).then_inc(s.f_exp, 1)
                act.wait_ge(s.w_used, w.at("product"))
                split(0)
                act.wait_ge(s.f_sig, w.at("f_sig"))
                A(ge[:], zf[:], ACT.Ln).then_inc(s.f_log, 1)
                A(gk[:], zf[:], ACT.Copy, scale=-1.0, bias=1.0).then_inc(s.f_kept, 1)
                act.wait_ge(s.b_scan, w.at("b_scan"))
                A(ge[:], gb[:], ACT.Exp).then_inc(s.b_exp, 1)
                act.wait_ge(s.f_kept, w.at("f_kept"))
                A(zf[:], gb[:], ACT.Exp, scale=-1.0).then_inc(s.b_neg, 1)
                act.wait_ge(s.w_used, w.at("product"))
                split(1)
                act.wait_ge(s.q_dec, w.at("q_dec"))
                act.wait_ge(s.b_left, w.at("b_left"))
                A(ge[:], ge[:], ACT.Exp).then_inc(s.b_left_exp, 1)
                act.wait_ge(s.lin_free, w.at("lin_out", 2))
                A(gb[:], zg[:], ACT.Exp, scale=-1.0).then_inc(s.g_exp, 1)
                act.wait_ge(s.w_used, w.at("product"))
                split(0)
                w.skip("lin_out", 3)
                w.skip("w_used")
                act.wait_ge(s.w_used, w.at("product", 3))
                split(0)
                split(1)

                def a_out(T):
                    act.wait_ge(s.ao_full, w.at("ao_full"))
                    A(zi[:, T * P:(T + 1) * P], lin[1][:, 0:P], ACT.Copy).then_inc(s.ao_out, 1)

                def b_out(T):
                    act.wait_ge(s.bo_full, w.at("bo_full"))
                    A(y[:, ds(h + HEADS, 1), T * P:(T + 1) * P].rearrange("p k t -> p (k t)"),
                      lin[1][:, HALF:HALF + P], ACT.Copy).then_inc(s.bo_out, 1)

                act.wait_ge(s.vt_full, w.at("vt_full"))
                A(vtok_b[:].rearrange("p k d -> p (k d)"), wide[1][:], ACT.Copy).then_inc(s.vt_out, 1)
                for T in range(KT):
                    W = (T + 1) * P
                    act.wait_ge(s.s_max, w.at("s_max"))
                    A(prob[:, T % 2, 0:W], prob[:, T % 2, 0:W], ACT.Exp, bias=stat[:, T % 2, 1:2], scale=B_SCALE,
                      accum_out=stat[:, T % 2, 2:3]).then_inc(s.p_exp, 1)
                    if T:
                        a_out(T - 1)
                        b_out(T - 1)
                    act.wait_ge(s.t_full, w.at("t_full"))
                    A(probT[:, 0:T + 1].rearrange("p k q -> p (k q)"), wide[1][:, 0:W], ACT.Copy).then_inc(s.t_out, 1)
                a_out(KT - 1)
                b_out(KT - 1)
                act.wait_ge(s.ao_out, w.at("ao_out", 8))
                A(ge[:], zi[:], ACT.Square).then_inc(s.o_sq, 1)
                act.wait_ge(s.o_stat, w.at("o_stat"))
                A(gb[:], wide[0][:], ACT.Sqrt, bias=eps[:, 0:1], scale=1.0 / P).then_inc(s.o_root, 1)
            act.wait_ge(s.o_done, w.at("o_done", HEADS))
            act.dma_start(x[:], xv_d).then_inc(s.x_in, 16)
            act.wait_ge(s.bo_out, w.at("bo_out", KT * HEADS))
            split_y()
            out_projection()
            boundary(0, 2)

            for layer in range(LAYERS):
                act.dma_start(m_raw[:], mem_d).then_inc(s.mem_in, 16)
                act.wait_ge(s.mem_in, w.at("mem_in", 16))
                for k in range(KT):
                    c = MNW + layer * KT + k
                    A(m_hi[:, k], m_raw[:, k], ACT.Copy, scale=par[:, c:c + 1]).then_inc(s.m_hi_done, 1)
                with w.repeat(HEADS, product=6, w_used=6, w_load0=48, w_load1=48, vt_full=1, s_max=4, t_full=4,
                              bo_full=4) as h:
                    for j in range(6):
                        act.wait_ge(s.w_used, w.at("product"))
                        split(j % 2)
                    act.wait_ge(s.vt_full, w.at("vt_full"))
                    A(xvt[:].rearrange("p k d -> p (k d)"), wide[0][:, 0:HALF], ACT.Copy).then_inc(s.vt_out, 1)

                    def softmax(p):
                        act.wait_ge(s.s_max, w.at("s_max"))
                        for i in range(2):
                            c = (p % 2) * HALF + i * MEM
                            ins = A(xp[:, p % 2, i], wide[0][:, c:c + MEM], ACT.Exp, bias=xstat[:, p % 2, 1, i:i + 1],
                                    scale=X_SCALE, accum_out=xstat[:, p % 2, 2, i:i + 1])
                        ins.then_inc(s.p_exp, 1)

                    def transposed(p):
                        act.wait_ge(s.t_full, w.at("t_full"))
                        A(xpT[p // 2][:, :, (p % 2) * MEM:(p % 2 + 1) * MEM],
                          wide[1][:, (p % 2) * HALF:(p % 2 + 1) * HALF].rearrange("p (k q) -> p k q", k=2),
                          ACT.Copy).then_inc(s.t_out, 1)

                    def output(half):
                        for j in range(2):
                            act.wait_ge(s.bo_full, w.at("bo_full"))
                            A(y[:, ds(h * 2 + j, 1), half * HALF:(half + 1) * HALF].rearrange("p k t -> p (k t)"),
                              lin[half][:, j * HALF:(j + 1) * HALF], ACT.Copy).then_inc(s.bo_out, 1)

                    softmax(0)
                    softmax(1)
                    for p in range(2):
                        transposed(p)
                        softmax(p + 2)
                    output(0)
                    transposed(2)
                    transposed(3)
                    output(1)
                w.skip("lin_out", 6 * HEADS)
                act.wait_ge(s.bo_out, w.at("bo_out", 4 * HEADS))
                split_y()
                out_projection()
                boundary(layer, 4)

                def up(c):
                    for j in range(2):
                        act.wait_ge(s.w_used, w.at("product"))
                        split(0)
                        act.wait_ge(s.lin_free, w.at("lin_out"))
                        A(f_act[:], gate[:], ACT.Silu).then_inc(s.silu_done, 1)
                        act.wait_ge(s.w_used, w.at("product"))
                        w.skip("lin_out")
                        split(1)
                        act.wait_ge(s.hid_done, w.at("hid_done"))
                        A(hid_hi[:, 2 * (c % 2) + j], f_act[:], ACT.Copy).then_inc(s.hid_hi_done, 1)

                def down(c, last):
                    for j in range(2):
                        act.wait_ge(s.w_used, w.at("product"))
                        if not last:
                            split(j)
                        if c == FC - 1:
                            for n in range(4 * j, 4 * j + 4):
                                act.wait_ge(s.out_free, w.at("sum_out"))
                                act.wait_ge(s.sq_free, w.at("sq_free"))
                                A(sq[:, n % 2], y[:, n], ACT.Square).then_inc(s.sq_done, 1)
                        else:
                            w.skip("sum_out", 4)

                up(0)
                with w.repeat(FC // 2, product=12, w_used=12, w_load0=96, w_load1=96, lin_out=8, hid_done=4,
                              sum_out=16):
                    up(1)
                    down(0, False)
                    up(0)
                    down(1, False)
                down(FC - 1, layer == LAYERS - 1)
                if layer == LAYERS - 1:
                    boundary(None, None)
                    continue
                boundary(None, None, s5=True)

                with w.repeat(KT, m1_full=2):
                    act.wait_ge(s.m1_full, w.at("m1_full"))
                    src = lin[0][:].rearrange("p (g c) -> p g c", g=8)
                    A(m1[:, 0, 0], src, ACT.Copy)
                    A(m1[:, 1, 0].rearrange("p g (h c) -> p g h c", h=2),
                      src.rearrange("p g (h c) -> p g h c", h=2)[:, :, ::-1], ACT.Copy).then_inc(s.m1a_out, 1)
                    w.skip("m1_full")
                act.wait_ge(s.x_out, w.at("x_taken", KT))
                A(kpad[:, :, 0:7 * GC], ident[0:16, 0:112].unsqueeze(1).to_broadcast([16, 8, 112]), ACT.Copy,
                  scale=0.0)

                def kernels(wait):
                    act.wait_ge(s.k_full, w.at("k_full"))
                    if wait:
                        act.wait_ge(s.t_in, w.at("t_in", 128))
                    for b in range(2):
                        ins = A(kpad[:, 4 * b:4 * b + 4, 7 * GC:23 * GC],
                                lin[b][0:16, :].rearrange("p (g c) -> p g c", g=4), ACT.Copy)
                    ins.then_inc(s.k_out, 1)

                def toeplitz(b, k):
                    act.wait_ge(s.yt_full, w.at("yt_full"))
                    A(ub[:, :, ds(k * 8, 8)].rearrange("p t g j -> p t (g j)"),
                      wide[b][:].rearrange("p (t c) -> p t c", t=2), ACT.Copy).then_inc(s.yt_out, 1)

                kernels(False)
                with w.repeat(KT // 2 - 1, k_full=2, t_in=256, yt_full=2) as i:
                    for b in range(2):
                        kernels(True)
                        toeplitz(b, i * 2 + b)
                kernels(True)
                toeplitz(0, KT - 2)
                toeplitz(1, KT - 1)
                for k in range(KT):
                    act.wait_ge(s.g_in, w.at("g_in"))
                    A(y[:, k], yT[:, k], ACT.Gelu).then_inc(s.g_done, 1)
                    act.wait_ge(s.g_done, w.at("g_done"))
                    A(h_hi[:, k], y[:, k], ACT.Copy).then_inc(s.hi_done, 1)

                with w.repeat(KT // 2, product=4, w_used=4, w_load0=32, w_load1=32, glu_done=2, sq_free=2) as i:
                    for b in range(2):
                        act.wait_ge(s.w_used, w.at("product"))
                        split(0)
                        act.wait_ge(s.w_used, w.at("product"))
                        A(sg[:], lin[1][:], ACT.Sigmoid).then_inc(s.sg_done, 1)
                        split(1)
                        act.wait_ge(s.glu_done, w.at("glu_done"))
                        act.wait_ge(s.sq_free, w.at("sq_free"))
                        A(sq[:, b], y[:, ds(i * 2 + b, 1)].rearrange("p k t -> p (k t)"),
                          ACT.Square).then_inc(s.sq_done, 1)
                w.skip("lin_out", 2 * KT)
                boundary(1, 2)

        @block.vector
        def _(dve):
            w = Counts(dve, sems)
            V = nc.vector

            def step(ins):
                ins.then_inc(s.v_step, 1)
                dve.wait_ge(s.v_step, w.at("v_step"))

            def split(parity):
                dve.wait_ge(s.w_hi_done, w.at("w_hi_done"))
                V.tensor_tensor(w_lo[:, parity], w_raw[:, parity], w_hi[:, parity].bitcast(F32),
                                ALU.subtract).then_inc(s.w_ready, 1)

            def factor():
                dve.wait_ge(s.sqrt_done, w.at("sqrt_done"))
                step(V.reciprocal(root8[:], root8[:]))
                for a in (0, 4):
                    V.tensor_tensor(acc[:, a * P:(a + 4) * P].rearrange("p (t n) -> p t n", n=P),
                                    ident[:].unsqueeze(1).to_broadcast([P, 4, P]),
                                    root8[:, a:a + 4].unsqueeze(2).to_broadcast([P, 4, P]), ALU.mult).then_inc(s.diag_done, 1)

            def low(src, k, scale=None):
                dve.wait_ge(s.hi_done, w.at("hi_done"))
                if scale is None:
                    V.tensor_tensor(h_lo[:, k], src[:, k], h_hi[:, k].bitcast(F32), ALU.subtract).then_inc(s.h_ready, 1)
                else:
                    V.scalar_tensor_tensor(h_lo[:, k], src[:, k], scale, h_hi[:, k].bitcast(F32), ALU.mult,
                                           ALU.subtract).then_inc(s.h_ready, 1)

            def natural(ap):
                return ap.rearrange("p (s j) -> p j s", s=SB)

            def boundary(layer, post, nlayer, pre, blocked=False):
                factor()
                w.skip("rstd_done")
                for k in range(KT):
                    dve.wait_ge(s.tmp_done, w.at("tmp_done"))
                    xk_, tk = x[:, k], tmp[:, k % 2]
                    if blocked:
                        xk_, tk = xk_.rearrange("p (j s) -> p j s", s=SB), natural(tk)
                    V.scalar_tensor_tensor(xk_, tk, nw(layer, post, k), xk_, ALU.mult,
                                           ALU.add).then_inc(s.x_done, 1)
                    if pre is not None and k:
                        low(x, k - 1, nw(nlayer, pre, k - 1))
                w.skip("x_done", KT)
                if pre is not None:
                    low(x, KT - 1, nw(nlayer, pre, KT - 1))
                    factor()
                    dve.wait_ge(s.rstd_done, w.at("rstd_done"))

            def split_y():
                for k in range(KT):
                    low(y, k)

            def out_projection():
                with w.repeat(KT // 2, w_hi_done=2):
                    for j in range(2):
                        split(j)
                w.skip("lin_out", KT)
                w.skip("product", KT)

            V.memset(ones[:], 1.0)
            V.memset(eps[:, 1:2], float(np.pi / 2))
            V.memset(eps[:, 0:1], EPS).then_inc(s.setup, 1)
            dve.wait_ge(s.par_in, w.at("par_in", 32))
            lg = par[:, LBL:LBL + 3 * HEADS]
            step(V.tensor_tensor(lbt[:, 0:4], lg[:, 0:4], lg[:, 4:8], ALU.max))
            step(V.tensor_tensor(lbt[:, 0:4], lbt[:, 0:4], lg[:, 8:12], ALU.max))
            V.tensor_tensor(lbt[:, 4:16].rearrange("p (r h) -> p r h", r=3), lg.rearrange("p (r h) -> p r h", r=3),
                            lbt[:, 0:4].unsqueeze(1).to_broadcast([P, 3, 4]), ALU.subtract).then_inc(s.lb_max, 1)
            dve.wait_ge(s.x_in, w.at("x_in", 16))
            for k in range(KT):
                low(x, k, nw(0, 0, k))
            dve.wait_ge(s.sqrt_done, w.at("sqrt_done"))
            V.reciprocal(rstd_m[:], rstd_m[:]).then_inc(s.rstd_m_done, 1)
            dve.wait_ge(s.rstd_m_done, w.at("rstd_m_done"))
            factor()
            dve.wait_ge(s.rstd_done, w.at("rstd_done"))
            dve.wait_ge(s.lb_exp, w.at("lb_exp"))
            step(V.tensor_tensor(lbt[:, 16:20], lbt[:, 4:8], lbt[:, 8:12], ALU.add))
            step(V.tensor_tensor(lbt[:, 16:20], lbt[:, 16:20], lbt[:, 12:16], ALU.add))
            step(V.reciprocal(lbt[:, 20:24], lbt[:, 16:20]))
            step(V.tensor_tensor(hp[:, :, 0], lbt[:, 4:8], lbt[:, 20:24], ALU.mult))
            step(V.tensor_scalar(hp[:, :, 1], hp[:, :, 0], -1.0, 1.0, ALU.mult, ALU.add))
            step(V.tensor_copy(hp[:, :, 2], par[:, ONW:ONW + HEADS]))
            dve.wait_ge(s.s5_in, w.at("s5_in", 32))
            dve.wait_ge(s.s5_exp, w.at("s5_exp"))
            step(V.tensor_scalar(sv[:, 7], sp_in[:, 0], -1e-4, None, ALU.min))
            V.tensor_tensor(sv[:, 1], sv[:, 0], sv[:, 7], ALU.mult)
            step(V.tensor_tensor(sv[:, 2], sv[:, 0], sp_in[:, 1], ALU.mult))
            step(V.tensor_scalar(sv[:, 12], sv[:, 2], 1.0 / TWO_PI, None, ALU.mult))
            step(V.tensor_scalar(sv[:, 12], sv[:, 12], ROUND, None, ALU.add))
            step(V.tensor_scalar(sv[:, 12], sv[:, 12], -ROUND, None, ALU.add))
            for part in TURN:
                step(V.scalar_tensor_tensor(sv[:, 2], sv[:, 12], -part, sv[:, 2], ALU.mult, ALU.add))
            V.tensor_scalar(sv[:, 2], sv[:, 2], PI_IN, -PI_IN, ALU.min, ALU.max).then_inc(s.s5_mag, 1)
            dve.wait_ge(s.s5_trig, w.at("s5_trig", 2))
            step(V.tensor_tensor(sv[:, 8], sv[:, 3], sv[:, 6], ALU.mult))
            step(V.tensor_tensor(sv[:, 13], sv[:, 3], sv[:, 5], ALU.mult))
            step(V.tensor_scalar(sv[:, 9], sv[:, 13], sgn[:, 0:1], None, ALU.mult))
            step(V.tensor_scalar(sv[:, 14], sv[:, 8], -1.0, None, ALU.add))
            step(V.tensor_tensor(sv[:, 0], sv[:, 7], sv[:, 7], ALU.mult))
            step(V.tensor_tensor(sv[:, 1], sp_in[:, 1], sp_in[:, 1], ALU.mult))
            step(V.tensor_tensor(sv[:, 0], sv[:, 0], sv[:, 1], ALU.add))
            step(V.reciprocal(sv[:, 0], sv[:, 0]))
            step(V.tensor_tensor(sv[:, 1], sv[:, 14], sv[:, 7], ALU.mult))
            step(V.tensor_tensor(sv[:, 2], sv[:, 13], sp_in[:, 1], ALU.mult))
            step(V.tensor_tensor(sv[:, 1], sv[:, 1], sv[:, 2], ALU.add))
            step(V.tensor_tensor(sv[:, 10], sv[:, 1], sv[:, 0], ALU.mult))
            step(V.tensor_tensor(sv[:, 1], sv[:, 13], sv[:, 7], ALU.mult))
            step(V.tensor_tensor(sv[:, 2], sv[:, 14], sp_in[:, 1], ALU.mult))
            step(V.tensor_tensor(sv[:, 1], sv[:, 1], sv[:, 2], ALU.subtract))
            step(V.tensor_tensor(sv[:, 1], sv[:, 1], sv[:, 0], ALU.mult))
            V.tensor_scalar(sv[:, 11], sv[:, 1], sgn[:, 0:1], None, ALU.mult).then_inc(s.s5_made, 1)
            dve.wait_ge(s.con_in, w.at("con_in", 96))
            V.tensor_tensor(cosr[:], cosr[:], rstd[:], ALU.mult)
            V.tensor_tensor(sinr[:], sinr[:], rstd[:], ALU.mult)
            step(V.memset(scm[:], 0.0))
            split(0)
            split(1)
            with w.repeat(HEADS, product=8, w_hi_done=7, v_step=9 + 4 * KT, f_exp=1, f_log=1, b_exp=1, g_exp=1, a1_full=8,
                          ctr_full=8, s_full=8, p_exp=8, ao_full=8, o_root=1, st_done=8, rope_done=2, lin_out=7, o_done=1) as h:
                step(V.tensor_copy(cur[:], hp[:, ds(h, 1)].rearrange("p a b -> p (a b)")))
                dve.wait_ge(s.w_used, w.at("product"))
                V.tensor_tensor(zq[:], lin[0][:], rstd[:], ALU.mult).then_inc(s.lin_free, 1)
                split(0)
                dve.wait_ge(s.w_used, w.at("product"))
                V.tensor_tensor(zf[:], lin[1][:], rstd[:], ALU.mult).then_inc(s.lin_free, 1)
                split(1)
                dve.wait_ge(s.f_exp, w.at("f_exp"))
                step(V.tensor_scalar(zf[:], zf[:], 1.0, None, ALU.add))
                step(V.reciprocal(zf[:], zf[:]))
                V.tensor_scalar(zf[:], zf[:], cur[:, 1:2], cur[:, 0:1], ALU.mult, ALU.add).then_inc(s.f_sig, 1)
                dve.wait_ge(s.w_used, w.at("product"))
                V.tensor_tensor(zi[:], lin[0][:], rstd[:], ALU.mult).then_inc(s.lin_free, 1)
                split(0)
                dve.wait_ge(s.f_log, w.at("f_log"))
                V.tensor_tensor_scan(gb[:], first[:], ge[:], 0.0, ALU.mult, ALU.add).then_inc(s.b_scan, 1)
                dve.wait_ge(s.b_exp, w.at("b_exp"))
                V.tensor_copy(dec[:], ge[:].rearrange("p (c t) -> p c t", t=CH)[:, :, CH - 1])
                V.tensor_tensor(zq[:], zq[:], ge[:], ALU.mult).then_inc(s.q_dec, 1)
                dve.wait_ge(s.w_used, w.at("product"))
                V.tensor_tensor(zg[:], lin[1][:], rstd[:], ALU.mult).then_inc(s.lin_free, 1)
                split(1)
                for j, dst in ((0, bq), (1, bk)):
                    dve.wait_ge(s.w_used, w.at("product"))
                    if j:
                        dve.wait_ge(s.g_exp, w.at("g_exp"))
                        step(V.tensor_scalar(gb[:], gb[:], 1.0, None, ALU.add))
                        step(V.reciprocal(gb[:], gb[:]))
                        step(V.tensor_tensor(zg[:], zg[:], gb[:], ALU.mult))
                    V.tensor_tensor(dst[:], lin[j][:], cosr[:], ALU.mult)
                    V.tensor_tensor(prob[0:64, 0], lin[j][64:128, :], sinr[64:128, :], ALU.mult)
                    V.tensor_tensor(prob[64:128, 0], lin[j][0:64, :], sinr[0:64, :], ALU.mult).then_inc(s.lin_free, 1)
                    dve.wait_ge(s.lin_free, w.at("lin_out", (5, 1)[j]))
                    V.tensor_tensor(dst[:], dst[:], prob[:, 0], ALU.add).then_inc(s.rope_done, 1)
                    dve.wait_ge(s.rope_done, w.at("rope_done"))
                    if j == 0:
                        split(0)
                dve.wait_ge(s.w_used, w.at("product"))
                V.tensor_tensor(prob[:, 1], lin[0][:], rstd[:], ALU.mult).then_inc(s.lin_free, 1)
                dve.wait_ge(s.lin_free, w.at("lin_out"))
                w.skip("product")
                dve.sem_inc(s.w_ready, 1)
                split(0)
                split(1)
                step(V.memset(states[:, 0], 0.0))

                for T in range(KT):
                    W = (T + 1) * P
                    dve.wait_ge(s.a1_full, w.at("a1_full"))
                    if T >= 2:
                        dve.wait_ge(s.ao_full, w.at("ao_full"))
                    dve.wait_ge(s.s_full, w.at("s_full"))
                    V.tensor_copy(vtok[:, T % 2], lin[0][:, P:2 * P])
                    V.copy_predicated(scm[:, T % 2], causal[:].bitcast(mybir.dt.uint32), lin[0][:, 0:P])
                    V.tensor_tensor(vblk, lin[0][:, P:2 * P].unsqueeze(1).to_broadcast([P, 4, P]),
                                    blk[:].unsqueeze(2).to_broadcast([P, 4, P]), ALU.mult)
                    V.tensor_copy(ktok[:], lin[0][:, 2 * P:3 * P]).then_inc(s.a1_out, 1)
                    step(V.tensor_tensor_reduce(prob[:, T % 2, 0:W], wide[0][:, 0:W], logc[:, L - W:L], 1.0, -3e38,
                                                ALU.add, ALU.max, stat[:, T % 2, 0:1]))
                    V.tensor_scalar(stat[:, T % 2, 1:2], stat[:, T % 2, 0:1], -B_SCALE, None, ALU.mult).then_inc(s.s_max, 1)
                    dve.wait_ge(s.ctr_full, w.at("ctr_full"))
                    for c in range(4):
                        n = 4 * T + c
                        ins = V.scalar_tensor_tensor(states[:, (n + 1) % 8], states[:, n % 8], dec[:, n:n + 1],
                                                     lin[0][:, HALF + c * P:HALF + (c + 1) * P], ALU.mult, ALU.add)
                        if c < 3:
                            step(ins)
                        else:
                            ins.then_inc(s.st_done, 1)
                            dve.wait_ge(s.st_done, w.at("st_done"))
                    dve.wait_ge(s.p_exp, w.at("p_exp"))
                    V.reciprocal(stat[:, T % 2, 3:4], stat[:, T % 2, 2:3]).then_inc(s.p_sum, 1)
                dve.wait_ge(s.ao_full, w.at("ao_full", 2))
                dve.wait_ge(s.o_root, w.at("o_root"))
                step(V.reciprocal(gb[:], gb[:]))
                step(V.tensor_tensor(gb[:], gb[:], zi[:], ALU.mult))
                V.scalar_tensor_tensor(y[:, ds(h, 1)].rearrange("p k t -> p (k t)"), gb[:], cur[:, 2:3], zg[:],
                                       ALU.mult, ALU.mult).then_inc(s.o_done, 1)
                dve.wait_ge(s.o_done, w.at("o_done"))
            dve.wait_ge(s.bo_out, w.at("bo_out", KT * HEADS))
            split_y()
            out_projection()
            dve.wait_ge(s.x_in, w.at("x_in", 16))
            boundary(0, 1, 0, 2)

            for layer in range(LAYERS):
                for k in range(KT):
                    dve.wait_ge(s.m_hi_done, w.at("m_hi_done"))
                    c = MNW + layer * KT + k
                    V.scalar_tensor_tensor(m_lo[:, k], m_raw[:, k], par[:, c:c + 1], m_hi[:, k].bitcast(F32),
                                           ALU.mult, ALU.subtract).then_inc(s.m_ready, 1)
                with w.repeat(HEADS, product=6, w_hi_done=6, s_full=4, p_exp=4, v_step=4):
                    for j in range(6):
                        dve.wait_ge(s.w_used, w.at("product"))
                        if j < 2:
                            V.tensor_tensor(xq[:, j], lin[j][:], rstd[:], ALU.mult).then_inc(s.lin_free, 1)
                        else:
                            V.tensor_tensor((xk, xv)[j // 4][:, j % 2], lin[j % 2][:, 0:MEM], rstd_m[:],
                                            ALU.mult).then_inc(s.lin_free, 1)
                        split(j % 2)

                    def largest(p):
                        dve.wait_ge(s.s_full, w.at("s_full"))
                        step(V.tensor_reduce(xstat[:, p % 2, 0],
                                             wide[0][:, (p % 2) * HALF:(p % 2 + 1) * HALF].rearrange("p (i m) -> p i m", i=2),
                                             AX, ALU.max))
                        V.tensor_scalar(xstat[:, p % 2, 1], xstat[:, p % 2, 0], -X_SCALE, None,
                                        ALU.mult).then_inc(s.s_max, 1)

                    largest(0)
                    largest(1)
                    for p in range(4):
                        dve.wait_ge(s.p_exp, w.at("p_exp"))
                        V.reciprocal(xstat[:, p % 2, 3], xstat[:, p % 2, 2]).then_inc(s.p_sum, 1)
                        if p < 2:
                            largest(p + 2)
                w.skip("lin_out", 6 * HEADS)
                dve.wait_ge(s.bo_out, w.at("bo_out", 4 * HEADS))
                split_y()
                out_projection()
                boundary(layer, 3, layer, 4)

                def up(c):
                    for j in range(2):
                        dve.wait_ge(s.w_used, w.at("product"))
                        V.tensor_tensor(gate[:], lin[0][:], rstd[:], ALU.mult).then_inc(s.lin_free, 1)
                        w.skip("lin_out")
                        split(0)
                        dve.wait_ge(s.w_used, w.at("product"))
                        dve.wait_ge(s.silu_done, w.at("silu_done"))
                        V.tensor_tensor(gate[:], lin[1][:], rstd[:], ALU.mult).then_inc(s.lin_free, 1)
                        dve.wait_ge(s.lin_free, w.at("lin_out"))
                        V.tensor_tensor(f_act[:], f_act[:], gate[:], ALU.mult).then_inc(s.hid_done, 1)
                        split(1)
                        dve.wait_ge(s.hid_hi_done, w.at("hid_hi_done"))
                        V.tensor_tensor(hid_lo[:, 2 * (c % 2) + j], f_act[:], hid_hi[:, 2 * (c % 2) + j].bitcast(F32),
                                        ALU.subtract).then_inc(s.hid_ready, 1)

                def down(c, last):
                    for j in range(2):
                        for n in range(4 * j, 4 * j + 4):
                            if n % 4 == 3:
                                dve.wait_ge(s.w_used, w.at("product"))
                            else:
                                dve.wait_ge(s.out_full, w.at("out_full"))
                            V.tensor_tensor(y[:, n], y[:, n], wide[n % 2][:], ALU.add).then_inc(s.out_free, 1)
                        if not last:
                            split(j)

                dve.wait_ge(s.y_zero, w.at("y_zero"))
                up(0)
                with w.repeat(FC // 2, product=12, w_hi_done=12, out_full=12, silu_done=4, hid_hi_done=4, lin_out=8):
                    up(1)
                    down(0, False)
                    up(0)
                    down(1, False)
                down(FC - 1, layer == LAYERS - 1)
                if layer == 0:
                    dve.wait_ge(s.x_back, w.at("x_back", 16))
                boundary(layer, 5, None, None)
                if layer == LAYERS - 1:
                    continue
                factor()
                dve.wait_ge(s.rstd_done, w.at("rstd_done"))
                for k in range(KT):
                    V.scalar_tensor_tensor(natural(y[:, k]), x[:, k].rearrange("p (j s) -> p j s", s=SB), nw(1, 0, k),
                                           rstd[:].rearrange("p (j s) -> p j s", s=SB), ALU.mult,
                                           ALU.mult).then_inc(s.u_done, 1)
                with w.repeat(KT // 2, m1_full=4, x_full=2) as i:
                    for b in range(2):
                        dve.wait_ge(s.m1_full, w.at("m1_full", 2))
                        src = lin[1][:].rearrange("p (g c) -> p g c", g=8)
                        V.tensor_copy(m1[:, 0, 1], src)
                        V.tensor_copy(m1[:, 1, 1].rearrange("p g (h c) -> p g h c", h=2),
                                      src.rearrange("p g (h c) -> p g h c", h=2)[:, :, ::-1]).then_inc(s.m1b_out, 1)
                        dve.wait_ge(s.x_full, w.at("x_full"))
                        V.tensor_copy(hs[:, :, ds(i * 16 + 8 * b, 8)].rearrange("p o g j -> p o (g j)"),
                                      wide[b][:].rearrange("p (o c) -> p o c", o=2)).then_inc(s.x_out, 1)
                dve.wait_ge(s.pw_in, w.at("pw_in", 32))
                dve.wait_ge(s.x_out, w.at("x_taken", KT))
                step(V.tensor_scalar(sai_b[:, 0], sai_b[:, 1], -1.0, None, ALU.mult))

                UNROLL = 7
                with w.repeat((NB - 1) // UNROLL, v_step=4 * UNROLL) as i:
                    for n in range(UNROLL):
                        prev = hs[:, :, :, ds(i * UNROLL + n, 1)].rearrange("p o g j -> p o (g j)")
                        here = hs[:, :, :, ds(i * UNROLL + n + 1, 1)].rearrange("p o g j -> p o (g j)")
                        V.tensor_tensor(sc1[:], ar_b[:].unsqueeze(1).to_broadcast([P, 2, GR]), prev,
                                        ALU.mult).then_inc(s.v_step, 1)
                        V.tensor_tensor(sc2[:, ::-1], sai_b[:], prev, ALU.mult).then_inc(s.v_step, 1)
                        dve.wait_ge(s.v_step, w.at("v_step"))
                        V.tensor_tensor(sc1[:], sc1[:], here, ALU.add).then_inc(s.v_step, 1)
                        dve.wait_ge(s.v_step, w.at("v_step", 2))
                        step(V.tensor_tensor(here, sc1[:], sc2[:], ALU.add))
                dve.sem_inc(s.scan_done, 1)
                dve.wait_ge(s.yt_out, w.at("yt_out", KT))
                with w.repeat(KT // 2, y2_full=2) as i:
                    for b in range(2):
                        dve.wait_ge(s.y2_full, w.at("y2_full"))
                        v = ub[:, :, ds(i * 16 + 8 * b, 8), 1:NB]
                        V.tensor_tensor(v, wide[b][:].rearrange("p (t g j) -> p t g j", t=2, g=8)[:, :, :, 1:NB], v,
                                        ALU.add).then_inc(s.y2_out, 1)
                dve.wait_ge(s.yT_in, w.at("yT_in", 16))
                for k in range(KT):
                    V.scalar_tensor_tensor(yT[:, k], y[:, k], par[:, SD + k:SD + k + 1], yT[:, k], ALU.mult,
                                           ALU.add).then_inc(s.g_in, 1)
                    if k:
                        low(y, k - 1)
                low(y, KT - 1)
                with w.repeat(KT // 2, w_hi_done=4, sg_done=2, glu_done=2, product=4) as i:
                    for b in range(2):
                        dve.wait_ge(s.w_used, w.at("product"))
                        split(0)
                        dve.wait_ge(s.w_used, w.at("product"))
                        dve.wait_ge(s.sg_done, w.at("sg_done"))
                        V.tensor_tensor(y[:, ds(i * 2 + b, 1)].rearrange("p k t -> p (k t)"), lin[0][:], sg[:],
                                        ALU.mult).then_inc(s.glu_done, 1)
                        dve.wait_ge(s.glu_done, w.at("glu_done"))
                        dve.sem_inc(s.lin_free, 2)
                        split(1)
                w.skip("lin_out", 2 * KT)
                boundary(1, 1, 1, 2, blocked=True)

        @block.gpsimd
        def _(pool):
            w = Counts(pool, sems)
            G = nc.gpsimd

            def sum_squares():
                for k in range(KT):
                    pool.wait_ge(s.sq_done, w.at("sq_done"))
                    if k == 0:
                        G.tensor_copy(acc[:], sq[:, 0]).then_inc(s.sq_free, 1)
                    else:
                        G.tensor_tensor(acc[:], acc[:], sq[:, k % 2], ALU.add).then_inc(s.sq_free, 1)
                    pool.wait_ge(s.sq_free, w.at("acc_sum"))

            def boundary(pre=True):
                pool.wait_ge(s.rstd_done, w.at("rstd_done"))
                for k in range(KT):
                    if k >= 2:
                        pool.wait_ge(s.x_done, w.at("x_done"))
                    G.tensor_tensor(tmp[:, k % 2], y[:, k], rstd[:], ALU.mult).then_inc(s.tmp_done, 1)
                pool.wait_ge(s.x_done, w.at("x_done", 2))
                if pre:
                    pool.wait_ge(s.rstd_done, w.at("rstd_done"))
                    w.skip("sq_done", KT)
                    w.skip("acc_sum", KT)

            def step(ins):
                ins.then_inc(s.g_step, 1)
                pool.wait_ge(s.g_step, w.at("g_step"))

            def operators():
                pool.wait_ge(s.h_ready, w.at("h_ready", 5 * KT))
                pool.dma_start(t["x_d"].rearrange("(k p) t -> p k t", p=P), x[:]).then_inc(s.x_sent, 16)
                pool.wait_ge(s.x_sent, w.at("x_sent", 16))
                pool.dma_start(pc[:], t["pc_d"]).then_inc(s.ops_in, 16)
                pool.dma_start(o_src[0][:].rearrange("p g c -> p (g c)"), t["s5_b"][0]).then_inc(s.ops_in, 16)
                pool.dma_start(o_src[1][:].rearrange("p g c -> p (g c)"), t["s5_b"][1]).then_inc(s.ops_in, 16)
                pool.wait_ge(s.ops_in, w.at("ops_in", 48))

                def wide_(ap):
                    return ap.unsqueeze(2).to_broadcast([P, GR, GC])

                for own, sign in ((0, ALU.add), (1, ALU.subtract)):
                    step(G.tensor_tensor(o_dst[own][:], o_src[own][:], wide_(pc[:, 2]), ALU.mult))
                    step(G.tensor_tensor(o_tmp[:], o_src[1 - own][:], wide_(pc[:, 3]), ALU.mult))
                    step(G.tensor_tensor(o_dst[own][:], o_dst[own][:], o_tmp[:], sign))

                def first_power():
                    G.memset(pw[:, 0], 1.0)
                    step(G.memset(pw[:, 1], 0.0))

                def one(src, dst, dram, at, b, advance=True):
                    ins = G.tensor_tensor(dst[b][:], src[0][:], wide_(pw[:, 0]), ALU.mult)
                    ins = G.tensor_tensor(o_tmp[:], src[1][:], wide_(pw[:, 1]), ALU.mult)
                    if advance:
                        G.tensor_tensor(pt[:, 0], pw[:, 0], pc[:, 0], ALU.mult)
                        G.tensor_tensor(pt[:, 1], pw[:, 1], pc[:, 1], ALU.mult)
                        G.tensor_tensor(pt[:, 2], pw[:, 0], pc[:, 1], ALU.mult)
                        ins = G.tensor_tensor(pt[:, 3], pw[:, 1], pc[:, 0], ALU.mult)
                    step(ins)
                    step(G.tensor_tensor(dst[b][:], dst[b][:], o_tmp[:], ALU.add))
                    if advance:
                        G.tensor_tensor(pw[:, 0], pt[:, 0], pt[:, 1], ALU.subtract)
                    pool.dma_start(dram[ds(at, 1)].rearrange("a p c -> p (a c)"),
                                   dst[b][:].rearrange("p g c -> p (g c)")).then_inc((s.ops_out0, s.ops_out1)[b], 16)
                    if advance:
                        step(G.tensor_tensor(pw[:, 1], pt[:, 2], pt[:, 3], ALU.add))

                first_power()
                for n in range(2):
                    one(o_dst, o_src, t["w_d"], SB - 1 - n, n)
                with w.repeat(SB // 2 - 1, g_step=6, ops_out0=16, ops_out1=16) as i:
                    for b in range(2):
                        pool.wait_ge((s.ops_out0, s.ops_out1)[b], w.at(f"ops_out{b}", 16))
                        one(o_dst, o_src, t["w_d"], i * -2 + (SB - 3 - b), b)
                pool.wait_ge(s.ops_out0, w.at("ops_out0", 16))
                pool.wait_ge(s.ops_out1, w.at("ops_out1", 16))
                pool.dma_start(o_src[0][:].rearrange("p g c -> p (g c)"), t["s5_c"][0]).then_inc(s.ops_in, 16)
                pool.dma_start(o_src[1][:].rearrange("p g c -> p (g c)"), t["s5_c"][1]).then_inc(s.ops_in, 16)
                pool.wait_ge(s.ops_in, w.at("ops_in", 32))
                for b in range(2):
                    step(G.tensor_tensor(o_src[b][:], o_src[b][:], wide_(sgn[:, 1:2].to_broadcast([P, GR])), ALU.mult))
                first_power()
                for n in range(2):
                    one(o_src, o_dst, t["dd_d"], n, n)
                with w.repeat(SB // 2 - 1, g_step=6, ops_out0=16, ops_out1=16) as i:
                    for b in range(2):
                        pool.wait_ge((s.ops_out0, s.ops_out1)[b], w.at(f"ops_out{b}", 16))
                        one(o_src, o_dst, t["dd_d"], i * 2 + (2 + b), b)
                pool.wait_ge(s.ops_out0, w.at("ops_out0", 16))
                one(o_src, o_dst, t["dd_d"], SB, 0, advance=False)
                pool.dma_start(t["pw_d"], pw[:]).then_inc(s.ops_out1, 16)
                pool.wait_ge(s.ops_out0, w.at("ops_out0", 16))
                pool.wait_ge(s.ops_out1, w.at("ops_out1", 32))
                pool.dma_start(x[:], t["x_d"].rearrange("(k p) t -> p k t", p=P)).then_inc(s.x_back, 16)

            w.skip("sq_done", 1 + KT)
            w.skip("acc_sum", KT)
            w.skip("rstd_done")
            with w.repeat(HEADS, b_neg=1, q_dec=1, b_left_exp=1, p_sum=8):
                pool.wait_ge(s.b_neg, w.at("b_neg"))
                G.tensor_tensor(zf[:], zf[:], gk[:], ALU.mult).then_inc(s.k_inv, 1)
                pool.wait_ge(s.q_dec, w.at("q_dec"))
                b3 = gb[:].rearrange("p (c t) -> p c t", t=CH)
                G.tensor_tensor(ge[:].rearrange("p (c t) -> p c t", t=CH), b3[:, :, CH - 1:CH].to_broadcast([P, NCH, CH]),
                                b3, ALU.subtract).then_inc(s.b_left, 1)
                pool.wait_ge(s.b_left_exp, w.at("b_left_exp"))
                G.tensor_tensor(gk[:], gk[:], ge[:], ALU.mult).then_inc(s.k_end, 1)
                for T in range(KT):
                    W = (T + 1) * P
                    pool.wait_ge(s.p_sum, w.at("p_sum"))
                    G.tensor_tensor(prob[:, T % 2, 0:W], prob[:, T % 2, 0:W],
                                    stat[:, T % 2, 3:4].to_broadcast([P, W]), ALU.mult).then_inc(s.p_ready, 1)
            sum_squares()
            boundary()
            for layer in range(LAYERS):
                with w.repeat(HEADS, p_sum=4):
                    for p in range(4):
                        pool.wait_ge(s.p_sum, w.at("p_sum"))
                        G.tensor_tensor(xp[:, p % 2], xp[:, p % 2], xstat[:, p % 2, 3].unsqueeze(2).to_broadcast([P, 2, MEM]),
                                        ALU.mult).then_inc(s.p_ready, 1)
                sum_squares()
                boundary()
                G.memset(y[:], 0.0).then_inc(s.y_zero, 1)
                if layer == 0:
                    operators()
                sum_squares()
                boundary(pre=layer + 1 < LAYERS)
                if layer + 1 < LAYERS:

                    one4 = ones[:, 0:1].unsqueeze(2).unsqueeze(3).to_broadcast([P, SB, 8, GC])

                    def by_group(dst, src):
                        return G.tensor_tensor(dst[:].rearrange("p g n c -> p n g c"),
                                               src.rearrange("p n (g c) -> p n g c", c=GC),
                                               one4, ALU.mult)

                    with w.repeat(KT // 2, wt_in0=16, wt_in1=16, m1_full=4):
                        for b in range(2):
                            pool.wait_ge((s.wt_in0, s.wt_in1)[b], w.at(f"wt_in{b}", 16))
                            by_group(wr, wt[b][:]).then_inc(s.wr_done, 1)
                            pool.wait_ge(s.m1_full, w.at("m1_full", 2))
                    pool.wait_ge(s.yt_full, w.at("yt_full", KT))
                    pool.wait_ge(s.d_in0, w.at("d_in0", 16 * KT))
                    pool.wait_ge(s.d_in1, w.at("d_in1", 16 * KT))
                    for b in range(2):
                        pool.wait_ge((s.d_in0, s.d_in1)[b], w.at(f"d_in{b}", 16))
                        by_group(dr[b], dt_[b][:, 1:]).then_inc(s.dr_done, 1)
                    with w.repeat(KT // 2 - 1, d_in0=16, d_in1=16, y2_full=2):
                        for b in range(2):
                            pool.wait_ge(s.y2_full, w.at("y2_full"))
                            pool.wait_ge((s.d_in0, s.d_in1)[b], w.at(f"d_in{b}", 16))
                            by_group(dr[b], dt_[b][:, 1:]).then_inc(s.dr_done, 1)
                    sum_squares()
                    boundary()

        @block.tensor
        def _(pe):
            w = Counts(pe, sems)
            MM = nc.tensor.matmul
            for sem in (s.w_used, s.w_ready, s.lin_free, s.out_free, s.sq_free, s.x_out, s.y2_out):
                pe.sem_inc(sem, 2)

            def passes(out, w_h, w_l, a_h, a_l, first, last, spans):
                for n, (a, b) in enumerate(((w_h, a_h), (w_h, a_l), (w_l, a_h))):
                    for lo_, hi_ in spans:
                        ins = MM(out[:, lo_:hi_], a, b[:, lo_:hi_], start=first and n == 0, stop=last and n == 2)
                return ins

            TOK = ((0, HALF), (HALF, L))

            def linear(parity, a_h, a_l, spans=TOK, used=1, ahead=None):
                pe.wait_ge(s.w_ready, w.at("w_split"))
                pe.wait_ge(s.lin_free, w.at("lin_free"))
                for k in range(KT):
                    if ahead:
                        ahead(k)
                    ins = passes(lin[parity], col8(w_hi, parity)[:, k], col8(w_lo, parity)[:, k], a_h[:, k], a_l[:, k],
                                 k == 0, k == KT - 1, spans)
                ins.then_inc(s.w_used, used)

            def token_sums(src, first, last):
                for T in range(KT):
                    ins = MM(wide[1][:, T:T + 1], src[:, T * P:(T + 1) * P], ones[:, 0:1], start=first and T == 0,
                             stop=last and T == KT - 1)
                return ins

            def spread():
                for lo_, hi_ in TOK:
                    pe.wait_ge(s.diag_done, w.at("diag_done"))
                    MM(wide[0][:, lo_:hi_], ones[:], acc[:, lo_:hi_], start=True, stop=True).then_inc(s.spread_full, 1)

            def post_norm():
                pe.wait_ge(s.sq_free, w.at("acc_sum", KT))
                token_sums(acc, True, True).then_inc(s.stat_full, 1)
                w.skip("sq_done", KT)
                spread()

            def pre_sums(k):
                pe.wait_ge(s.sq_done, w.at("sq_done"))
                token_sums(sq[:, k % 2], k == 0, k == KT - 1).then_inc(s.sq_free, 1)
                w.skip("acc_sum")

            def arriving(k):
                pe.wait_ge(s.h_ready, w.at("h_ready"))

            def arriving_normed(k):
                pre_sums(k)
                arriving(k)

            def spread_midway(k):
                if k == KT // 2:
                    spread()

            def first_pair():
                linear(0, h_hi, h_lo, ahead=arriving_normed)
                linear(1, h_hi, h_lo, ahead=spread_midway)

            def out_projection():
                linear(0, h_hi, h_lo, ahead=arriving)
                linear(1, h_hi, h_lo)
                with w.repeat(KT // 2 - 1, w_split=2, lin_free=2):
                    for j in range(2):
                        linear(j, h_hi, h_lo)
                w.skip("lin_out", KT)
                post_norm()

            pe.wait_ge(s.sq_done, w.at("sq_done"))
            for k in range(KT):
                ins = MM(lin[1][:, 0:MEM], ones[:], m_sq[:, k], start=k == 0, stop=k == KT - 1)
            ins.then_inc(s.stat_full, 1)
            pe.wait_ge(s.par_in, w.at("par_in", 32))

            for k in range(KT):
                pre_sums(k)
            spread()
            pe.wait_ge(s.h_ready, w.at("h_ready", KT))
            with w.repeat(HEADS, w_split=8, lin_free=7, lin_out=7, q_dec=1, k_inv=1, k_end=1, rope_done=2, vt_out=1,
                          a1_out=8, s_max=8, st_done=8, ao_out=8, bo_out=8, t_out=8, p_ready=8, o_sq=1, o_root=0):
                for j in range(7):
                    linear(j % 2, h_hi, h_lo, used=2 if j == 6 else 1)
                pe.wait_ge(s.lin_free, w.at("lin_out", 7))
                pe.wait_ge(s.q_dec, w.at("q_dec"))
                pe.wait_ge(s.k_inv, w.at("k_inv"))
                pe.wait_ge(s.k_end, w.at("k_end"))
                pe.wait_ge(s.rope_done, w.at("rope_done", 2))

                def a_tile(T):
                    c = slice(T * P, (T + 1) * P)
                    MM(lin[0][:, 0:P], zf[:, c], zq[:, c], start=True, stop=True)
                    nc.tensor.transpose(lin[0][:, P:2 * P], zi[:, c], ident[:])
                    nc.tensor.transpose(lin[0][:, 2 * P:3 * P], gk[:, c], ident[:]).then_inc(s.a1_full, 1)

                def b_scores(T):
                    if T:
                        pe.wait_ge(s.s_max, w.at("s_max"))
                    W = (T + 1) * P
                    for lo_ in range(0, W, HALF):
                        hi_ = min(W, lo_ + HALF)
                        ins = MM(wide[0][:, lo_:hi_], bq[:, T * P:(T + 1) * P], bk[:, lo_:hi_], start=True, stop=True)
                    ins.then_inc(s.s_full, 1)

                def a_output(T):
                    pe.wait_ge(s.st_done, w.at("st_done"))
                    if T:
                        pe.wait_ge(s.ao_out, w.at("ao_out"))
                    MM(lin[1][:, 0:P], vtok[:, T % 2], scm[:, T % 2], start=True, stop=True)
                    for c in range(4):
                        n = 4 * T + c
                        ins = MM(lin[1][:, c * CH:(c + 1) * CH], states[:, n % 8], zq[:, n * CH:(n + 1) * CH],
                                 start=False, stop=True, skip_group_check=True)
                    ins.then_inc(s.ao_full, 1)

                def b_output(T):
                    pe.wait_ge(s.t_out, w.at("t_out"))
                    if T:
                        pe.wait_ge(s.bo_out, w.at("bo_out"))
                    for k in range(T + 1):
                        ins = MM(lin[1][:, HALF:HALF + P], vtok_b[:, k], probT[:, k], start=k == 0, stop=k == T)
                    ins.then_inc(s.bo_full, 1)

                for T in range(KT):
                    a_tile(T)
                    b_scores(T)
                    if T == 0:
                        for k in range(KT):
                            ins = nc.tensor.transpose(wide[1][:, k * P:(k + 1) * P], prob[:, 1, k * P:(k + 1) * P], ident[:])
                        ins.then_inc(s.vt_full, 1)
                    else:
                        a_output(T - 1)
                        b_output(T - 1)
                    pe.wait_ge(s.a1_out, w.at("a1_out"))
                    MM(lin[0][:, HALF:L], ktok[:], vblk.rearrange("p c v -> p (c v)"), start=True,
                       stop=True).then_inc(s.ctr_full, 1)
                    pe.wait_ge(s.p_ready, w.at("p_ready"))
                    if T == 0:
                        pe.wait_ge(s.vt_out, w.at("vt_out"))
                    for k in range(T + 1):
                        ins = nc.tensor.transpose(wide[1][:, k * P:(k + 1) * P], prob[:, T % 2, k * P:(k + 1) * P], ident[:])
                    ins.then_inc(s.t_full, 1)
                a_output(KT - 1)
                b_output(KT - 1)
                pe.wait_ge(s.s_max, w.at("s_max"))
                pe.wait_ge(s.o_sq, w.at("o_sq"))
                for lo_, hi_ in TOK:
                    ins = MM(wide[0][:, lo_:hi_], ones[:], ge[:, lo_:hi_], start=True, stop=True)
                ins.then_inc(s.o_stat, 1)
                w.skip("w_split")
                pe.wait_ge(s.ao_out, w.at("ao_out"))
                pe.wait_ge(s.bo_out, w.at("bo_out"))
            out_projection()

            for layer in range(LAYERS):
                def attention_turn(first):
                    if first:
                        first_pair()
                    for j in range(6):
                        if j == 2:
                            pe.wait_ge(s.m_ready, KT * (layer + 1))
                        if j < 2:
                            if not first:
                                linear(j, h_hi, h_lo)
                        else:
                            linear(j % 2, m_hi, m_lo, ((0, MEM),))
                    pe.wait_ge(s.lin_free, w.at("lin_out", 6))
                    for k in range(2):
                        for j in range(2):
                            c = (2 * k + j) * P
                            ins = nc.tensor.transpose(wide[0][:, c:c + P], xv[:, j, k * P:(k + 1) * P], ident[:])
                    ins.then_inc(s.vt_full, 1)
                    pe.wait_ge(s.vt_out, w.at("vt_out"))

                    def scores(p):
                        if p >= 2:
                            pe.wait_ge(s.p_exp, w.at("p_exp"))
                        for i in range(2):
                            c, q = (p % 2) * HALF + i * MEM, 2 * p + i
                            for j in range(2):
                                ins = MM(wide[0][:, c:c + MEM], xq[:, j, q * P:(q + 1) * P], xk[:, j], start=j == 0, stop=j == 1)
                        ins.then_inc(s.s_full, 1)

                    def transposes(p):
                        pe.wait_ge(s.p_ready, w.at("p_ready"))
                        for k in range(2):
                            for i in range(2):
                                c = (p % 2) * HALF + (2 * k + i) * P
                                ins = nc.tensor.transpose(wide[1][:, c:c + P], xp[:, p % 2, i, k * P:(k + 1) * P], ident[:])
                        ins.then_inc(s.t_full, 1)

                    def output(half):
                        pe.wait_ge(s.t_out, w.at("t_out", 2))
                        for j in range(2):
                            for k in range(2):
                                ins = MM(lin[half][:, j * HALF:(j + 1) * HALF], xvt[:, k, j * P:(j + 1) * P],
                                         xpT[half][:, k], start=k == 0, stop=k == 1)
                            ins.then_inc(s.bo_full, 1)

                    scores(0)
                    scores(1)
                    for p in range(2):
                        transposes(p)
                        scores(p + 2)
                    output(0)
                    transposes(2)
                    transposes(3)
                    output(1)
                    pe.wait_ge(s.p_exp, w.at("p_exp", 2))
                    pe.wait_ge(s.bo_out, w.at("bo_out", 4))

                attention_turn(True)
                with w.repeat(HEADS - 1, w_split=6, lin_free=6, lin_out=6, vt_out=1, p_exp=4, p_ready=4, t_out=4, bo_out=4):
                    attention_turn(False)
                out_projection()

                def up(first=False):
                    for j in range(2):
                        if first and j == 0:
                            first_pair()
                        else:
                            linear(0, h_hi, h_lo)
                            linear(1, h_hi, h_lo)

                def down(c):
                    pe.wait_ge(s.hid_ready, w.at("hid_ready", 2))
                    for j in range(2):
                        pe.wait_ge(s.w_ready, w.at("w_split"))
                        for n in range(4):
                            pe.wait_ge(s.out_free, w.at("out_free"))
                            for k in range(2):
                                m = n * P
                                t_ = 2 * (c % 2) + k
                                ins = passes(wide[n % 2], col2(w_hi, j)[:, k, m:m + P], col2(w_lo, j)[:, k, m:m + P],
                                             hid_hi[:, t_], hid_lo[:, t_], k == 0, k == 1, TOK)
                            ins.then_inc(s.w_used if n == 3 else s.out_full, 1)

                up(first=True)
                with w.repeat(FC // 2, w_split=12, lin_free=8, hid_ready=4, out_free=16):
                    up()
                    down(0)
                    up()
                    down(1)
                down(FC - 1)
                w.skip("lin_out", 2 * FT)
                w.skip("sum_out", FC * KT)
                post_norm()
                if layer == LAYERS - 1:
                    continue
                for k in range(KT):
                    pre_sums(k)
                spread()

                def u_dyn(t2, g):
                    return ub[:, t2, ds(g, 1)].rearrange("p g j -> p (g j)")

                with w.repeat(KT // 2, wr_done=2, m1a_out=2, m1b_out=2, x_out=2) as i:
                    for b in range(2):
                        pe.wait_ge(s.wr_done, w.at("wr_done"))
                        for t2 in range(2):
                            for g in range(8):
                                ins = nc.tensor.transpose(lin[t2][:, g * P:(g + 1) * P],
                                                          wr[:, g, 8 * t2:8 * t2 + 8].rearrange("p n c -> p (n c)"), ident[:])
                            ins.then_inc(s.m1_full, 1)
                        pe.wait_ge(s.m1a_out, w.at("m1a_out"))
                        pe.wait_ge(s.m1b_out, w.at("m1b_out"))
                        pe.wait_ge(s.u_in, 16 * SB)
                        pe.wait_ge(s.x_out, w.at("x_out"))
                        for o in range(2):
                            for g in range(8):
                                for t2 in range(2):
                                    ins = MM(wide[b][:, o * HALF + g * NB:o * HALF + (g + 1) * NB], m1[:, o, t2, g],
                                             u_dyn(t2, i * 16 + (8 * b + g)), start=t2 == 0, stop=t2 == 1)
                        ins.then_inc(s.x_full, 1)
                pe.wait_ge(s.x_out, w.at("x_out", 2))

                def kernels(b):
                    pe.wait_ge((s.d_in0, s.d_in1)[b], w.at(f"d_in{b}", 32))
                    for g in range(8):
                        ins = MM(lin[g // 4][0:16, (g % 4) * 256:(g % 4 + 1) * 256], w15[b][:, g * GC:(g + 1) * GC],
                                 dt_[b][:, 0:SB, g * GC:(g + 1) * GC], start=True, stop=True)
                    ins.then_inc(s.k_full, 1)

                def toeplitz(b, k8, wait):
                    pe.wait_ge(s.t_in, w.at("t_in", 128))
                    if wait:
                        pe.wait_ge(s.yt_out, w.at("yt_out"))
                    for g in range(8):
                        MM(wide[b][:, g * NB:(g + 1) * NB], tz[:, g, 0:P], u_dyn(0, k8 + g), start=True, stop=True)
                        o = wide[b][:, HALF + g * NB:HALF + (g + 1) * NB]
                        MM(o, tz[:, g, 0:P], u_dyn(1, k8 + g), start=True, stop=False)
                        ins = MM(o, tz[:, g, P:2 * P], u_dyn(0, k8 + g), start=False, stop=True)
                    ins.then_inc(s.yt_full, 1)

                kernels(0)
                pe.wait_ge(s.k_out, w.at("k_out"))
                with w.repeat(KT // 2 - 1, d_in0=32, d_in1=32, t_in=256, yt_out=2, k_out=2) as i:
                    for b in range(2):
                        kernels(1 - b)
                        toeplitz(b, i * 16 + 8 * b, False)
                        pe.wait_ge(s.yt_out, w.at("yt_out"))
                        pe.wait_ge(s.k_out, w.at("k_out"))
                kernels(1)
                toeplitz(0, (KT - 2) * 8, False)
                pe.wait_ge(s.yt_out, w.at("yt_out"))
                pe.wait_ge(s.k_out, w.at("k_out"))
                toeplitz(1, (KT - 1) * 8, False)
                pe.wait_ge(s.yt_out, w.at("yt_out"))
                pe.wait_ge(s.scan_done, w.at("scan_done"))
                with w.repeat(KT // 2, dr_done=2, y2_out=2) as i:
                    for b in range(2):
                        pe.wait_ge(s.dr_done, w.at("dr_done"))
                        pe.wait_ge(s.y2_out, w.at("y2_out"))
                        for t2 in range(2):
                            for g in range(8):
                                c = t2 * HALF + g * NB
                                ins = MM(wide[b][:, c + 1:c + NB], dr[b][:, g, 8 * t2:8 * t2 + 8].rearrange("p n c -> p (n c)"),
                                         hs[:, 0, ds(i * 16 + (8 * b + g), 1), 0:NB - 1].rearrange("p g j -> p (g j)"),
                                         start=True, stop=True)
                        ins.then_inc(s.y2_full, 1)
                linear(0, h_hi, h_lo, ahead=arriving)
                linear(1, h_hi, h_lo)
                with w.repeat(KT - 1, w_split=2, lin_free=2):
                    for j in range(2):
                        linear(j, h_hi, h_lo)
                w.skip("lin_out", 2 * KT)
                post_norm()


_IN = ("ab_w_in", "ab_w_out", "s5_w_glu", "xattn_wq", "xattn_wkv", "xattn_wo", "ffn_w_in", "ffn_w_out")


def constants():
    c = np.zeros((P, NCON), np.float32)
    c[:, C_ID:C_ID + P] = np.eye(P)
    i = np.arange(P)
    c[:, C_CAUSAL:C_CAUSAL + P] = (i[:, None] // CH == i[None] // CH) & (i[:, None] <= i[None])
    c[:, C_BLK:C_BLK + 4] = i[:, None] // CH == np.arange(4)[None]
    back = i[:, None] + (L - P) - np.arange(L)[None]
    times = (back >= 0) * ((back <= 128) * 1.0 + ((back % 4 == 0) & (back <= 512)) + (back % 16 == 0))
    c[:, C_LOGC:C_LOGC + L] = np.where(times > 0, np.log(np.maximum(times, 1)) / B_SCALE, -1e30)
    half = 64
    freq = np.float32(10000.0) ** (-np.arange(half, dtype=np.float32) / half)
    ang = (np.arange(L, dtype=np.float32)[None] * freq[:, None]).astype(np.float32).astype(np.float64)
    c[:, C_COS:C_COS + L] = np.tile(np.cos(ang), (2, 1))
    c[:, C_SIN:C_SIN + L] = np.concatenate([np.sin(ang), -np.sin(ang)])
    c[:, C_SIGN] = np.where(i < 64, -1, 1)
    c[:, C_SIGN + 1] = np.where(i < 64, 1, -1)
    c[:, C_FIRST:C_FIRST + L] = (np.arange(L) % CH != 0)[None]
    return c


def kernel(**inputs):
    import concourse.bacc as bacc
    from concourse.bass_utils import run_bass_kernel_spmd

    a = {k: np.asarray(v) for k, v in inputs.items()}
    arrays = {n: np.ascontiguousarray(a[n]) for n in _IN}
    arrays["xT"] = np.ascontiguousarray(a["x"][0].T)
    arrays["memT"] = np.ascontiguousarray(a["mem"][0].T)

    def tiles(v):
        return np.moveaxis(v.reshape(*v.shape[:-1], -1, P), -1, 0).reshape(P, -1)

    arrays["par"] = np.concatenate([tiles(a[n]) for n in ("norm_w", "mem_norm_w", "hgrn_lb_logits",
                                                          "hgrn_out_norm_w", "s5_d")], axis=1)
    arrays["con"] = constants()
    lr, li = a["s5_lambda_re"][0].T, a["s5_lambda_im"][0].T
    dt = np.broadcast_to(a["s5_log_dt"][0][None], lr.shape)
    arrays["s5_small"] = np.tile(np.concatenate([lr, li, dt], axis=1), (2, 1))
    for n, re, im in (("s5_b", a["s5_b_re"][0].transpose(1, 0, 2), a["s5_b_im"][0].transpose(1, 0, 2)),
                      ("s5_c", a["s5_c_re"][0].transpose(2, 0, 1), a["s5_c_im"][0].transpose(2, 0, 1))):
        re, im = re.reshape(64, -1), im.reshape(64, -1)
        arrays[n] = np.stack([np.concatenate([re, im]), np.concatenate([im, re])])
    nc = bacc.Bacc("TRN2", target_bir_lowering=False, num_devices=1)
    t = {n: nc.dram_tensor(n, v.shape, F32, kind="ExternalInput").ap() for n, v in arrays.items()}
    t["out"] = nc.dram_tensor("out", (D, L), F32, kind="ExternalOutput").ap()
    for n, shape in (("u_d", (D, L)), ("y_d", (D, L)), ("x_d", (D, L)), ("w_d", (SB, P, GR * GC)),
                     ("dd_d", (SB + 1, P, GR * GC)), ("pc_d", (P, 4, GR)), ("pw_d", (P, 2, GR))):
        t[n] = nc.dram_tensor(n, shape, F32, kind="Internal").ap()
    program(nc, t)
    r = run_bass_kernel_spmd(nc, [arrays], core_ids=[0])
    return np.ascontiguousarray(r.results[0]["out"].T)[None]
```

```python
from contextlib import ExitStack, contextmanager

import concourse.bass as bass
import numpy as np
from concourse import mybir

F32 = mybir.dt.float32
F32R = mybir.dt.float32r
ALU = mybir.AluOpType
ACT = mybir.ActivationFunctionType
AX = mybir.AxisListType.X
ds = bass.ds

P = 128
D = 1024
L = 1024
LAYERS = 2
KT = D // P
HALF = 512
MEM = 256
DFF = 2816
FT = DFF // P
FC = FT // 2
HEADS = 4
CH = 32
NCH = L // CH
EPS = 1e-6
B_SCALE = 128 ** -0.5
X_SCALE = 256 ** -0.5
AW = 512

GR = 64
GC = 16
SB = 16
NB = L // SB

TWO_PI = 2 * np.pi
ROUND = 1.5 * 2 ** 23
TURN = (6.28125, 0.0019350051879882812, float(TWO_PI - 6.28125 - 0.0019350051879882812))
PI_IN = 3.1415925

NW = 0
MNW = NW + 2 * 6 * KT
LBL = MNW + 2 * KT
ONW = LBL + 3 * HEADS
SD = ONW + HEADS
NPAR = SD + KT
C_ID = 0
C_CAUSAL = C_ID + P
C_BLK = C_CAUSAL + P
C_SIGN = C_BLK + 4
C_LOGC = C_SIGN + 4
C_COS = C_LOGC + L
C_SIN = C_COS + L
C_FIRST = C_SIN + L
NCON = C_FIRST + L


ALIASES = (("product", 2), ("w_split", 2), ("lin_out", 2), ("sum_out", 2), ("acc_sum", 2), ("x_taken", 2),
           ("y2_added", 2))


class Count:

    def __init__(self, n=0):
        self.n, self.i, self.per, self.base = n, None, 0, 0

    def next(self, k=1):
        self.n += k
        return self.n if self.i is None else self.i * self.per + self.n


class Counts:

    def __init__(self, eng, names):
        self.eng = eng
        self.c = {name: Count() for name in names}
        for name, primed in ALIASES:
            self.c[name] = Count(primed)

    def at(self, name, k=1):
        return self.c[name].next(k)

    def skip(self, name, k=1):
        self.c[name].next(k)

    @contextmanager
    def repeat(self, n, **per):
        with self.eng.Fori(0, n) as i:
            for name, c in self.c.items():
                c.i, c.per, c.base = i, per.get(name, 0), c.n
            yield i
            for name, c in self.c.items():
                assert c.n - c.base == c.per, (name, c.n - c.base, c.per)
                c.i, c.n = None, c.base + c.per * n


def program(nc, t):
    with ExitStack() as ctx:
        def place(name, shape, dt, at):
            return nc.alloc_sbuf_tensor_at(name, shape, dt, offset=BASE + at)

        BASE = (nc.sbuf_base + 31) // 32 * 32
        KB = 1024
        FENCE = 163 * KB + 45 * KB - 256
        ctx.enter_context(nc.sbuf_tensor("fence", [P, FENCE // 4], F32))
        x = place("x", [P, KT, L], F32, 0)
        h_hi = place("h_hi", [P, KT, L], F32R, 32 * KB)
        h_lo = place("h_lo", [P, KT, L], F32R, 64 * KB)
        y = place("y", [P, KT, L], F32, 96 * KB)
        w_raw = place("w_raw", [P, 2, L], F32, 128 * KB)
        w_hi = place("w_hi", [P, 2, L], F32R, 136 * KB)
        w_lo = place("w_lo", [P, 2, L], F32R, 144 * KB)
        rstd = place("rstd", [P, L], F32, 152 * KB)
        acc = place("acc", [P, L], F32, 156 * KB)
        ident = place("ident", [P, P], F32, 160 * KB)
        ones = place("ones", [P, P], F32, 160 * KB + 512)
        par = place("par", [P, NPAR], F32, 161 * KB)
        eps = place("eps", [P, 2], F32, 161 * KB + 640)
        lbt = place("lbt", [P, 8 * HEADS], F32, 161 * KB + 704)
        root8 = place("root8", [P, KT], F32, 161 * KB + 832)
        root8_hi = place("root8_hi", [P, KT], F32R, 161 * KB + 928)
        root8_lo = place("root8_lo", [P, KT], F32, 161 * KB + 960)
        diag_hi = place("diag_hi", [P, KT, P], F32R, 156 * KB)
        diag_lo = place("diag_lo", [P, KT, P], F32R, 152 * KB)
        rstd_m = place("rstd_m", [P, MEM], F32, 162 * KB)
        A0 = 163 * KB
        ones_r = place("ones_r", [P, P], F32R, A0 + 45120)
        sq = place("sq", [P, 2, L], F32, A0 + 32 * KB)
        tmp = place("tmp", [P, 2, L], F32, A0)

        zq = place("zq", [P, L], F32, 0)
        zf = place("zf", [P, L], F32, 4 * KB)
        zi = place("zi", [P, L], F32, 8 * KB)
        zg = place("zg", [P, L], F32, 12 * KB)
        gk = place("gk", [P, L], F32, 16 * KB)
        gb = place("gb", [P, L], F32, 20 * KB)
        ge = place("ge", [P, L], F32, 24 * KB)
        bq = place("bq", [P, L], F32, 28 * KB)
        bk = place("bk", [P, L], F32, A0)
        vtok_b = place("vtok_b", [P, KT, P], F32, A0 + 4 * KB)
        prob = place("prob", [P, 2, L], F32, A0 + 8 * KB)
        probT = place("probT", [P, KT, P], F32, A0 + 16 * KB)
        cosr = place("cosr", [P, L], F32, A0 + 20 * KB)
        sinr = place("sinr", [P, L], F32, A0 + 24 * KB)
        logc = place("logc", [P, L], F32, A0 + 28 * KB)
        first = place("first", [P, L], F32, A0 + 32 * KB)
        states = place("states", [P, 8, P], F32, A0 + 36 * KB)
        M0 = A0 + 40 * KB
        ktok = place("ktok", [P, P], F32, M0)
        vtok = place("vtok", [P, 2, P], F32, M0 + 512)
        X0 = M0 + 1536
        causal = place("causal", [P, P], F32, X0)
        scm = place("scm", [P, 2, P], F32, X0 + 512)
        blk = place("blk", [P, 4], F32, X0 + 1536)
        dec = place("dec", [P, NCH], F32, X0 + 1536 + 32)
        hp = place("hp", [P, HEADS, 3], F32, 161 * KB + 864)
        cur = place("cur", [P, 3], F32, X0 + 1536 + 224)
        stat = place("stat", [P, 2, 4], F32, X0 + 1536 + 256)
        vblk = acc[:, 0:512].rearrange("p (c v) -> p c v", c=4)

        hid_hi = place("hid_hi", [P, 4, L], F32R, A0)
        hid_lo = place("hid_lo", [P, 4, L], F32R, A0 + 16 * KB)
        gate = place("gate", [P, L], F32, A0 + 32 * KB)
        f_act = place("act", [P, L], F32, A0 + 36 * KB)

        m_hi = place("m_hi", [P, KT, MEM], F32R, A0)
        m_lo = place("m_lo", [P, KT, MEM], F32R, A0 + 8 * KB)
        xq = place("xq", [P, 2, L], F32, A0 + 16 * KB)
        xk = place("xk", [P, 2, MEM], F32, A0 + 24 * KB)
        xv = place("xv", [P, 2, MEM], F32, A0 + 26 * KB)
        xvt = place("xvt", [P, 2, MEM], F32, A0 + 28 * KB)
        xp = place("xp", [P, 2, 2, MEM], F32, A0 + 36 * KB + 64)
        xpT = [place(f"xpT{i}", [P, 2, HALF], F32, A0 + (32, 40)[i] * KB + 64 * i) for i in range(2)]
        xstat = place("xstat", [P, 2, 4, 2], F32, A0 + 36 * KB)
        m_raw = place("m_raw", [P, KT, MEM], F32, A0 + 36 * KB + 64)
        m_sq = place("m_sq", [P, KT, MEM], F32, 96 * KB)

        sg = place("sg", [P, L], F32, A0 + 8 * KB)
        sgn = place("sgn", [P, 2], F32, 161 * KB + 672)
        o_src = [place(f"o_src{i}", [P, GR, GC], F32, 4 * i * KB) for i in range(2)]
        o_dst = [place(f"o_dst{i}", [P, GR, GC], F32, (8 + 4 * i) * KB) for i in range(2)]
        o_tmp = place("o_tmp", [P, GR, GC], F32, 16 * KB)
        pw = place("pw", [P, 2, GR], F32, 20 * KB)
        pc = place("pc", [P, 4, GR], F32, 20 * KB + 8704)
        pt = place("pt", [P, 4, GR], F32, 20 * KB + 8704 + 1024)
        sp_in = place("sp_in", [P, 3, GR], F32, A0)
        sv = place("sv", [P, 16, GR], F32, A0 + 1024)

        ub = place("ub", [P, 2, GR, NB], F32, 32 * KB)
        hs = place("hs", [P, 2, GR, NB], F32, 64 * KB)
        yT = place("yT", [P, KT, L], F32, 64 * KB)
        wt = [place(f"wt{i}", [P, SB, P], F32, A0 + 32 * i * KB) for i in range(2)]
        m1 = place("m1", [P, 2, 2, 8, P], F32, A0 + 8 * KB)
        wr = place("wr", [P, 8, SB, GC], F32, A0 + 24 * KB)
        dr = [place(f"dr{i}", [P, 8, SB, GC], F32, A0 + (18 + 8 * i) * KB) for i in range(2)]
        dt_ = [place(f"dt{i}", [P, SB + 1, P], F32, A0 + 8704 * i) for i in range(2)]
        w15 = [place(f"w15_{i}", [P, P], F32, A0 + 17408 + 512 * i) for i in range(2)]
        kpad = place("kpad", [16, 8, 23 * GC], F32, A0 + 18432)
        tz = [place(f"tz{i}", [P, 8, 2 * P], F32, (A0 + 30208, 152 * KB)[i]) for i in range(2)]
        ar_b = place("ar_b", [P, GR], F32, A0 + 41 * KB)
        sai_b = place("sai_b", [P, 2, GR], F32, A0 + 41 * KB + 256)
        sc1 = place("sc1", [P, 2, GR], F32, A0 + 41 * KB + 768)
        sc2 = place("sc2", [P, 2, GR], F32, A0 + 41 * KB + 1280)

        bank = [ctx.enter_context(nc.psum_tensor(f"bank{i}", [P, 1024], F32)) for i in range(4)]
        lin = bank[0:2]
        wide = bank[2:4]

        names = """
            par_in x_in con_in0 con_in1 mem_in out_done w_load0 w_load1 w_hi_done w_ready w_used
            lin_free out_full out_free setup lb_max lb_exp sq_done sq_free stat_full sqrt_done
            diag_done spread_full tmp_done rstd_m_done rstd_done x_done hi_done h_ready v_step
            g_step f_exp f_sig f_kept f_log b_scan b_exp q_dec b_neg y_zero k_inv b_left b_left_exp
            k_end g_exp a1_full a1_out ctr_full st_done ao_full ao_out s_full s_max p_exp p_sum
            p_ready t_full t_out bo_full bo_out vt_full vt_out o_sq o_stat o_root o_done rope_done
            s5_in s5_exp s5_mag s5_abs s5_trig s5_made s5_kept x_sent ops_in ops_out0 ops_out1
            x_back u_done u_out0 u_out1 u_in0 u_in1 wt_in0 wt_in1 wr_done dr_done m1_full m1a_out
            m1b_out x_full x_out pw_in d_in0 d_in1 k_full k_out t_in0 t_in1 yt_full yt_out scan_done
            y2_full y2_out y_sent0 y_sent1 yT_in0 yT_in1 g_in g_done  m_hi_done
            m_ready silu_done hid_done hid_hi_done hid_ready
        """
        sems = {n: ctx.enter_context(nc.semaphore(n)) for n in names.split()}
        s = type("Sems", (), sems)
        block = ctx.enter_context(nc.Block())

        def nw(layer, which, k):
            c = NW + (layer * 6 + which) * KT + k
            return par[:, c:c + 1]

        con = t["con"]
        xv_d = t["xT"].rearrange("(k p) t -> p k t", p=P)
        mem_d = t["memT"].rearrange("(k p) t -> p k t", p=P)
        out_d = t["out"].rearrange("(k p) t -> p k t", p=P)

        def w_view(name, layer=0):
            return t[name][layer].rearrange("(k p) n -> p k n", p=P)

        def col8(ap, parity):
            return ap[:, parity].rearrange("p (k n) -> p k n", k=KT)

        def col2(ap, parity):
            return ap[:, parity].rearrange("p (k n) -> p k n", k=2)

        @block.sync
        def _(sp):
            w = Counts(sp, sems)
            sp.dma_start(par[:], t["par"]).then_inc(s.par_in, 16)
            sp.dma_start(ident[:], con[:, C_ID:C_ID + P]).then_inc(s.par_in, 16)
            sp.dma_start(sp_in[:].rearrange("p a g -> p (a g)"), t["s5_small"]).then_inc(s.s5_in, 16)
            sp.dma_start(sgn[:], con[:, C_SIGN:C_SIGN + 2]).then_inc(s.s5_in, 16)
            sp.dma_start(m_raw[:], mem_d).then_inc(s.mem_in, 16)
            sp.dma_start(x[:], xv_d).then_inc(s.x_in, 16)

            def load(parity, dst, src):
                sp.wait_ge(s.w_ready, w.at("w_ready"))
                sp.dma_start(dst, src).then_inc((s.w_load0, s.w_load1)[parity], 16)

            def columns(parity, src, n0):
                load(parity, col8(w_raw, parity), src[:, :, ds(n0, P)])

            win = w_view("ab_w_in")
            with w.repeat(HEADS, w_ready=8) as h:
                for j in range(7):
                    columns(j % 2, win, h * P + j * AW)
                w.skip("w_ready")
            wout = w_view("ab_w_out")
            with w.repeat(KT // 2, w_ready=2) as i:
                for j in range(2):
                    columns(j, wout, i * (2 * P) + j * P)
            for layer in range(LAYERS):
                wq, wkv, wo = w_view("xattn_wq", layer), w_view("xattn_wkv", layer), w_view("xattn_wo", layer)
                with w.repeat(HEADS, w_ready=6) as h:
                    for j in range(2):
                        columns(j, wq, h * MEM + j * P)
                    for j in range(2):
                        columns(j, wkv, h * MEM + j * P)
                    for j in range(2):
                        columns(j, wkv, h * MEM + (D + j * P))
                with w.repeat(KT // 2, w_ready=2) as i:
                    for j in range(2):
                        columns(j, wo, i * (2 * P) + j * P)
                wi, wd = w_view("ffn_w_in", layer), t["ffn_w_out"][layer]

                def up(c):
                    for j in range(2):
                        columns(0, wi, c * (2 * P) + j * P)
                        columns(1, wi, c * (2 * P) + (DFF + j * P))

                def down(c):
                    for j in range(2):
                        load(j, col2(w_raw, j),
                             wd[ds(c * (2 * P), 2 * P), j * HALF:(j + 1) * HALF].rearrange("(k p) n -> p k n", p=P))

                up(0)
                with w.repeat(FC // 2, w_ready=12) as i:
                    up(i * 2 + 1)
                    down(i * 2)
                    up(i * 2 + 2)
                    down(i * 2 + 1)
                down(FC - 1)
                if layer == 1 or LAYERS == 1:
                    continue
                wg = w_view("s5_w_glu")
                for j in range(2):
                    columns(j, wg, (1 - j) * D)
                ud = t["u_d"].rearrange("(k p) t -> k p t", p=P)
                for k in range(KT):
                    sp.wait_ge(s.u_done, w.at("u_done"))
                    sp.dma_start(ud[k], y[:, k]).then_inc((s.u_out0, s.u_out1)[k // 4], 16)

                def by_channel(name, n):
                    return t[name].rearrange("(g c) (s j) -> s c g j", c=GC, s=SB)[n]

                def wt_load(k, b):
                    sp.dma_start(wt[b][:], t["w_d"].rearrange("n p c -> p n c")[:, :, ds(k * P, P)]).then_inc(
                        (s.wt_in0, s.wt_in1)[b], 16)

                wt_load(0, 0)
                wt_load(1, 1)
                for half in range(2):
                    g0 = half * GR // 2
                    sp.wait_ge((s.u_out0, s.u_out1)[half], 16 * KT // 2)
                    for n in range(SB):
                        p0 = (n % 8) * GC
                        sp.dma_start(ub[p0:p0 + GC, n // 8, g0:g0 + GR // 2],
                                     by_channel("u_d", n)[:, g0:g0 + GR // 2]).then_inc((s.u_in0, s.u_in1)[half], 16)
                with w.repeat(KT // 2 - 1, wr_done=2) as i:
                    for b in range(2):
                        sp.wait_ge(s.wr_done, w.at("wr_done"))
                        wt_load(i * 2 + (2 + b), b)
                sp.wait_ge(s.x_out, w.at("x_taken", KT))
                sp.dma_start(ar_b[:], t["pw_d"][:, 0]).then_inc(s.pw_in, 16)
                sp.dma_start(sai_b[:, 0], t["pw_d"][:, 1]).then_inc(s.pw_in, 16)

                def d_load(k, b, with_w15):
                    sp.dma_start(dt_[b][:], t["dd_d"].rearrange("n p c -> p n c")[:, :, ds(k * P, P)]).then_inc((s.d_in0, s.d_in1)[b], 16)
                    if with_w15:
                        sp.dma_start(w15[b][:], t["w_d"][SB - 1][:, ds(k * P, P)]).then_inc((s.d_in0, s.d_in1)[b], 16)

                def t_load(b):
                    sp.wait_ge(s.k_out, w.at("k_out"))
                    for n in range(8):
                        c = (7 - n) * GC
                        sp.dma_start(tz[b][n * GC:(n + 1) * GC], kpad[:, :, c:c + 2 * P]).then_inc((s.t_in0, s.t_in1)[b], 16)

                for k in range(2):
                    d_load(k, k, True)
                for k in range(2):
                    t_load(k)
                    d_load(k + 2, k, True)
                with w.repeat(KT // 2 - 2, k_out=2) as i:
                    for b in range(2):
                        t_load(b)
                        d_load(i * 2 + (4 + b), b, True)
                for b in range(2):
                    t_load(b)
                    d_load(b, b, False)
                with w.repeat(KT // 2 - 1, dr_done=2) as i:
                    for b in range(2):
                        sp.wait_ge(s.dr_done, w.at("dr_done"))
                        d_load(i * 2 + 2 + b, b, False)
                yd = t["y_d"].rearrange("(k p) t -> p k t", p=P)
                for half in range(2):
                    g0, k0 = half * GR // 2, half * KT // 2
                    sp.wait_ge(s.y2_out, w.at("y2_added", KT // 2))
                    for n in range(SB):
                        p0 = (n % 8) * GC
                        sp.dma_start(by_channel("y_d", n)[:, g0:g0 + GR // 2],
                                     ub[p0:p0 + GC, n // 8, g0:g0 + GR // 2]).then_inc((s.y_sent0, s.y_sent1)[half], 16)
                    sp.wait_ge((s.y_sent0, s.y_sent1)[half], 16 * SB)
                    sp.dma_start(yT[:, k0:k0 + KT // 2], yd[:, k0:k0 + KT // 2]).then_inc((s.yT_in0, s.yT_in1)[half], 16)
                with w.repeat(KT - 1, w_ready=2) as i:
                    for j in range(2):
                        columns(j, wg, i * P + (P + (1 - j) * D))
            w.skip("x_done", KT * (3 * LAYERS - 1))
            for k in range(KT):
                sp.wait_ge(s.x_done, w.at("x_done"))
                sp.dma_start(out_d[:, k], x[:, k]).then_inc(s.out_done, 16)
            sp.wait_ge(s.out_done, 16 * KT)

        @block.scalar
        def _(act):
            w = Counts(act, sems)
            A = nc.scalar.activation

            def split(parity):
                act.wait_ge((s.w_load0, s.w_load1)[parity], w.at(f"w_load{parity}", 16))
                act.wait_ge(s.w_used, w.at("w_used"))
                A(w_hi[:, parity], w_raw[:, parity], ACT.Copy).then_inc(s.w_hi_done, 1)

            def factor(pre):
                if pre:
                    act.wait_ge(s.sq_free, w.at("acc_sum", KT))
                else:
                    act.wait_ge(s.stat_full, w.at("stat_full"))
                    w.skip("acc_sum", KT)
                A(root8[:], wide[1][:, 0:KT], ACT.Sqrt, bias=eps[:, 0:1], scale=1.0 / D).then_inc(s.sqrt_done, 1)
                for lo_, hi_ in ((0, HALF), (HALF, L)):
                    act.wait_ge(s.spread_full, w.at("spread_full"))
                    ins = A(rstd[:, lo_:hi_], wide[0][:, lo_:hi_], ACT.Copy)
                ins.then_inc(s.rstd_done, 1)

            def prenorm(layer, which, k):
                A(h_hi[:, k], x[:, k], ACT.Copy, scale=nw(layer, which, k)).then_inc(s.hi_done, 1)
                act.wait_ge(s.sq_free, w.at("sq_free"))
                A(sq[:, k % 2], x[:, k], ACT.Square).then_inc(s.sq_done, 1)

            def boundary(layer, which, s5=False):
                factor(False)
                for k in range(KT):
                    act.wait_ge(s.x_done, w.at("x_done"))
                    if which is not None:
                        prenorm(layer, which, k)
                    if s5:
                        act.wait_ge(s.sq_free, w.at("sq_free"))
                        A(sq[:, k % 2], x[:, k], ACT.Square).then_inc(s.sq_done, 1)
                if which is not None or s5:
                    factor(True)

            def split_y():
                for k in range(KT):
                    A(h_hi[:, k], y[:, k], ACT.Copy).then_inc(s.hi_done, 1)

            def out_projection():
                with w.repeat(KT // 2, product=2, w_used=2, w_load0=16, w_load1=16, sq_free=2) as i:
                    for j in range(2):
                        act.wait_ge(s.w_used, w.at("product"))
                        act.wait_ge(s.sq_free, w.at("sq_free"))
                        A(sq[:, j], lin[j][:], ACT.Square).then_inc(s.sq_done, 1)
                        A(y[:, ds(i * 2 + j, 1)].rearrange("p k t -> p (k t)"), lin[j][:],
                          ACT.Copy).then_inc(s.lin_free, 1)
                        split(j)
                w.skip("lin_out", KT)

            act.wait_ge(s.setup, w.at("setup"))
            act.wait_ge(s.par_in, w.at("par_in", 32))
            act.wait_ge(s.lb_max, w.at("lb_max"))
            A(lbt[:, 4:16], lbt[:, 4:16], ACT.Exp).then_inc(s.lb_exp, 1)

            act.wait_ge(s.s5_in, w.at("s5_in", 32))
            A(sv[:, 0], sp_in[:, 2], ACT.Exp).then_inc(s.s5_exp, 1)
            act.wait_ge(s.s5_mag, w.at("s5_mag"))
            A(sv[:, 3], sv[:, 1], ACT.Exp).then_inc(s.s5_abs, 1)
            A(sv[:, 4], sv[:, 2], ACT.Abs).then_inc(s.s5_abs, 1)
            act.wait_ge(s.s5_abs, w.at("s5_abs", 2))
            A(sv[:, 5], sv[:, 2], ACT.Sin).then_inc(s.s5_trig, 1)
            A(sv[:, 6], sv[:, 4], ACT.Sin, scale=-1.0, bias=eps[:, 1:2]).then_inc(s.s5_trig, 1)
            act.wait_ge(s.s5_made, w.at("s5_made"))
            act.dma_start(t["pc_d"], sv[:, 8:12]).then_inc(s.s5_kept, 16)

            act.wait_ge(s.mem_in, w.at("mem_in", 16))
            A(m_sq[:], m_raw[:], ACT.Square).then_inc(s.sq_done, 1)
            act.wait_ge(s.sq_done, w.at("sq_done"))
            act.wait_ge(s.stat_full, w.at("stat_full"))
            A(rstd_m[:], lin[1][:, 0:MEM], ACT.Sqrt, bias=eps[:, 0:1], scale=1.0 / D).then_inc(s.sqrt_done, 1)
            split(0)
            split(1)
            act.dma_start(cosr[:], con[:, C_COS:C_COS + L]).then_inc(s.con_in0, 16)
            act.dma_start(sinr[:], con[:, C_SIN:C_SIN + L]).then_inc(s.con_in0, 16)
            act.dma_start(logc[:], con[:, C_LOGC:C_LOGC + L]).then_inc(s.con_in0, 16)
            act.wait_ge(s.x_in, w.at("x_in", 16))
            for k in range(KT):
                prenorm(0, 0, k)
            factor(True)
            act.dma_start(first[:], con[:, C_FIRST:C_FIRST + L]).then_inc(s.con_in1, 16)
            act.dma_start(causal[:], con[:, C_CAUSAL:C_CAUSAL + P]).then_inc(s.con_in1, 16)
            act.dma_start(blk[:], con[:, C_BLK:C_BLK + 4]).then_inc(s.con_in1, 16)
            with w.repeat(HEADS, product=8, w_used=8, w_load0=64, w_load1=48, lin_out=7, f_sig=1, f_kept=1, b_scan=1,
                          q_dec=1, b_left=1, vt_full=1, s_max=8, t_full=8, ao_full=8, bo_full=8,
                          ao_out=8, o_stat=1) as h:
                act.wait_ge(s.w_used, w.at("product"))
                split(0)
                act.wait_ge(s.w_used, w.at("product"))
                split(1)
                act.wait_ge(s.lin_free, w.at("lin_out", 2))
                A(zf[:], zf[:], ACT.Exp, scale=-1.0).then_inc(s.f_exp, 1)
                act.wait_ge(s.w_used, w.at("product"))
                split(0)
                act.wait_ge(s.f_sig, w.at("f_sig"))
                A(ge[:], zf[:], ACT.Ln).then_inc(s.f_log, 1)
                A(gk[:], zf[:], ACT.Copy, scale=-1.0, bias=1.0).then_inc(s.f_kept, 1)
                act.wait_ge(s.b_scan, w.at("b_scan"))
                A(ge[:], gb[:], ACT.Exp).then_inc(s.b_exp, 1)
                act.wait_ge(s.f_kept, w.at("f_kept"))
                A(zf[:], gb[:], ACT.Exp, scale=-1.0).then_inc(s.b_neg, 1)
                act.wait_ge(s.w_used, w.at("product"))
                split(1)
                act.wait_ge(s.q_dec, w.at("q_dec"))
                act.wait_ge(s.b_left, w.at("b_left"))
                A(ge[:], ge[:], ACT.Exp).then_inc(s.b_left_exp, 1)
                act.wait_ge(s.lin_free, w.at("lin_out", 2))
                A(gb[:], zg[:], ACT.Exp, scale=-1.0).then_inc(s.g_exp, 1)
                act.wait_ge(s.w_used, w.at("product"))
                split(0)
                w.skip("lin_out", 3)
                w.skip("w_used")
                act.wait_ge(s.w_used, w.at("product", 3))
                split(0)
                split(1)

                def a_out(T):
                    act.wait_ge(s.ao_full, w.at("ao_full"))
                    A(zi[:, T * P:(T + 1) * P], lin[1][:, 0:P], ACT.Copy).then_inc(s.ao_out, 1)

                def b_out(T):
                    act.wait_ge(s.bo_full, w.at("bo_full"))
                    A(y[:, ds(h + HEADS, 1), T * P:(T + 1) * P].rearrange("p k t -> p (k t)"),
                      lin[1][:, HALF:HALF + P], ACT.Copy).then_inc(s.bo_out, 1)

                def tile_out(T):
                    a_out(T)
                    act.wait_ge(s.t_full, w.at("t_full"))
                    A(probT[:, 0:T + 1].rearrange("p k q -> p (k q)"), wide[1][:, 0:(T + 1) * P],
                      ACT.Copy).then_inc(s.t_out, 1)
                    b_out(T)

                act.wait_ge(s.vt_full, w.at("vt_full"))
                A(vtok_b[:].rearrange("p k d -> p (k d)"), wide[1][:], ACT.Copy).then_inc(s.vt_out, 1)
                for T in range(KT):
                    W = (T + 1) * P
                    act.wait_ge(s.s_max, w.at("s_max"))
                    A(prob[:, T % 2, 0:W], prob[:, T % 2, 0:W], ACT.Exp, bias=stat[:, T % 2, 1:2], scale=B_SCALE,
                      accum_out=stat[:, T % 2, 2:3]).then_inc(s.p_exp, 1)
                    if T:
                        tile_out(T - 1)
                tile_out(KT - 1)
                act.wait_ge(s.ao_out, w.at("ao_out", 8))
                A(ge[:], zi[:], ACT.Square).then_inc(s.o_sq, 1)
                act.wait_ge(s.o_stat, w.at("o_stat"))
                A(ge[:], wide[0][:], ACT.Sqrt, bias=eps[:, 0:1], scale=1.0 / P).then_inc(s.o_root, 1)
            act.wait_ge(s.o_done, w.at("o_done", HEADS))
            act.dma_start(x[:], xv_d).then_inc(s.x_in, 16)
            act.wait_ge(s.bo_out, w.at("bo_out", KT * HEADS))
            split_y()
            out_projection()
            boundary(0, 2)

            for layer in range(LAYERS):
                act.dma_start(m_raw[:], mem_d).then_inc(s.mem_in, 16)
                act.wait_ge(s.mem_in, w.at("mem_in", 16))
                for k in range(KT):
                    c = MNW + layer * KT + k
                    A(m_hi[:, k], m_raw[:, k], ACT.Copy, scale=par[:, c:c + 1]).then_inc(s.m_hi_done, 1)
                with w.repeat(HEADS, product=6, w_used=6, w_load0=48, w_load1=48, vt_full=1, s_max=4, t_full=4,
                              bo_full=4) as h:
                    def softmax(p):
                        act.wait_ge(s.s_max, w.at("s_max"))
                        for i in range(2):
                            c = (p % 2) * HALF + i * MEM
                            ins = A(xp[:, p % 2, i], wide[0][:, c:c + MEM], ACT.Exp, bias=xstat[:, p % 2, 1, i:i + 1],
                                    scale=X_SCALE, accum_out=xstat[:, p % 2, 2, i:i + 1])
                        ins.then_inc(s.p_exp, 1)

                    def transposed(p):
                        act.wait_ge(s.t_full, w.at("t_full"))
                        A(xpT[p // 2][:, :, (p % 2) * MEM:(p % 2 + 1) * MEM],
                          wide[1][:, (1 - p % 2) * HALF:(2 - p % 2) * HALF].rearrange("p (k q) -> p k q", k=2),
                          ACT.Copy).then_inc(s.t_out, 1)

                    def output(half):
                        for j in range(2):
                            act.wait_ge(s.bo_full, w.at("bo_full"))
                            A(y[:, ds(h * 2 + j, 1), half * HALF:(half + 1) * HALF].rearrange("p k t -> p (k t)"),
                              lin[half][:, j * HALF:(j + 1) * HALF], ACT.Copy).then_inc(s.bo_out, 1)

                    for j in range(6):
                        act.wait_ge(s.w_used, w.at("product"))
                        split(j % 2)
                        if j >= 4:
                            softmax(j - 4)
                    act.wait_ge(s.vt_full, w.at("vt_full"))
                    A(xvt[:].rearrange("p k d -> p (k d)"), wide[1][:, 0:HALF], ACT.Copy).then_inc(s.vt_out, 1)
                    for p in range(2):
                        transposed(p)
                        softmax(p + 2)
                    output(0)
                    transposed(2)
                    transposed(3)
                    output(1)
                w.skip("lin_out", 6 * HEADS)
                act.wait_ge(s.bo_out, w.at("bo_out", 4 * HEADS))
                split_y()
                out_projection()
                boundary(layer, 4)

                def up(c):
                    for j in range(2):
                        act.wait_ge(s.w_used, w.at("product"))
                        split(0)
                        act.wait_ge(s.lin_free, w.at("lin_out"))
                        A(f_act[:], gate[:], ACT.Silu).then_inc(s.silu_done, 1)
                        act.wait_ge(s.w_used, w.at("product"))
                        w.skip("lin_out")
                        split(1)
                        act.wait_ge(s.hid_done, w.at("hid_done"))
                        A(hid_hi[:, 2 * (c % 2) + j], f_act[:], ACT.Copy).then_inc(s.hid_hi_done, 1)

                def down(c, last):
                    for j in range(2):
                        if c == FC - 1:
                            for n in range(4 * j, 4 * j + 4):
                                act.wait_ge(s.out_free, w.at("sum_out"))
                                act.wait_ge(s.sq_free, w.at("sq_free"))
                                A(sq[:, n % 2], y[:, n], ACT.Square).then_inc(s.sq_done, 1)
                        else:
                            w.skip("sum_out", 4)
                        act.wait_ge(s.w_used, w.at("product"))
                        if not last:
                            split(j)

                up(0)
                with w.repeat(FC // 2, product=12, w_used=12, w_load0=96, w_load1=96, lin_out=8, hid_done=4,
                              sum_out=16):
                    up(1)
                    down(0, False)
                    up(0)
                    down(1, False)
                down(FC - 1, layer == LAYERS - 1)
                if layer == LAYERS - 1:
                    boundary(None, None)
                    continue
                boundary(None, None, s5=True)

                with w.repeat(KT // 2, m1_full=4):
                    for b in range(2):
                        act.wait_ge(s.m1_full, w.at("m1_full"))
                        A(m1[:, b, 0].rearrange("p g c -> p (g c)"), lin[0][:], ACT.Copy).then_inc(s.m1a_out, 1)
                        w.skip("m1_full")
                act.wait_ge(s.x_out, w.at("x_taken", KT))
                A(kpad[:, :, 0:7 * GC], ident[0:16, 0:112].unsqueeze(1).to_broadcast([16, 8, 112]), ACT.Copy,
                  scale=0.0)

                def kernels(wait):
                    act.wait_ge(s.k_full, w.at("k_full"))
                    if wait is not None:
                        act.wait_ge((s.t_in0, s.t_in1)[wait], w.at(f"t_in{wait}", 128))
                    for b in range(2):
                        ins = A(kpad[:, 4 * b:4 * b + 4, 7 * GC:23 * GC],
                                lin[b][0:16, :].rearrange("p (g c) -> p g c", g=4), ACT.Copy)
                    ins.then_inc(s.k_out, 1)

                def toeplitz(b, k):
                    act.wait_ge(s.yt_full, w.at("yt_full"))
                    A(ub[:, :, ds(k * 8, 8)], wide[b][:].rearrange("p (g t j) -> p t g j", g=8, t=2),
                      ACT.Copy).then_inc(s.yt_out, 1)

                kernels(None)
                kernels(0)
                with w.repeat(KT // 2 - 1, k_full=2, t_in0=128, t_in1=128, yt_full=2) as i:
                    for b in range(2):
                        toeplitz(b, i * 2 + b)
                        kernels(1 - b)
                toeplitz(0, KT - 2)
                toeplitz(1, KT - 1)
                for half in range(2):
                    tiles_ = range(half * KT // 2, (half + 1) * KT // 2)
                    for k in tiles_:
                        act.wait_ge(s.g_in, w.at("g_in"))
                        A(y[:, k], yT[:, k], ACT.Gelu).then_inc(s.g_done, 1)
                    if half == 0:
                        act.wait_ge(s.y_sent0, 16 * SB)
                        act.wait_ge(s.y_sent1, 16 * SB)
                    for k in tiles_:
                        act.wait_ge(s.g_done, w.at("g_done"))
                        A(h_hi[:, k], y[:, k], ACT.Copy).then_inc(s.hi_done, 1)

                with w.repeat(KT // 2, product=4, w_used=4, w_load0=32, w_load1=32, lin_out=4, sq_free=2) as i:
                    for b in range(2):
                        act.wait_ge(s.w_used, w.at("product"))
                        A(sg[:], lin[0][:], ACT.Sigmoid).then_inc(s.lin_free, 1)
                        split(0)
                        act.wait_ge(s.w_used, w.at("product"))
                        split(1)
                        act.wait_ge(s.lin_free, w.at("lin_out", 2))
                        act.wait_ge(s.sq_free, w.at("sq_free"))
                        A(sq[:, b], y[:, ds(i * 2 + b, 1)].rearrange("p k t -> p (k t)"),
                          ACT.Square).then_inc(s.sq_done, 1)
                boundary(1, 2)

        @block.vector
        def _(dve):
            w = Counts(dve, sems)
            V = nc.vector

            def step(ins):
                ins.then_inc(s.v_step, 1)
                dve.wait_ge(s.v_step, w.at("v_step"))

            def split(parity):
                dve.wait_ge(s.w_hi_done, w.at("w_hi_done"))
                V.tensor_tensor(w_lo[:, parity], w_raw[:, parity], w_hi[:, parity].bitcast(F32),
                                ALU.subtract).then_inc(s.w_ready, 1)

            def factor():
                dve.wait_ge(s.sqrt_done, w.at("sqrt_done"))
                step(V.reciprocal(root8[:], root8[:]))
                step(V.tensor_copy(root8_hi[:], root8[:]))
                step(V.tensor_tensor(root8_lo[:], root8[:], root8_hi[:].bitcast(F32), ALU.subtract))
                for a in (0, 4):
                    eye = ident[:].unsqueeze(1).to_broadcast([P, 4, P])
                    for diag, part in ((diag_hi, root8_hi[:].bitcast(F32)), (diag_lo, root8_lo[:])):
                        ins = V.tensor_tensor(diag[:, a:a + 4], eye, part[:, a:a + 4].unsqueeze(2).to_broadcast([P, 4, P]),
                                              ALU.mult)
                    ins.then_inc(s.diag_done, 1)

            def low(src, k, scale=None):
                dve.wait_ge(s.hi_done, w.at("hi_done"))
                if scale is None:
                    V.tensor_tensor(h_lo[:, k], src[:, k], h_hi[:, k].bitcast(F32), ALU.subtract).then_inc(s.h_ready, 1)
                else:
                    V.scalar_tensor_tensor(h_lo[:, k], src[:, k], scale, h_hi[:, k].bitcast(F32), ALU.mult,
                                           ALU.subtract).then_inc(s.h_ready, 1)

            def natural(ap):
                return ap.rearrange("p (s j) -> p j s", s=SB)

            def boundary(layer, post, nlayer, pre, blocked=False):
                factor()
                w.skip("rstd_done")
                for k in range(KT):
                    dve.wait_ge(s.tmp_done, w.at("tmp_done"))
                    xk_, tk = x[:, k], tmp[:, k % 2]
                    if blocked:
                        xk_, tk = xk_.rearrange("p (j s) -> p j s", s=SB), natural(tk)
                    V.scalar_tensor_tensor(xk_, tk, nw(layer, post, k), xk_, ALU.mult,
                                           ALU.add).then_inc(s.x_done, 1)
                    if pre is not None and k:
                        low(x, k - 1, nw(nlayer, pre, k - 1))
                w.skip("x_done", KT)
                if pre is not None:
                    low(x, KT - 1, nw(nlayer, pre, KT - 1))
                    factor()
                    dve.wait_ge(s.rstd_done, w.at("rstd_done"))

            def split_y():
                for k in range(KT):
                    low(y, k)

            def out_projection():
                with w.repeat(KT // 2, w_hi_done=2):
                    for j in range(2):
                        split(j)
                w.skip("lin_out", KT)
                w.skip("product", KT)

            step(V.memset(ones[:], 1.0))
            V.tensor_copy(ones_r[:], ones[:])
            V.memset(eps[:, 1:2], float(np.pi / 2))
            V.memset(eps[:, 0:1], EPS).then_inc(s.setup, 1)
            dve.wait_ge(s.par_in, w.at("par_in", 32))
            lg = par[:, LBL:LBL + 3 * HEADS]
            step(V.tensor_tensor(lbt[:, 0:4], lg[:, 0:4], lg[:, 4:8], ALU.max))
            step(V.tensor_tensor(lbt[:, 0:4], lbt[:, 0:4], lg[:, 8:12], ALU.max))
            V.tensor_tensor(lbt[:, 4:16].rearrange("p (r h) -> p r h", r=3), lg.rearrange("p (r h) -> p r h", r=3),
                            lbt[:, 0:4].unsqueeze(1).to_broadcast([P, 3, 4]), ALU.subtract).then_inc(s.lb_max, 1)
            dve.wait_ge(s.lb_exp, w.at("lb_exp"))
            step(V.tensor_tensor(lbt[:, 16:20], lbt[:, 4:8], lbt[:, 8:12], ALU.add))
            step(V.tensor_tensor(lbt[:, 16:20], lbt[:, 16:20], lbt[:, 12:16], ALU.add))
            step(V.reciprocal(lbt[:, 20:24], lbt[:, 16:20]))
            step(V.tensor_tensor(hp[:, :, 0], lbt[:, 4:8], lbt[:, 20:24], ALU.mult))
            step(V.tensor_scalar(hp[:, :, 1], hp[:, :, 0], -1.0, 1.0, ALU.mult, ALU.add))
            step(V.tensor_copy(hp[:, :, 2], par[:, ONW:ONW + HEADS]))
            dve.wait_ge(s.s5_in, w.at("s5_in", 32))
            dve.wait_ge(s.s5_exp, w.at("s5_exp"))
            step(V.tensor_scalar(sv[:, 7], sp_in[:, 0], -1e-4, None, ALU.min))
            V.tensor_tensor(sv[:, 1], sv[:, 0], sv[:, 7], ALU.mult)
            step(V.tensor_tensor(sv[:, 2], sv[:, 0], sp_in[:, 1], ALU.mult))
            step(V.tensor_scalar(sv[:, 12], sv[:, 2], 1.0 / TWO_PI, None, ALU.mult))
            step(V.tensor_scalar(sv[:, 12], sv[:, 12], ROUND, None, ALU.add))
            step(V.tensor_scalar(sv[:, 12], sv[:, 12], -ROUND, None, ALU.add))
            for part in TURN:
                step(V.scalar_tensor_tensor(sv[:, 2], sv[:, 12], -part, sv[:, 2], ALU.mult, ALU.add))
            V.tensor_scalar(sv[:, 2], sv[:, 2], PI_IN, -PI_IN, ALU.min, ALU.max).then_inc(s.s5_mag, 1)
            dve.wait_ge(s.s5_trig, w.at("s5_trig", 2))
            step(V.tensor_tensor(sv[:, 8], sv[:, 3], sv[:, 6], ALU.mult))
            step(V.tensor_tensor(sv[:, 13], sv[:, 3], sv[:, 5], ALU.mult))
            step(V.tensor_scalar(sv[:, 9], sv[:, 13], sgn[:, 0:1], None, ALU.mult))
            step(V.tensor_scalar(sv[:, 14], sv[:, 8], -1.0, None, ALU.add))
            step(V.tensor_tensor(sv[:, 0], sv[:, 7], sv[:, 7], ALU.mult))
            step(V.tensor_tensor(sv[:, 1], sp_in[:, 1], sp_in[:, 1], ALU.mult))
            step(V.tensor_tensor(sv[:, 0], sv[:, 0], sv[:, 1], ALU.add))
            step(V.reciprocal(sv[:, 0], sv[:, 0]))
            step(V.tensor_tensor(sv[:, 1], sv[:, 14], sv[:, 7], ALU.mult))
            step(V.tensor_tensor(sv[:, 2], sv[:, 13], sp_in[:, 1], ALU.mult))
            step(V.tensor_tensor(sv[:, 1], sv[:, 1], sv[:, 2], ALU.add))
            step(V.tensor_tensor(sv[:, 10], sv[:, 1], sv[:, 0], ALU.mult))
            step(V.tensor_tensor(sv[:, 1], sv[:, 13], sv[:, 7], ALU.mult))
            step(V.tensor_tensor(sv[:, 2], sv[:, 14], sp_in[:, 1], ALU.mult))
            step(V.tensor_tensor(sv[:, 1], sv[:, 1], sv[:, 2], ALU.subtract))
            step(V.tensor_tensor(sv[:, 1], sv[:, 1], sv[:, 0], ALU.mult))
            V.tensor_scalar(sv[:, 11], sv[:, 1], sgn[:, 0:1], None, ALU.mult).then_inc(s.s5_made, 1)
            split(0)
            split(1)
            dve.wait_ge(s.x_in, w.at("x_in", 16))
            for k in range(KT):
                low(x, k, nw(0, 0, k))
            dve.wait_ge(s.sqrt_done, w.at("sqrt_done"))
            V.reciprocal(rstd_m[:], rstd_m[:]).then_inc(s.rstd_m_done, 1)
            dve.wait_ge(s.rstd_m_done, w.at("rstd_m_done"))
            factor()
            dve.wait_ge(s.rstd_done, w.at("rstd_done"))
            dve.wait_ge(s.con_in0, w.at("con_in0", 48))
            V.tensor_tensor(cosr[:], cosr[:], rstd[:], ALU.mult)
            V.tensor_tensor(sinr[:], sinr[:], rstd[:], ALU.mult)
            dve.wait_ge(s.con_in1, w.at("con_in1", 48))
            dve.wait_ge(s.s5_kept, w.at("s5_kept", 16))
            step(V.memset(scm[:], 0.0))
            with w.repeat(HEADS, product=8, w_hi_done=7, v_step=7 + 4 * KT, f_exp=1, f_log=1, b_exp=1, g_exp=1, a1_full=8,
                          ctr_full=8, s_full=8, p_exp=8, ao_full=8, o_root=1, st_done=8, rope_done=2, lin_out=7, o_done=1) as h:
                step(V.tensor_copy(cur[:], hp[:, ds(h, 1)].rearrange("p a b -> p (a b)")))
                dve.wait_ge(s.w_used, w.at("product"))
                V.tensor_tensor(zq[:], lin[0][:], rstd[:], ALU.mult).then_inc(s.lin_free, 1)
                split(0)
                dve.wait_ge(s.w_used, w.at("product"))
                V.tensor_tensor(zf[:], lin[1][:], rstd[:], ALU.mult).then_inc(s.lin_free, 1)
                split(1)
                dve.wait_ge(s.f_exp, w.at("f_exp"))
                step(V.tensor_scalar(zf[:], zf[:], 1.0, None, ALU.add))
                step(V.reciprocal(zf[:], zf[:]))
                V.tensor_scalar(zf[:], zf[:], cur[:, 1:2], cur[:, 0:1], ALU.mult, ALU.add).then_inc(s.f_sig, 1)
                dve.wait_ge(s.w_used, w.at("product"))
                V.tensor_tensor(zi[:], lin[0][:], rstd[:], ALU.mult).then_inc(s.lin_free, 1)
                split(0)
                dve.wait_ge(s.f_log, w.at("f_log"))
                V.tensor_tensor_scan(gb[:], first[:], ge[:], 0.0, ALU.mult, ALU.add).then_inc(s.b_scan, 1)
                dve.wait_ge(s.b_exp, w.at("b_exp"))
                V.tensor_copy(dec[:], ge[:].rearrange("p (c t) -> p c t", t=CH)[:, :, CH - 1])
                V.tensor_tensor(zq[:], zq[:], ge[:], ALU.mult).then_inc(s.q_dec, 1)
                dve.wait_ge(s.w_used, w.at("product"))
                V.tensor_tensor(zg[:], lin[1][:], rstd[:], ALU.mult).then_inc(s.lin_free, 1)
                split(1)
                for j, dst in ((0, bq), (1, bk)):
                    dve.wait_ge(s.w_used, w.at("product"))
                    V.tensor_tensor(dst[:], lin[j][:], cosr[:], ALU.mult)
                    V.tensor_tensor(prob[0:64, 0], lin[j][64:128, :], sinr[64:128, :], ALU.mult)
                    V.tensor_tensor(prob[64:128, 0], lin[j][0:64, :], sinr[0:64, :], ALU.mult).then_inc(s.lin_free, 1)
                    dve.wait_ge(s.lin_free, w.at("lin_out", (5, 1)[j]))
                    V.tensor_tensor(dst[:], dst[:], prob[:, 0], ALU.add).then_inc(s.rope_done, 1)
                    dve.wait_ge(s.rope_done, w.at("rope_done"))
                    if j == 0:
                        split(0)
                dve.sem_inc(s.w_ready, 1)
                dve.wait_ge(s.w_used, w.at("product"))
                V.tensor_tensor(prob[:, 1], lin[0][:], rstd[:], ALU.mult).then_inc(s.lin_free, 1)
                dve.wait_ge(s.lin_free, w.at("lin_out"))
                w.skip("product")
                split(0)
                split(1)
                step(V.memset(states[:, 0], 0.0))

                for T in range(KT):
                    W = (T + 1) * P
                    dve.wait_ge(s.a1_full, w.at("a1_full"))
                    if T >= 2:
                        dve.wait_ge(s.ao_full, w.at("ao_full"))
                    dve.wait_ge(s.s_full, w.at("s_full"))
                    V.tensor_copy(vtok[:, T % 2], lin[0][:, P:2 * P])
                    V.copy_predicated(scm[:, T % 2], causal[:].bitcast(mybir.dt.uint32), lin[0][:, 0:P])
                    V.tensor_tensor(vblk, lin[0][:, P:2 * P].unsqueeze(1).to_broadcast([P, 4, P]),
                                    blk[:].unsqueeze(2).to_broadcast([P, 4, P]), ALU.mult)
                    V.tensor_copy(ktok[:], lin[0][:, 2 * P:3 * P]).then_inc(s.a1_out, 1)
                    step(V.tensor_tensor_reduce(prob[:, T % 2, 0:W], wide[0][:, 0:W], logc[:, L - W:L], 1.0, -3e38,
                                                ALU.add, ALU.max, stat[:, T % 2, 0:1]))
                    V.tensor_scalar(stat[:, T % 2, 1:2], stat[:, T % 2, 0:1], -B_SCALE, None, ALU.mult).then_inc(s.s_max, 1)
                    dve.wait_ge(s.ctr_full, w.at("ctr_full"))
                    for c in range(4):
                        n = 4 * T + c
                        ins = V.scalar_tensor_tensor(states[:, (n + 1) % 8], states[:, n % 8], dec[:, n:n + 1],
                                                     lin[0][:, HALF + c * P:HALF + (c + 1) * P], ALU.mult, ALU.add)
                        if c < 3:
                            step(ins)
                        else:
                            ins.then_inc(s.st_done, 1)
                            dve.wait_ge(s.st_done, w.at("st_done"))
                    dve.wait_ge(s.p_exp, w.at("p_exp"))
                    V.reciprocal(stat[:, T % 2, 3:4], stat[:, T % 2, 2:3]).then_inc(s.p_sum, 1)
                dve.wait_ge(s.ao_full, w.at("ao_full", 2))
                dve.wait_ge(s.o_root, w.at("o_root"))
                dve.wait_ge(s.g_exp, w.at("g_exp"))
                step(V.scalar_tensor_tensor(gb[:], gb[:], 1.0, ge[:], ALU.add, ALU.mult))
                step(V.reciprocal(gb[:], gb[:]))
                step(V.tensor_tensor(gb[:], gb[:], zi[:], ALU.mult))
                V.scalar_tensor_tensor(y[:, ds(h, 1)].rearrange("p k t -> p (k t)"), gb[:], cur[:, 2:3], zg[:],
                                       ALU.mult, ALU.mult).then_inc(s.o_done, 1)
                dve.wait_ge(s.o_done, w.at("o_done"))
            dve.wait_ge(s.bo_out, w.at("bo_out", KT * HEADS))
            split_y()
            out_projection()
            dve.wait_ge(s.x_in, w.at("x_in", 16))
            boundary(0, 1, 0, 2)

            for layer in range(LAYERS):
                for k in range(KT):
                    dve.wait_ge(s.m_hi_done, w.at("m_hi_done"))
                    c = MNW + layer * KT + k
                    V.scalar_tensor_tensor(m_lo[:, k], m_raw[:, k], par[:, c:c + 1], m_hi[:, k].bitcast(F32),
                                           ALU.mult, ALU.subtract).then_inc(s.m_ready, 1)
                with w.repeat(HEADS, product=6, w_hi_done=6, s_full=4, p_exp=4, v_step=4):
                    def largest(p):
                        dve.wait_ge(s.s_full, w.at("s_full"))
                        step(V.tensor_reduce(xstat[:, p % 2, 0],
                                             wide[0][:, (p % 2) * HALF:(p % 2 + 1) * HALF].rearrange("p (i m) -> p i m", i=2),
                                             AX, ALU.max))
                        V.tensor_scalar(xstat[:, p % 2, 1], xstat[:, p % 2, 0], -X_SCALE, None,
                                        ALU.mult).then_inc(s.s_max, 1)

                    for j in range(6):
                        dve.wait_ge(s.w_used, w.at("product"))
                        if j < 2:
                            V.tensor_tensor(xq[:, j], lin[j][:], rstd[:], ALU.mult).then_inc(s.lin_free, 1)
                        else:
                            V.tensor_tensor((xk, xv)[j // 4][:, j % 2], lin[j % 2][:, 0:MEM], rstd_m[:],
                                            ALU.mult).then_inc(s.lin_free, 1)
                        split(j % 2)
                        if j >= 4:
                            largest(j - 4)
                    for p in range(4):
                        dve.wait_ge(s.p_exp, w.at("p_exp"))
                        V.reciprocal(xstat[:, p % 2, 3], xstat[:, p % 2, 2]).then_inc(s.p_sum, 1)
                        if p < 2:
                            largest(p + 2)
                w.skip("lin_out", 6 * HEADS)
                dve.wait_ge(s.bo_out, w.at("bo_out", 4 * HEADS))
                split_y()
                out_projection()
                boundary(layer, 3, layer, 4)

                def up(c):
                    for j in range(2):
                        dve.wait_ge(s.w_used, w.at("product"))
                        V.tensor_tensor(gate[:], lin[0][:], rstd[:], ALU.mult).then_inc(s.lin_free, 1)
                        w.skip("lin_out")
                        split(0)
                        dve.wait_ge(s.w_used, w.at("product"))
                        dve.wait_ge(s.silu_done, w.at("silu_done"))
                        V.tensor_tensor(gate[:], lin[1][:], rstd[:], ALU.mult).then_inc(s.lin_free, 1)
                        dve.wait_ge(s.lin_free, w.at("lin_out"))
                        V.tensor_tensor(f_act[:], f_act[:], gate[:], ALU.mult).then_inc(s.hid_done, 1)
                        split(1)
                        dve.wait_ge(s.hid_hi_done, w.at("hid_hi_done"))
                        V.tensor_tensor(hid_lo[:, 2 * (c % 2) + j], f_act[:], hid_hi[:, 2 * (c % 2) + j].bitcast(F32),
                                        ALU.subtract).then_inc(s.hid_ready, 1)

                def down(c, last):
                    for j in range(2):
                        for n in range(4 * j, 4 * j + 4):
                            if n % 4 == 3:
                                dve.wait_ge(s.w_used, w.at("product"))
                            else:
                                dve.wait_ge(s.out_full, w.at("out_full"))
                            V.tensor_tensor(y[:, n], y[:, n], wide[n % 2][:], ALU.add).then_inc(s.out_free, 1)
                        if not last:
                            split(j)

                dve.wait_ge(s.y_zero, w.at("y_zero"))
                up(0)
                with w.repeat(FC // 2, product=12, w_hi_done=12, out_full=12, silu_done=4, hid_hi_done=4, lin_out=8):
                    up(1)
                    down(0, False)
                    up(0)
                    down(1, False)
                down(FC - 1, layer == LAYERS - 1)
                if layer == 0:
                    dve.wait_ge(s.x_back, w.at("x_back", 16))
                boundary(layer, 5, None, None)
                if layer == LAYERS - 1:
                    continue
                factor()
                dve.wait_ge(s.rstd_done, w.at("rstd_done"))
                for k in range(KT):
                    V.scalar_tensor_tensor(natural(y[:, k]), x[:, k].rearrange("p (j s) -> p j s", s=SB), nw(1, 0, k),
                                           rstd[:].rearrange("p (j s) -> p j s", s=SB), ALU.mult,
                                           ALU.mult).then_inc(s.u_done, 1)
                def operator(b):
                    dve.wait_ge(s.m1_full, w.at("m1_full", 2))
                    V.tensor_copy(m1[:, b, 1].rearrange("p g c -> p (g c)"), lin[1][:]).then_inc(s.m1b_out, 1)

                def keep_inputs(b, g0):
                    dve.wait_ge(s.x_full, w.at("x_full"))
                    for dst, src, o in ((0, 0, 1), (0, 64, 0), (64, 0, 0)):
                        n = P if o == 1 else 64
                        ins = V.tensor_copy(hs[dst:dst + n, o, ds(g0, 8)].rearrange("p g j -> p (g j)"),
                                            wide[b][src:src + n, 0:HALF])
                    ins.then_inc(s.x_out, 1)

                operator(0)
                with w.repeat(KT // 2 - 1, m1_full=4, x_full=2) as i:
                    for b in range(2):
                        operator(1 - b)
                        keep_inputs(b, i * 16 + 8 * b)
                operator(1)
                keep_inputs(0, (KT - 2) * 8)
                keep_inputs(1, (KT - 1) * 8)
                dve.wait_ge(s.pw_in, w.at("pw_in", 32))
                dve.wait_ge(s.x_out, w.at("x_taken", KT))
                step(V.tensor_scalar(sai_b[:, 1], sai_b[:, 0], -1.0, None, ALU.mult))

                UNROLL = 7
                with w.repeat((NB - 1) // UNROLL, v_step=4 * UNROLL) as i:
                    for n in range(UNROLL):
                        prev = hs[:, :, :, ds(i * UNROLL + n, 1)].rearrange("p o g j -> p o (g j)")
                        here = hs[:, :, :, ds(i * UNROLL + n + 1, 1)].rearrange("p o g j -> p o (g j)")
                        V.tensor_tensor(sc1[:], ar_b[:].unsqueeze(1).to_broadcast([P, 2, GR]), prev,
                                        ALU.mult).then_inc(s.v_step, 1)
                        V.tensor_tensor(sc2[:, ::-1], sai_b[:], prev, ALU.mult).then_inc(s.v_step, 1)
                        dve.wait_ge(s.v_step, w.at("v_step"))
                        V.tensor_tensor(sc1[:], sc1[:], here, ALU.add).then_inc(s.v_step, 1)
                        dve.wait_ge(s.v_step, w.at("v_step", 2))
                        step(V.tensor_tensor(here, sc1[:], sc2[:], ALU.add))
                dve.sem_inc(s.scan_done, 1)
                dve.wait_ge(s.yt_out, w.at("yt_out", KT))
                with w.repeat(KT // 2, y2_full=2) as i:
                    for b in range(2):
                        dve.wait_ge(s.y2_full, w.at("y2_full"))
                        v = ub[:, :, ds(i * 16 + 8 * b, 8), 1:NB]
                        V.tensor_tensor(v, wide[b][:].rearrange("p (t g j) -> p t g j", t=2, g=8)[:, :, :, 1:NB], v,
                                        ALU.add).then_inc(s.y2_out, 1)
                for half in range(2):
                    tiles_ = range(half * KT // 2, (half + 1) * KT // 2)
                    dve.wait_ge((s.yT_in0, s.yT_in1)[half], 16)
                    for k in tiles_:
                        V.scalar_tensor_tensor(yT[:, k], y[:, k], par[:, SD + k:SD + k + 1], yT[:, k], ALU.mult,
                                               ALU.add).then_inc(s.g_in, 1)
                    for k in tiles_:
                        low(y, k)
                with w.repeat(KT // 2, w_hi_done=4, product=4, lin_out=4) as i:
                    for b in range(2):
                        dve.wait_ge(s.w_used, w.at("product"))
                        split(0)
                        dve.wait_ge(s.w_used, w.at("product"))
                        dve.wait_ge(s.lin_free, w.at("lin_out"))
                        V.tensor_tensor(y[:, ds(i * 2 + b, 1)].rearrange("p k t -> p (k t)"), lin[1][:], sg[:],
                                        ALU.mult).then_inc(s.lin_free, 1)
                        w.skip("lin_out")
                        split(1)
                boundary(1, 1, 1, 2, blocked=True)

        @block.gpsimd
        def _(pool):
            w = Counts(pool, sems)
            G = nc.gpsimd

            def sum_squares():
                for k in range(KT):
                    pool.wait_ge(s.sq_done, w.at("sq_done"))
                    if k == 0:
                        G.tensor_copy(acc[:], sq[:, 0]).then_inc(s.sq_free, 1)
                    else:
                        G.tensor_tensor(acc[:], acc[:], sq[:, k % 2], ALU.add).then_inc(s.sq_free, 1)
                    pool.wait_ge(s.sq_free, w.at("acc_sum"))

            def boundary(pre=True):
                pool.wait_ge(s.rstd_done, w.at("rstd_done"))
                for k in range(KT):
                    if k >= 2:
                        pool.wait_ge(s.x_done, w.at("x_done"))
                    G.tensor_tensor(tmp[:, k % 2], y[:, k], rstd[:], ALU.mult).then_inc(s.tmp_done, 1)
                pool.wait_ge(s.x_done, w.at("x_done", 2))
                if pre:
                    pool.wait_ge(s.rstd_done, w.at("rstd_done"))
                    w.skip("sq_done", KT)
                    w.skip("acc_sum", KT)

            def step(ins):
                ins.then_inc(s.g_step, 1)
                pool.wait_ge(s.g_step, w.at("g_step"))

            def operators():
                pool.wait_ge(s.h_ready, w.at("h_ready", 5 * KT))
                pool.dma_start(t["x_d"].rearrange("(k p) t -> p k t", p=P), x[:]).then_inc(s.x_sent, 16)
                pool.wait_ge(s.x_sent, w.at("x_sent", 16))
                pool.dma_start(pc[:], t["pc_d"]).then_inc(s.ops_in, 16)
                pool.dma_start(o_src[0][:].rearrange("p g c -> p (g c)"), t["s5_b"][0]).then_inc(s.ops_in, 16)
                pool.dma_start(o_src[1][:].rearrange("p g c -> p (g c)"), t["s5_b"][1]).then_inc(s.ops_in, 16)
                pool.wait_ge(s.ops_in, w.at("ops_in", 48))

                def wide_(ap):
                    return ap.unsqueeze(2).to_broadcast([P, GR, GC])

                for own, sign in ((0, ALU.add), (1, ALU.subtract)):
                    step(G.tensor_tensor(o_dst[own][:], o_src[own][:], wide_(pc[:, 2]), ALU.mult))
                    step(G.tensor_tensor(o_tmp[:], o_src[1 - own][:], wide_(pc[:, 3]), ALU.mult))
                    step(G.tensor_tensor(o_dst[own][:], o_dst[own][:], o_tmp[:], sign))

                def first_power():
                    G.memset(pw[:, 0], 1.0)
                    step(G.memset(pw[:, 1], 0.0))

                def one(src, dst, dram, at, b, advance=True):
                    G.tensor_tensor(dst[b][:], src[0][:], wide_(pw[:, 0]), ALU.mult)
                    ins = G.tensor_tensor(o_tmp[:], src[1][:], wide_(pw[:, 1]), ALU.mult)
                    if advance:
                        G.tensor_tensor(pt[:, 0], pw[:, 0], pc[:, 0], ALU.mult)
                        G.tensor_tensor(pt[:, 1], pw[:, 1], pc[:, 1], ALU.mult)
                        G.tensor_tensor(pt[:, 2], pw[:, 0], pc[:, 1], ALU.mult)
                        ins = G.tensor_tensor(pt[:, 3], pw[:, 1], pc[:, 0], ALU.mult)
                    step(ins)
                    step(G.tensor_tensor(dst[b][:], dst[b][:], o_tmp[:], ALU.add))
                    if advance:
                        G.tensor_tensor(pw[:, 0], pt[:, 0], pt[:, 1], ALU.subtract)
                    pool.dma_start(dram[ds(at, 1)].rearrange("a p c -> p (a c)"),
                                   dst[b][:].rearrange("p g c -> p (g c)")).then_inc((s.ops_out0, s.ops_out1)[b], 16)
                    if advance:
                        step(G.tensor_tensor(pw[:, 1], pt[:, 2], pt[:, 3], ALU.add))

                first_power()
                for n in range(2):
                    one(o_dst, o_src, t["w_d"], SB - 1 - n, n)
                with w.repeat(SB // 2 - 1, g_step=6, ops_out0=16, ops_out1=16) as i:
                    for b in range(2):
                        pool.wait_ge((s.ops_out0, s.ops_out1)[b], w.at(f"ops_out{b}", 16))
                        one(o_dst, o_src, t["w_d"], i * -2 + (SB - 3 - b), b)
                pool.wait_ge(s.ops_out0, w.at("ops_out0", 16))
                pool.wait_ge(s.ops_out1, w.at("ops_out1", 16))
                pool.dma_start(o_src[0][:].rearrange("p g c -> p (g c)"), t["s5_c"][0]).then_inc(s.ops_in, 16)
                pool.dma_start(o_src[1][:].rearrange("p g c -> p (g c)"), t["s5_c"][1]).then_inc(s.ops_in, 16)
                pool.wait_ge(s.ops_in, w.at("ops_in", 32))
                for b in range(2):
                    step(G.tensor_tensor(o_src[b][:], o_src[b][:], wide_(sgn[:, 1:2].to_broadcast([P, GR])), ALU.mult))
                first_power()
                for n in range(2):
                    one(o_src, o_dst, t["dd_d"], n, n)
                with w.repeat(SB // 2 - 1, g_step=6, ops_out0=16, ops_out1=16) as i:
                    for b in range(2):
                        pool.wait_ge((s.ops_out0, s.ops_out1)[b], w.at(f"ops_out{b}", 16))
                        one(o_src, o_dst, t["dd_d"], i * 2 + (2 + b), b)
                pool.wait_ge(s.ops_out0, w.at("ops_out0", 16))
                one(o_src, o_dst, t["dd_d"], SB, 0, advance=False)
                pool.dma_start(t["pw_d"], pw[:]).then_inc(s.ops_out1, 16)
                pool.wait_ge(s.ops_out0, w.at("ops_out0", 16))
                pool.wait_ge(s.ops_out1, w.at("ops_out1", 32))
                pool.dma_start(x[:], t["x_d"].rearrange("(k p) t -> p k t", p=P)).then_inc(s.x_back, 16)

            w.skip("sq_done", 1 + KT)
            w.skip("acc_sum", KT)
            w.skip("rstd_done")
            with w.repeat(HEADS, b_neg=1, q_dec=1, b_left_exp=1, p_sum=8):
                pool.wait_ge(s.b_neg, w.at("b_neg"))
                G.tensor_tensor(zf[:], zf[:], gk[:], ALU.mult).then_inc(s.k_inv, 1)
                pool.wait_ge(s.q_dec, w.at("q_dec"))
                b3 = gb[:].rearrange("p (c t) -> p c t", t=CH)
                G.tensor_tensor(ge[:].rearrange("p (c t) -> p c t", t=CH), b3[:, :, CH - 1:CH].to_broadcast([P, NCH, CH]),
                                b3, ALU.subtract).then_inc(s.b_left, 1)
                pool.wait_ge(s.b_left_exp, w.at("b_left_exp"))
                G.tensor_tensor(gk[:], gk[:], ge[:], ALU.mult).then_inc(s.k_end, 1)
                for T in range(KT):
                    W = (T + 1) * P
                    pool.wait_ge(s.p_sum, w.at("p_sum"))
                    G.tensor_tensor(prob[:, T % 2, 0:W], prob[:, T % 2, 0:W],
                                    stat[:, T % 2, 3:4].to_broadcast([P, W]), ALU.mult).then_inc(s.p_ready, 1)
            sum_squares()
            boundary()
            for layer in range(LAYERS):
                with w.repeat(HEADS, p_sum=4):
                    for p in range(4):
                        pool.wait_ge(s.p_sum, w.at("p_sum"))
                        G.tensor_tensor(xp[:, p % 2], xp[:, p % 2], xstat[:, p % 2, 3].unsqueeze(2).to_broadcast([P, 2, MEM]),
                                        ALU.mult).then_inc(s.p_ready, 1)
                sum_squares()
                boundary()
                G.memset(y[:], 0.0).then_inc(s.y_zero, 1)
                if layer == 0:
                    operators()
                sum_squares()
                boundary(pre=layer + 1 < LAYERS)
                if layer + 1 < LAYERS:

                    one4 = ones[:, 0:1].unsqueeze(2).unsqueeze(3).to_broadcast([P, SB, 8, GC])

                    def by_group(dst, src):
                        return G.tensor_tensor(dst[:].rearrange("p g n c -> p n g c"),
                                               src.rearrange("p n (g c) -> p n g c", c=GC),
                                               one4, ALU.mult)

                    with w.repeat(KT // 2, wt_in0=16, wt_in1=16, m1_full=4):
                        for b in range(2):
                            pool.wait_ge((s.wt_in0, s.wt_in1)[b], w.at(f"wt_in{b}", 16))
                            by_group(wr, wt[b][:]).then_inc(s.wr_done, 1)
                            pool.wait_ge(s.m1_full, w.at("m1_full", 2))
                    pool.wait_ge(s.yt_full, w.at("yt_full", KT))
                    pool.wait_ge(s.d_in0, w.at("d_in0", 16 * KT))
                    pool.wait_ge(s.d_in1, w.at("d_in1", 16 * KT))
                    for b in range(2):
                        pool.wait_ge((s.d_in0, s.d_in1)[b], w.at(f"d_in{b}", 16))
                        by_group(dr[b], dt_[b][:, 1:]).then_inc(s.dr_done, 1)
                    with w.repeat(KT // 2 - 1, d_in0=16, d_in1=16, y2_full=2):
                        for b in range(2):
                            pool.wait_ge(s.y2_full, w.at("y2_full"))
                            pool.wait_ge((s.d_in0, s.d_in1)[b], w.at(f"d_in{b}", 16))
                            by_group(dr[b], dt_[b][:, 1:]).then_inc(s.dr_done, 1)
                    sum_squares()
                    boundary()

        @block.tensor
        def _(pe):
            w = Counts(pe, sems)
            MM = nc.tensor.matmul
            for sem in (s.w_used, s.w_ready, s.lin_free, s.out_free, s.sq_free, s.x_out, s.y2_out):
                pe.sem_inc(sem, 2)

            def passes(out, w_h, w_l, a_h, a_l, first, last, spans):
                for n, (a, b) in enumerate(((w_h, a_h), (w_h, a_l), (w_l, a_h))):
                    for lo_, hi_ in spans:
                        ins = MM(out[:, lo_:hi_], a, b[:, lo_:hi_], start=first and n == 0, stop=last and n == 2)
                return ins

            TOK = ((0, HALF), (HALF, L))

            def linear(parity, a_h, a_l, spans=TOK, used=1, ahead=None):
                pe.wait_ge(s.w_ready, w.at("w_split"))
                pe.wait_ge(s.lin_free, w.at("lin_free"))
                for k in range(KT):
                    if ahead:
                        ahead(k)
                    ins = passes(lin[parity], col8(w_hi, parity)[:, k], col8(w_lo, parity)[:, k], a_h[:, k], a_l[:, k],
                                 k == 0, k == KT - 1, spans)
                ins.then_inc(s.w_used, used)

            def token_sums(src, first, last):
                for T in range(KT):
                    ins = MM(wide[1][:, T:T + 1], src[:, T * P:(T + 1) * P], ones[:, 0:1], start=first and T == 0,
                             stop=last and T == KT - 1)
                return ins

            def spread():
                for lo_, hi_ in TOK:
                    pe.wait_ge(s.diag_done, w.at("diag_done"))
                    for diag in (diag_hi, diag_lo):
                        ins = MM(wide[0][:, lo_:hi_], ones_r[:], diag[:].rearrange("p t n -> p (t n)")[:, lo_:hi_],
                                 start=diag is diag_hi, stop=diag is diag_lo)
                    ins.then_inc(s.spread_full, 1)

            def post_norm():
                pe.wait_ge(s.sq_free, w.at("acc_sum", KT))
                token_sums(acc, True, True).then_inc(s.stat_full, 1)
                w.skip("sq_done", KT)
                spread()

            def pre_sums(k):
                pe.wait_ge(s.sq_done, w.at("sq_done"))
                token_sums(sq[:, k % 2], k == 0, k == KT - 1).then_inc(s.sq_free, 1)
                w.skip("acc_sum")

            def arriving(k):
                pe.wait_ge(s.h_ready, w.at("h_ready"))

            def arriving_normed(k):
                pre_sums(k)
                arriving(k)

            def spread_midway(k):
                if k == 2:
                    spread()

            def first_pair():
                linear(0, h_hi, h_lo, ahead=arriving_normed)
                linear(1, h_hi, h_lo, ahead=spread_midway)

            def out_projection():
                linear(0, h_hi, h_lo, ahead=arriving)
                linear(1, h_hi, h_lo)
                with w.repeat(KT // 2 - 1, w_split=2, lin_free=2):
                    for j in range(2):
                        linear(j, h_hi, h_lo)
                w.skip("lin_out", KT)
                post_norm()

            pe.wait_ge(s.sq_done, w.at("sq_done"))
            for k in range(KT):
                ins = MM(lin[1][:, 0:MEM], ones[:], m_sq[:, k], start=k == 0, stop=k == KT - 1)
            ins.then_inc(s.stat_full, 1)
            pe.wait_ge(s.par_in, w.at("par_in", 32))


            def mixer_turn(first):
                if first:
                    first_pair()
                for j in range(2 if first else 0, 7):
                    linear(j % 2, h_hi, h_lo, used=2 if j == 6 else 1)
                pe.wait_ge(s.lin_free, w.at("lin_out", 7))
                pe.wait_ge(s.q_dec, w.at("q_dec"))
                pe.wait_ge(s.k_inv, w.at("k_inv"))
                pe.wait_ge(s.k_end, w.at("k_end"))
                pe.wait_ge(s.rope_done, w.at("rope_done", 2))

                def a_tile(T):
                    c = slice(T * P, (T + 1) * P)
                    MM(lin[0][:, 0:P], zf[:, c], zq[:, c], start=True, stop=True)
                    nc.tensor.transpose(lin[0][:, P:2 * P], zi[:, c], ident[:])
                    nc.tensor.transpose(lin[0][:, 2 * P:3 * P], gk[:, c], ident[:]).then_inc(s.a1_full, 1)

                def b_scores(T):
                    if T:
                        pe.wait_ge(s.s_max, w.at("s_max"))
                    W = (T + 1) * P
                    for lo_ in range(0, W, HALF):
                        hi_ = min(W, lo_ + HALF)
                        ins = MM(wide[0][:, lo_:hi_], bq[:, T * P:(T + 1) * P], bk[:, lo_:hi_], start=True, stop=True)
                    ins.then_inc(s.s_full, 1)

                def a_output(T):
                    pe.wait_ge(s.st_done, w.at("st_done"))
                    if T:
                        pe.wait_ge(s.ao_out, w.at("ao_out"))
                    MM(lin[1][:, 0:P], vtok[:, T % 2], scm[:, T % 2], start=True, stop=True)
                    for c in range(4):
                        n = 4 * T + c
                        ins = MM(lin[1][:, c * CH:(c + 1) * CH], states[:, n % 8], zq[:, n * CH:(n + 1) * CH],
                                 start=False, stop=True, skip_group_check=True)
                    ins.then_inc(s.ao_full, 1)

                def b_output(T):
                    pe.wait_ge(s.t_out, w.at("t_out"))
                    if T:
                        pe.wait_ge(s.bo_out, w.at("bo_out"))
                    for k in range(T + 1):
                        ins = MM(lin[1][:, HALF:HALF + P], vtok_b[:, k], probT[:, k], start=k == 0, stop=k == T)
                    ins.then_inc(s.bo_full, 1)

                def b_transposes(T):
                    pe.wait_ge(s.p_ready, w.at("p_ready"))
                    if T == 0:
                        pe.wait_ge(s.vt_out, w.at("vt_out"))
                    for k in range(T + 1):
                        ins = nc.tensor.transpose(wide[1][:, k * P:(k + 1) * P], prob[:, T % 2, k * P:(k + 1) * P], ident[:])
                    ins.then_inc(s.t_full, 1)

                for T in range(KT + 1):
                    if T < KT:
                        a_tile(T)
                        b_scores(T)
                    if T:
                        a_output(T - 1)
                        b_transposes(T - 1)
                    else:
                        for k in range(KT):
                            ins = nc.tensor.transpose(wide[1][:, k * P:(k + 1) * P], prob[:, 1, k * P:(k + 1) * P], ident[:])
                        ins.then_inc(s.vt_full, 1)
                    if T < KT:
                        pe.wait_ge(s.a1_out, w.at("a1_out"))
                        MM(lin[0][:, HALF:L], ktok[:], vblk.rearrange("p c v -> p (c v)"), start=True,
                           stop=True).then_inc(s.ctr_full, 1)
                    if T:
                        b_output(T - 1)
                pe.wait_ge(s.s_max, w.at("s_max"))
                pe.wait_ge(s.o_sq, w.at("o_sq"))
                for lo_, hi_ in TOK:
                    ins = MM(wide[0][:, lo_:hi_], ones[:], ge[:, lo_:hi_], start=True, stop=True)
                ins.then_inc(s.o_stat, 1)
                w.skip("w_split")
                pe.wait_ge(s.ao_out, w.at("ao_out"))
                pe.wait_ge(s.bo_out, w.at("bo_out"))

            mixer_turn(True)
            with w.repeat(HEADS - 1, w_split=8, lin_free=7, lin_out=7, q_dec=1, k_inv=1, k_end=1, rope_done=2, vt_out=1,
                          a1_out=8, s_max=8, st_done=8, ao_out=8, bo_out=8, t_out=8, p_ready=8, o_sq=1, o_root=0):
                mixer_turn(False)
            out_projection()

            for layer in range(LAYERS):
                def attention_turn(first):
                    if first:
                        first_pair()
                    def scores(p):
                        if p >= 2:
                            pe.wait_ge(s.p_exp, w.at("p_exp"))
                        for i in range(2):
                            c, q = (p % 2) * HALF + i * MEM, 2 * p + i
                            for j in range(2):
                                ins = MM(wide[0][:, c:c + MEM], xq[:, j, q * P:(q + 1) * P], xk[:, j], start=j == 0, stop=j == 1)
                        ins.then_inc(s.s_full, 1)

                    def transposes(p):
                        pe.wait_ge(s.p_ready, w.at("p_ready"))
                        for k in range(2):
                            for i in range(2):
                                c = (1 - p % 2) * HALF + (2 * k + i) * P
                                ins = nc.tensor.transpose(wide[1][:, c:c + P], xp[:, p % 2, i, k * P:(k + 1) * P], ident[:])
                        ins.then_inc(s.t_full, 1)

                    def output(half):
                        pe.wait_ge(s.t_out, w.at("t_out", 2))
                        for j in range(2):
                            for k in range(2):
                                ins = MM(lin[half][:, j * HALF:(j + 1) * HALF], xvt[:, k, j * P:(j + 1) * P],
                                         xpT[half][:, k], start=k == 0, stop=k == 1)
                            ins.then_inc(s.bo_full, 1)

                    for j in range(6):
                        if j == 2:
                            pe.wait_ge(s.m_ready, KT * (layer + 1))
                        if j >= 2:
                            linear(j % 2, m_hi, m_lo, ((0, MEM),))
                        elif not first:
                            linear(j, h_hi, h_lo)
                        if j == 4:
                            pe.wait_ge(s.lin_free, w.at("lin_out", 4))
                            scores(0)
                    scores(1)
                    pe.wait_ge(s.lin_free, w.at("lin_out", 2))
                    for k in range(2):
                        for j in range(2):
                            c = (2 * k + j) * P
                            ins = nc.tensor.transpose(wide[1][:, c:c + P], xv[:, j, k * P:(k + 1) * P], ident[:])
                    ins.then_inc(s.vt_full, 1)
                    for p in range(2):
                        if p:
                            pe.wait_ge(s.vt_out, w.at("vt_out"))
                        transposes(p)
                        scores(p + 2)
                    output(0)
                    transposes(2)
                    transposes(3)
                    output(1)
                    pe.wait_ge(s.p_exp, w.at("p_exp", 2))
                    pe.wait_ge(s.bo_out, w.at("bo_out", 4))

                attention_turn(True)
                with w.repeat(HEADS - 1, w_split=6, lin_free=6, lin_out=6, vt_out=1, p_exp=4, p_ready=4, t_out=4, bo_out=4):
                    attention_turn(False)
                out_projection()

                def up(first=False):
                    for j in range(2):
                        if first and j == 0:
                            first_pair()
                        else:
                            linear(0, h_hi, h_lo)
                            linear(1, h_hi, h_lo)

                def down(c):
                    pe.wait_ge(s.hid_ready, w.at("hid_ready", 2))
                    for j in range(2):
                        pe.wait_ge(s.w_ready, w.at("w_split"))
                        for n in range(4):
                            pe.wait_ge(s.out_free, w.at("out_free"))
                            for k in range(2):
                                m = n * P
                                t_ = 2 * (c % 2) + k
                                ins = passes(wide[n % 2], col2(w_hi, j)[:, k, m:m + P], col2(w_lo, j)[:, k, m:m + P],
                                             hid_hi[:, t_], hid_lo[:, t_], k == 0, k == 1, TOK)
                            ins.then_inc(s.w_used if n == 3 else s.out_full, 1)

                up(first=True)
                with w.repeat(FC // 2, w_split=12, lin_free=8, hid_ready=4, out_free=16):
                    up()
                    down(0)
                    up()
                    down(1)
                down(FC - 1)
                w.skip("lin_out", 2 * FT)
                w.skip("sum_out", FC * KT)
                post_norm()
                if layer == LAYERS - 1:
                    continue
                for k in range(KT):
                    pre_sums(k)
                spread()

                def u_dyn(t2, g):
                    return ub[:, t2, ds(g, 1)].rearrange("p g j -> p (g j)")

                def transposes():
                    pe.wait_ge(s.wr_done, w.at("wr_done"))
                    for t2 in range(2):
                        for g in range(8):
                            ins = nc.tensor.transpose(lin[t2][:, g * P:(g + 1) * P],
                                                      wr[:, g, 8 * t2:8 * t2 + 8].rearrange("p n c -> p (n c)"), ident[:])
                        ins.then_inc(s.m1_full, 1)

                def inputs(b, g0, last=False):
                    pe.wait_ge(s.m1a_out, w.at("m1a_out"))
                    pe.wait_ge(s.m1b_out, w.at("m1b_out"))
                    if not last:
                        transposes()
                    pe.wait_ge(s.x_out, w.at("x_out"))
                    for g in range(8):
                        for t2 in range(2):
                            ins = MM(wide[b][:, g * NB:(g + 1) * NB], m1[:, b, t2, g], u_dyn(t2, g0 + g),
                                     start=t2 == 0, stop=t2 == 1)
                    ins.then_inc(s.x_full, 1)

                transposes()
                pe.wait_ge(s.u_in0, 16 * SB)
                with w.repeat(KT // 4, wr_done=2, m1a_out=2, m1b_out=2, x_out=2) as i:
                    for b in range(2):
                        inputs(b, i * 16 + 8 * b)
                pe.wait_ge(s.u_in1, 16 * SB)
                for k in range(KT // 2, KT):
                    inputs(k % 2, 8 * k, last=k == KT - 1)
                pe.wait_ge(s.x_out, w.at("x_out", 2))

                def kernels(b):
                    pe.wait_ge((s.d_in0, s.d_in1)[b], w.at(f"d_in{b}", 32))
                    for g in range(8):
                        ins = MM(lin[g // 4][0:16, (g % 4) * 256:(g % 4 + 1) * 256], w15[b][:, g * GC:(g + 1) * GC],
                                 dt_[b][:, 0:SB, g * GC:(g + 1) * GC], start=True, stop=True)
                    ins.then_inc(s.k_full, 1)

                def toeplitz(b, k8):
                    pe.wait_ge((s.t_in0, s.t_in1)[b], w.at(f"t_in{b}", 128))
                    for g in range(8):
                        c = g * 2 * NB
                        MM(wide[b][:, c:c + 2 * NB], tz[b][:, g, 0:P],
                           ub[:, :, ds(k8 + g, 1)].rearrange("p t g j -> p t (g j)"), start=True, stop=False)
                        ins = MM(wide[b][:, c + NB:c + 2 * NB], tz[b][:, g, P:2 * P], u_dyn(0, k8 + g), start=False,
                                 stop=True)
                    ins.then_inc(s.yt_full, 1)

                kernels(0)
                pe.wait_ge(s.k_out, w.at("k_out"))
                kernels(1)
                with w.repeat(KT // 2 - 1, d_in0=32, d_in1=32, t_in0=128, t_in1=128, yt_out=2, k_out=2) as i:
                    for b in range(2):
                        toeplitz(b, i * 16 + 8 * b)
                        pe.wait_ge(s.k_out, w.at("k_out"))
                        kernels(b)
                        pe.wait_ge(s.yt_out, w.at("yt_out"))
                pe.wait_ge(s.k_out, w.at("k_out"))
                for b in range(2):
                    toeplitz(b, (KT - 2 + b) * 8)
                    pe.wait_ge(s.yt_out, w.at("yt_out"))
                pe.wait_ge(s.scan_done, w.at("scan_done"))
                with w.repeat(KT // 2, dr_done=2, y2_out=2) as i:
                    for b in range(2):
                        pe.wait_ge(s.dr_done, w.at("dr_done"))
                        pe.wait_ge(s.y2_out, w.at("y2_out"))
                        for t2 in range(2):
                            for g in range(8):
                                c = t2 * HALF + g * NB
                                ins = MM(wide[b][:, c + 1:c + NB], dr[b][:, g, 8 * t2:8 * t2 + 8].rearrange("p n c -> p (n c)"),
                                         hs[:, 1, ds(i * 16 + (8 * b + g), 1), 0:NB - 1].rearrange("p g j -> p (g j)"),
                                         start=True, stop=True)
                        ins.then_inc(s.y2_full, 1)
                linear(0, h_hi, h_lo, ahead=arriving)
                linear(1, h_hi, h_lo)
                with w.repeat(KT - 1, w_split=2, lin_free=2):
                    for j in range(2):
                        linear(j, h_hi, h_lo)
                w.skip("lin_out", 2 * KT)
                post_norm()


_IN = ("ab_w_in", "ab_w_out", "s5_w_glu", "xattn_wq", "xattn_wkv", "xattn_wo", "ffn_w_in", "ffn_w_out")


def constants():
    c = np.zeros((P, NCON), np.float32)
    c[:, C_ID:C_ID + P] = np.eye(P)
    i = np.arange(P)
    c[:, C_CAUSAL:C_CAUSAL + P] = (i[:, None] // CH == i[None] // CH) & (i[:, None] <= i[None])
    c[:, C_BLK:C_BLK + 4] = i[:, None] // CH == np.arange(4)[None]
    back = i[:, None] + (L - P) - np.arange(L)[None]
    times = (back >= 0) * ((back <= 128) * 1.0 + ((back % 4 == 0) & (back <= 512)) + (back % 16 == 0))
    c[:, C_LOGC:C_LOGC + L] = np.where(times > 0, np.log(np.maximum(times, 1)) / B_SCALE, -1e30)
    half = 64
    freq = np.float32(10000.0) ** (-np.arange(half, dtype=np.float32) / half)
    ang = (np.arange(L, dtype=np.float32)[None] * freq[:, None]).astype(np.float32).astype(np.float64)
    c[:, C_COS:C_COS + L] = np.tile(np.cos(ang), (2, 1))
    c[:, C_SIN:C_SIN + L] = np.concatenate([np.sin(ang), -np.sin(ang)])
    c[:, C_SIGN] = np.where(i < 64, -1, 1)
    c[:, C_SIGN + 1] = np.where(i < 64, 1, -1)
    c[:, C_FIRST:C_FIRST + L] = (np.arange(L) % CH != 0)[None]
    return c


def kernel(**inputs):
    import concourse.bacc as bacc
    from concourse.bass_utils import run_bass_kernel_spmd

    a = {k: np.asarray(v) for k, v in inputs.items()}
    arrays = {n: np.ascontiguousarray(a[n]) for n in _IN}
    arrays["xT"] = np.ascontiguousarray(a["x"][0].T)
    arrays["memT"] = np.ascontiguousarray(a["mem"][0].T)

    def tiles(v):
        return np.moveaxis(v.reshape(*v.shape[:-1], -1, P), -1, 0).reshape(P, -1)

    arrays["par"] = np.concatenate([tiles(a[n]) for n in ("norm_w", "mem_norm_w", "hgrn_lb_logits",
                                                          "hgrn_out_norm_w", "s5_d")], axis=1)
    arrays["con"] = constants()
    lr, li = a["s5_lambda_re"][0].T, a["s5_lambda_im"][0].T
    dt = np.broadcast_to(a["s5_log_dt"][0][None], lr.shape)
    arrays["s5_small"] = np.tile(np.concatenate([lr, li, dt], axis=1), (2, 1))
    for n, re, im in (("s5_b", a["s5_b_re"][0].transpose(1, 0, 2), a["s5_b_im"][0].transpose(1, 0, 2)),
                      ("s5_c", a["s5_c_re"][0].transpose(2, 0, 1), a["s5_c_im"][0].transpose(2, 0, 1))):
        re, im = re.reshape(64, -1), im.reshape(64, -1)
        arrays[n] = np.stack([np.concatenate([re, im]), np.concatenate([im, re])])
    nc = bacc.Bacc("TRN2", target_bir_lowering=False, num_devices=1)
    t = {n: nc.dram_tensor(n, v.shape, F32, kind="ExternalInput").ap() for n, v in arrays.items()}
    t["out"] = nc.dram_tensor("out", (D, L), F32, kind="ExternalOutput").ap()
    for n, shape in (("u_d", (D, L)), ("y_d", (D, L)), ("x_d", (D, L)), ("w_d", (SB, P, GR * GC)),
                     ("dd_d", (SB + 1, P, GR * GC)), ("pc_d", (P, 4, GR)), ("pw_d", (P, 2, GR))):
        t[n] = nc.dram_tensor(n, shape, F32, kind="Internal").ap()
    program(nc, t)
    r = run_bass_kernel_spmd(nc, [arrays], core_ids=[0])
    return np.ascontiguousarray(r.results[0]["out"].T)[None]
```
